# Optimizing a Trainium2 kernel written in Bass

```python
import math
import jax
import jax.numpy as jnp
from jax import lax
import numpy as np

D_MODEL = 1024
BATCH = 1
SEQ = 512
DEPTH = 1

N_MEM = 256
Q_BLOCK = 128
RMS_EPS = 1e-6
NEG_INF = -1e30
ROPE_THETA = 10000.0
POS_OFFSET_MAX = 1024

DIFF_HEADS = 8
DIFF_HALF_DIM = 32
DIFF_V_DIM = 2 * DIFF_HALF_DIM
DIFF_QK_WIDTH = DIFF_HEADS * 2 * DIFF_HALF_DIM
DIFF_WIDTH = DIFF_HEADS * DIFF_V_DIM

MLA_HEADS = 8
MLA_Q_RANK = 256
MLA_KV_RANK = 128
MLA_NOPE_DIM = 64
MLA_ROPE_DIM = 32
MLA_QK_DIM = MLA_NOPE_DIM + MLA_ROPE_DIM
MLA_V_DIM = 64
MLA_WIDTH = MLA_HEADS * MLA_V_DIM

MIX_WIDTH = DIFF_WIDTH + MLA_WIDTH
IN_SPLITS = (DIFF_QK_WIDTH,
             2 * DIFF_QK_WIDTH,
             2 * DIFF_QK_WIDTH + DIFF_WIDTH,
             2 * DIFF_QK_WIDTH + DIFF_WIDTH + MLA_Q_RANK,
             2 * DIFF_QK_WIDTH + DIFF_WIDTH + MLA_Q_RANK + MLA_KV_RANK)
IN_PROJ_WIDTH = IN_SPLITS[-1] + MLA_ROPE_DIM

MEM_HEADS = 4
MEM_HEAD_DIM = 128
MEM_WIDTH = MEM_HEADS * MEM_HEAD_DIM

N_GROUPS = 4
EXPERTS_PER_GROUP = 8
N_EXPERTS = N_GROUPS * EXPERTS_PER_GROUP
TOP_K_IN_GROUP = 2
EXPERT_FF = 256
EXPERT_BLOCK = 128


def _rms_norm(x, gain):
    xf = x.astype(jnp.float32)
    y = xf * lax.rsqrt(jnp.mean(xf * xf, axis=-1, keepdims=True) + RMS_EPS)
    return (y * gain.astype(jnp.float32)).astype(x.dtype)

def _alibi_slopes(n_heads):
    return 2.0 ** (-8.0 * jnp.arange(1, n_heads + 1, dtype=jnp.float32) / n_heads)

def _rope_angles(positions, dim):
    inv_freq = ROPE_THETA ** (-jnp.arange(0, dim, 2, dtype=jnp.float32) / dim)
    ang = positions.astype(jnp.float32)[..., None] * inv_freq
    return jnp.cos(ang), jnp.sin(ang)

def _apply_rope(x, cos, sin):
    half = x.shape[-1] // 2
    x1 = x[..., :half].astype(jnp.float32)
    x2 = x[..., half:].astype(jnp.float32)
    return jnp.concatenate([x1 * cos - x2 * sin, x2 * cos + x1 * sin], axis=-1).astype(x.dtype)

def _causal_mask(start, seq_len):
    q_idx = start + jnp.arange(Q_BLOCK)
    k_idx = jnp.arange(seq_len)
    return k_idx[None, :] <= q_idx[:, None]

def _query_block_sweep(block_fn, seq_len):
    n_blocks = seq_len // Q_BLOCK
    out = lax.map(block_fn, jnp.arange(n_blocks))
    nb, b, qb, w = out.shape
    return out.transpose(1, 0, 2, 3).reshape(b, nb * qb, w)

def _differential_attention(q, k, v, positions, lam, lambda_init, out_gain):
    b, s, h, _ = q.shape
    q = q.transpose(0, 2, 1, 3)
    k = k.transpose(0, 2, 1, 3)
    v = v.transpose(0, 2, 1, 3)
    q1, q2 = q[..., :DIFF_HALF_DIM], q[..., DIFF_HALF_DIM:]
    k1, k2 = k[..., :DIFF_HALF_DIM], k[..., DIFF_HALF_DIM:]
    slopes = _alibi_slopes(h)
    scale = DIFF_HALF_DIM ** -0.5
    pos_f = positions.astype(jnp.float32)
    gain = out_gain.astype(jnp.float32) * (1.0 - lambda_init)

    def block_fn(i):
        start = i * Q_BLOCK
        qb1 = lax.dynamic_slice_in_dim(q1, start, Q_BLOCK, axis=2)
        qb2 = lax.dynamic_slice_in_dim(q2, start, Q_BLOCK, axis=2)
        pos_q = lax.dynamic_slice_in_dim(pos_f, start, Q_BLOCK, axis=1)
        dist = jnp.abs(pos_q[:, :, None] - pos_f[:, None, :])
        bias = -slopes[None, :, None, None] * dist[:, None]
        mask = _causal_mask(start, s)

        def attn_map(qb, kk):
            sc = jnp.einsum('bhqd,bhkd->bhqk', qb, kk, preferred_element_type=jnp.float32) * scale + bias
            return jax.nn.softmax(jnp.where(mask, sc, NEG_INF), axis=-1)

        a = attn_map(qb1, k1) - lam * attn_map(qb2, k2)
        o = jnp.einsum('bhqk,bhkd->bhqd', a.astype(v.dtype), v, preferred_element_type=jnp.float32)
        o = o * lax.rsqrt(jnp.mean(o * o, axis=-1, keepdims=True) + RMS_EPS) * gain
        return o.transpose(0, 2, 1, 3).reshape(b, Q_BLOCK, h * DIFF_V_DIM).astype(v.dtype)

    return _query_block_sweep(block_fn, s)

def _latent_attention(q, k, v):
    b, s, h, _ = q.shape
    q = q.transpose(0, 2, 1, 3)
    k = k.transpose(0, 2, 1, 3)
    v = v.transpose(0, 2, 1, 3)
    scale = MLA_QK_DIM ** -0.5

    def block_fn(i):
        start = i * Q_BLOCK
        qb = lax.dynamic_slice_in_dim(q, start, Q_BLOCK, axis=2)
        sc = jnp.einsum('bhqd,bhkd->bhqk', qb, k, preferred_element_type=jnp.float32) * scale
        p = jax.nn.softmax(jnp.where(_causal_mask(start, s), sc, NEG_INF), axis=-1)
        o = jnp.einsum('bhqk,bhkd->bhqd', p.astype(v.dtype), v, preferred_element_type=jnp.float32)
        return o.transpose(0, 2, 1, 3).reshape(b, Q_BLOCK, h * MLA_V_DIM).astype(v.dtype)

    return _query_block_sweep(block_fn, s)

def _memory_cross_attention(h, mem_n, w_q, w_kv, w_o):
    b, s, _ = h.shape
    n_mem = mem_n.shape[1]
    q = (h @ w_q).reshape(b, s, MEM_HEADS, MEM_HEAD_DIM)
    kv = (mem_n @ w_kv).reshape(b, n_mem, 2, MEM_HEADS, MEM_HEAD_DIM)
    k, v = kv[:, :, 0], kv[:, :, 1]
    sc = jnp.einsum('bshd,bmhd->bhsm', q, k, preferred_element_type=jnp.float32) * MEM_HEAD_DIM ** -0.5
    p = jax.nn.softmax(sc, axis=-1)
    o = jnp.einsum('bhsm,bmhd->bshd', p.astype(v.dtype), v).reshape(b, s, MEM_WIDTH)
    return o @ w_o

def _hierarchical_moe(h, w_group_router, b_group_router, w_expert_router, b_expert_router,
                      w_gate, w_up, w_down):
    b, s, d = h.shape
    n_tok = b * s
    hf = h.reshape(n_tok, d)
    g_logits = jnp.einsum('td,dg->tg', hf, w_group_router, preferred_element_type=jnp.float32) \
        + b_group_router.astype(jnp.float32)
    g_probs = jax.nn.softmax(g_logits, axis=-1)
    g_gate, g_sel = lax.top_k(g_probs, 1)
    e_logits = jnp.einsum('td,de->te', hf, w_expert_router, preferred_element_type=jnp.float32) \
        + b_expert_router.astype(jnp.float32)
    e_logits = e_logits.reshape(n_tok, N_GROUPS, EXPERTS_PER_GROUP)
    e_logits = jnp.take_along_axis(e_logits, g_sel[:, :, None], axis=1)[:, 0]
    e_probs = jax.nn.softmax(e_logits, axis=-1)
    e_gate, e_sel = lax.top_k(e_probs, TOP_K_IN_GROUP)
    e_gate = e_gate / jnp.sum(e_gate, axis=-1, keepdims=True)
    weights = (g_gate * e_gate).reshape(-1)
    expert_ids = (g_sel * EXPERTS_PER_GROUP + e_sel).reshape(-1)
    token_ids = jnp.repeat(jnp.arange(n_tok, dtype=jnp.int32), TOP_K_IN_GROUP)

    n_assign = n_tok * TOP_K_IN_GROUP
    n_blocks = -(-(n_assign + N_EXPERTS * (EXPERT_BLOCK - 1)) // EXPERT_BLOCK)
    n_slots = n_blocks * EXPERT_BLOCK
    order = jnp.argsort(expert_ids)
    sorted_e = expert_ids[order]
    counts = jnp.bincount(expert_ids, length=N_EXPERTS)
    padded = ((counts + EXPERT_BLOCK - 1) // EXPERT_BLOCK) * EXPERT_BLOCK
    seg_start = jnp.cumsum(counts) - counts
    padded_end = jnp.cumsum(padded)
    padded_start = padded_end - padded
    dest = padded_start[sorted_e] + (jnp.arange(n_assign) - seg_start[sorted_e])
    slot_token = jnp.full((n_slots,), n_tok, jnp.int32).at[dest].set(token_ids[order])
    slot_weight = jnp.zeros((n_slots,), jnp.float32).at[dest].set(weights[order])
    block_expert = jnp.minimum(
        jnp.searchsorted(padded_end, jnp.arange(n_blocks) * EXPERT_BLOCK, side='right'), N_EXPERTS - 1)
    h_pad = jnp.concatenate([hf, jnp.zeros((1, d), hf.dtype)], axis=0)

    def block_fn(args):
        tok, wt, e = args
        xb = h_pad[tok]
        hidden = jax.nn.silu(xb @ w_gate[e]) * (xb @ w_up[e])
        return (hidden @ w_down[e]) * wt[:, None].astype(hf.dtype)

    y = lax.map(block_fn, (slot_token.reshape(n_blocks, EXPERT_BLOCK),
                           slot_weight.reshape(n_blocks, EXPERT_BLOCK),
                           block_expert))
    out = jnp.zeros((n_tok + 1, d), hf.dtype).at[slot_token].add(y.reshape(n_slots, d))[:n_tok]
    return out.reshape(b, s, d)

def first_inputs(seed: int = 0) -> dict:
    key = jax.random.key(seed)
    ks = jax.random.split(key, 30)

    def w(k, shape, fan_in):
        return jax.random.normal(k, shape, jnp.float32) * fan_in ** -0.5

    def gain(k, shape):
        return 1.0 + 0.02 * jax.random.normal(k, shape, jnp.float32)

    x = jax.random.normal(ks[0], (BATCH, SEQ, D_MODEL), jnp.float32)
    mem = jax.random.normal(ks[1], (BATCH, N_MEM, D_MODEL), jnp.float32)
    offset = jax.random.randint(ks[2], (BATCH, 1), 0, POS_OFFSET_MAX, jnp.int32)
    positions = (offset + jnp.arange(SEQ, dtype=jnp.int32)[None, :]).astype(jnp.int32)
    return {
        'x': x,
        'mem': mem,
        'positions': positions,
        'norm_mix_g': gain(ks[3], (DEPTH, D_MODEL)),
        'w_in': w(ks[4], (DEPTH, D_MODEL, IN_PROJ_WIDTH), D_MODEL),
        'diff_lambda_q1': 0.1 * jax.random.normal(ks[5], (DEPTH, DIFF_HALF_DIM), jnp.float32),
        'diff_lambda_k1': 0.1 * jax.random.normal(ks[6], (DEPTH, DIFF_HALF_DIM), jnp.float32),
        'diff_lambda_q2': 0.1 * jax.random.normal(ks[7], (DEPTH, DIFF_HALF_DIM), jnp.float32),
        'diff_lambda_k2': 0.1 * jax.random.normal(ks[8], (DEPTH, DIFF_HALF_DIM), jnp.float32),
        'diff_out_g': gain(ks[9], (DEPTH, DIFF_V_DIM)),
        'mla_q_norm_g': gain(ks[10], (DEPTH, MLA_Q_RANK)),
        'w_mla_uq': w(ks[11], (DEPTH, MLA_Q_RANK, MLA_HEADS * MLA_QK_DIM), MLA_Q_RANK),
        'mla_kv_norm_g': gain(ks[12], (DEPTH, MLA_KV_RANK)),
        'w_mla_ukv': w(ks[13], (DEPTH, MLA_KV_RANK, MLA_HEADS * (MLA_NOPE_DIM + MLA_V_DIM)), MLA_KV_RANK),
        'mla_out_g': gain(ks[14], (DEPTH, MLA_WIDTH)),
        'w_out': w(ks[15], (DEPTH, MIX_WIDTH, D_MODEL), MIX_WIDTH),
        'norm_cross_g': gain(ks[16], (DEPTH, D_MODEL)),
        'norm_mem_g': gain(ks[17], (DEPTH, D_MODEL)),
        'w_mem_q': w(ks[18], (DEPTH, D_MODEL, MEM_WIDTH), D_MODEL),
        'w_mem_kv': w(ks[19], (DEPTH, D_MODEL, 2 * MEM_WIDTH), D_MODEL),
        'w_mem_o': w(ks[20], (DEPTH, MEM_WIDTH, D_MODEL), MEM_WIDTH),
        'norm_ffn_g': gain(ks[21], (DEPTH, D_MODEL)),
        'w_group_router': w(ks[22], (DEPTH, D_MODEL, N_GROUPS), D_MODEL),
        'b_group_router': 0.01 * jax.random.normal(ks[23], (DEPTH, N_GROUPS), jnp.float32),
        'w_expert_router': w(ks[24], (DEPTH, D_MODEL, N_EXPERTS), D_MODEL),
        'b_expert_router': 0.01 * jax.random.normal(ks[25], (DEPTH, N_EXPERTS), jnp.float32),
        'w_expert_gate': w(ks[26], (DEPTH, N_EXPERTS, D_MODEL, EXPERT_FF), D_MODEL),
        'w_expert_up': w(ks[27], (DEPTH, N_EXPERTS, D_MODEL, EXPERT_FF), D_MODEL),
        'w_expert_down': w(ks[28], (DEPTH, N_EXPERTS, EXPERT_FF, D_MODEL), EXPERT_FF),
        'norm_final_g': gain(ks[29], (D_MODEL,)),
    }

def first_block(x, mem, positions, norm_mix_g, w_in, diff_lambda_q1, diff_lambda_k1,
              diff_lambda_q2, diff_lambda_k2, diff_out_g, mla_q_norm_g, w_mla_uq,
              mla_kv_norm_g, w_mla_ukv, mla_out_g, w_out, norm_cross_g, norm_mem_g,
              w_mem_q, w_mem_kv, w_mem_o, norm_ffn_g, w_group_router, b_group_router,
              w_expert_router, b_expert_router, w_expert_gate, w_expert_up, w_expert_down,
              norm_final_g):
    b, s, _ = x.shape
    cos, sin = _rope_angles(positions, MLA_ROPE_DIM)
    for l in range(DEPTH):
        h = _rms_norm(x, norm_mix_g[l])
        proj = h @ w_in[l]
        q_d, k_d, v_d, c_q, c_kv, k_pe = jnp.split(proj, IN_SPLITS, axis=-1)

        lambda_init = 0.8 - 0.6 * math.exp(-0.3 * l)
        lam = (jnp.exp(jnp.sum(diff_lambda_q1[l].astype(jnp.float32) * diff_lambda_k1[l].astype(jnp.float32)))
               - jnp.exp(jnp.sum(diff_lambda_q2[l].astype(jnp.float32) * diff_lambda_k2[l].astype(jnp.float32)))
               + lambda_init)
        diff_out = _differential_attention(
            q_d.reshape(b, s, DIFF_HEADS, 2 * DIFF_HALF_DIM),
            k_d.reshape(b, s, DIFF_HEADS, 2 * DIFF_HALF_DIM),
            v_d.reshape(b, s, DIFF_HEADS, DIFF_V_DIM),
            positions, lam, lambda_init, diff_out_g[l])

        q_m = (_rms_norm(c_q, mla_q_norm_g[l]) @ w_mla_uq[l]).reshape(b, s, MLA_HEADS, MLA_QK_DIM)
        q_nope, q_pe = q_m[..., :MLA_NOPE_DIM], q_m[..., MLA_NOPE_DIM:]
        q_pe = _apply_rope(q_pe, cos[:, :, None, :], sin[:, :, None, :])
        q_m = jnp.concatenate([q_nope, q_pe], axis=-1)
        kv_m = (_rms_norm(c_kv, mla_kv_norm_g[l]) @ w_mla_ukv[l]).reshape(
            b, s, MLA_HEADS, MLA_NOPE_DIM + MLA_V_DIM)
        k_nope, v_m = kv_m[..., :MLA_NOPE_DIM], kv_m[..., MLA_NOPE_DIM:]
        k_pe = _apply_rope(k_pe, cos, sin)
        k_m = jnp.concatenate(
            [k_nope, jnp.broadcast_to(k_pe[:, :, None, :], (b, s, MLA_HEADS, MLA_ROPE_DIM))], axis=-1)
        mla_out = _rms_norm(_latent_attention(q_m, k_m, v_m), mla_out_g[l])

        x = x + jnp.concatenate([diff_out, mla_out], axis=-1) @ w_out[l]

        x = x + _memory_cross_attention(_rms_norm(x, norm_cross_g[l]), _rms_norm(mem, norm_mem_g[l]),
                                        w_mem_q[l], w_mem_kv[l], w_mem_o[l])

        x = x + _hierarchical_moe(_rms_norm(x, norm_ffn_g[l]), w_group_router[l], b_group_router[l],
                                  w_expert_router[l], b_expert_router[l],
                                  w_expert_gate[l], w_expert_up[l], w_expert_down[l])
    return _rms_norm(x, norm_final_g)


DEPTH_2 = 2

N_A_LAYERS = DEPTH_2 // 2
N_B_LAYERS = DEPTH_2 - N_A_LAYERS
EPS = 1e-6

GDN_HEADS = 6
GDN_DK = 128
GDN_DV = 128
GDN_QK_W = GDN_HEADS * GDN_DK
GDN_V_W = GDN_HEADS * GDN_DV
CONV_K = 4
CHUNK = 64

SWA_HEADS = 12
SWA_KV_HEADS = 2
SWA_DH = 64
SWA_GROUP = SWA_HEADS // SWA_KV_HEADS
SWA_Q_W = SWA_HEADS * SWA_DH
KV_W = SWA_KV_HEADS * SWA_DH
WINDOW = 128
SWA_BLOCK = 128
ROPE_THETA_2 = 500000.0
ROT_DIM = SWA_DH // 4

MEM_LEN = 256
MEM_DH = 64
MEM_W = MEM_HEADS * MEM_DH

D_MIX = GDN_V_W + MEM_W
GDN_IN = 2 * GDN_QK_W + 2 * GDN_V_W + 2 * GDN_HEADS + MEM_W
SWA_IN = SWA_Q_W + MEM_W
D_FF = -(-8 * D_MODEL // (3 * 256)) * 256


def rms_norm(x, g):
    xf = x.astype(jnp.float32)
    y = xf * lax.rsqrt(jnp.mean(xf * xf, axis=-1, keepdims=True) + EPS)
    return (y * g.astype(jnp.float32)).astype(x.dtype)

def l2_normalize(x):
    xf = x.astype(jnp.float32)
    return xf * lax.rsqrt(jnp.sum(xf * xf, axis=-1, keepdims=True) + EPS)

def rope_tables(positions):
    inv = ROPE_THETA_2 ** (-jnp.arange(0, ROT_DIM, 2, dtype=jnp.float32) / ROT_DIM)
    ang = positions.astype(jnp.float32)[..., None] * inv
    return jnp.cos(ang), jnp.sin(ang)

def apply_partial_rope(x, cos, sin):
    half = ROT_DIM // 2
    xf = x.astype(jnp.float32)
    x1, x2 = xf[..., :half], xf[..., half:ROT_DIM]
    c, s = cos[:, :, None, :], sin[:, :, None, :]
    out = jnp.concatenate([x1 * c - x2 * s, x2 * c + x1 * s, xf[..., ROT_DIM:]], axis=-1)
    return out.astype(x.dtype)

def causal_depthwise_conv(x, w):
    c = x.shape[-1]
    return lax.conv_general_dilated(
        x, w[:, None, :].astype(x.dtype), window_strides=(1,), padding=[(CONV_K - 1, 0)],
        dimension_numbers=("NWC", "WIO", "NWC"), feature_group_count=c)

def swiglu(h, w_gate_up, w_down):
    gu = h @ w_gate_up
    return (jax.nn.silu(gu[..., :D_FF]) * gu[..., D_FF:]) @ w_down

def gated_delta_rule_chunked(q, k, v, g, beta):
    b_sz, s_len, n_h, dk = q.shape
    dv = v.shape[-1]
    n_ch = s_len // CHUNK

    def chunks(t):
        t = t.reshape((b_sz, n_ch, CHUNK, n_h) + t.shape[3:])
        return jnp.moveaxis(t, 3, 1)

    q = chunks(q) * (dk ** -0.5)
    k = chunks(k)
    v = chunks(v)
    beta = chunks(beta)
    gc = jnp.cumsum(chunks(g), axis=-1)
    tril = jnp.tril(jnp.ones((CHUNK, CHUNK), dtype=bool))
    strict = jnp.tril(jnp.ones((CHUNK, CHUNK), dtype=bool), -1)
    decay = jnp.exp(jnp.where(tril, gc[..., :, None] - gc[..., None, :], -jnp.inf))
    kb = k * beta[..., None]
    lower = jnp.where(strict, jnp.einsum("bhncd,bhnkd->bhnck", kb, k) * decay, 0.0)
    rhs = jnp.concatenate([v * beta[..., None], kb * jnp.exp(gc)[..., None]], axis=-1)
    sol = lax.linalg.triangular_solve(lower, rhs, left_side=True, lower=True, unit_diagonal=True)
    u, w = sol[..., :dv], sol[..., dv:]
    intra = jnp.einsum("bhncd,bhnkd->bhnck", q, k) * decay
    q_g = q * jnp.exp(gc)[..., None]
    k_g = k * jnp.exp(gc[..., -1:] - gc)[..., None]
    g_last = jnp.exp(gc[..., -1])
    xs = tuple(jnp.moveaxis(t, 2, 0) for t in (u, w, intra, q_g, k_g, g_last))

    def step(state, inp):
        u_n, w_n, a_n, qg_n, kg_n, gl_n = inp
        v_new = u_n - jnp.einsum("bhck,bhkv->bhcv", w_n, state)
        o_n = jnp.einsum("bhck,bhkv->bhcv", qg_n, state) + jnp.einsum("bhcs,bhsv->bhcv", a_n, v_new)
        state = state * gl_n[..., None, None] + jnp.einsum("bhck,bhcv->bhkv", kg_n, v_new)
        return state, o_n

    s0 = jnp.zeros((b_sz, n_h, dk, dv), jnp.float32)
    _, o = lax.scan(step, s0, xs)
    return jnp.transpose(o, (1, 0, 3, 2, 4)).reshape(b_sz, s_len, n_h, dv)

def gated_deltanet_mixer(h, w_in, conv_w, a_log, dt_bias, norm_g):
    b_sz, s_len, _ = h.shape
    proj = h @ w_in
    o1 = 2 * GDN_QK_W + GDN_V_W
    qkv = jax.nn.silu(causal_depthwise_conv(proj[..., :o1], conv_w))
    z = proj[..., o1:o1 + GDN_V_W]
    o2 = o1 + GDN_V_W
    b_logit = proj[..., o2:o2 + GDN_HEADS].astype(jnp.float32)
    a_logit = proj[..., o2 + GDN_HEADS:o2 + 2 * GDN_HEADS].astype(jnp.float32)
    mem_q = proj[..., o2 + 2 * GDN_HEADS:]
    q = l2_normalize(qkv[..., :GDN_QK_W].reshape(b_sz, s_len, GDN_HEADS, GDN_DK))
    k = l2_normalize(qkv[..., GDN_QK_W:2 * GDN_QK_W].reshape(b_sz, s_len, GDN_HEADS, GDN_DK))
    v = qkv[..., 2 * GDN_QK_W:].reshape(b_sz, s_len, GDN_HEADS, GDN_DV).astype(jnp.float32)
    beta = jax.nn.sigmoid(b_logit)
    g = -jnp.exp(a_log.astype(jnp.float32)) * jax.nn.softplus(a_logit + dt_bias.astype(jnp.float32))
    o = gated_delta_rule_chunked(q, k, v, g, beta)
    o = rms_norm(o, norm_g) * jax.nn.silu(z.reshape(b_sz, s_len, GDN_HEADS, GDN_DV).astype(jnp.float32))
    return o.reshape(b_sz, s_len, GDN_V_W).astype(h.dtype), mem_q

def sliding_window_attention(q, k, v, sinks):
    b_sz, s_len = q.shape[:2]
    nb = s_len // SWA_BLOCK
    qb = q.reshape(b_sz, nb, SWA_BLOCK, SWA_KV_HEADS, SWA_GROUP, SWA_DH)
    kb = k.reshape(b_sz, nb, SWA_BLOCK, SWA_KV_HEADS, SWA_DH)
    vb = v.reshape(b_sz, nb, SWA_BLOCK, SWA_KV_HEADS, SWA_DH)
    pad = jnp.zeros_like(kb[:, :1])
    kw = jnp.concatenate([jnp.concatenate([pad, kb[:, :-1]], axis=1), kb], axis=2)
    vw = jnp.concatenate([jnp.concatenate([pad, vb[:, :-1]], axis=1), vb], axis=2)
    s = jnp.einsum("bnqhgd,bnkhd->bnhgqk", qb, kw).astype(jnp.float32) * (SWA_DH ** -0.5)
    qi = jnp.arange(SWA_BLOCK)[:, None] + SWA_BLOCK
    ki = jnp.arange(2 * SWA_BLOCK)[None, :]
    diff = qi - ki
    band = (diff >= 0) & (diff < WINDOW)
    has_prev = jnp.arange(nb) > 0
    mask = band[None] & (has_prev[:, None, None] | (ki >= SWA_BLOCK)[None])
    s = jnp.where(mask[None, :, None, None], s, -jnp.inf)
    sink = sinks.astype(jnp.float32).reshape(SWA_KV_HEADS, SWA_GROUP)[None, None, :, :, None, None]
    m = jnp.maximum(jnp.max(s, axis=-1, keepdims=True), sink)
    p = jnp.exp(s - m)
    p = (p / (jnp.sum(p, axis=-1, keepdims=True) + jnp.exp(sink - m))).astype(v.dtype)
    o = jnp.einsum("bnhgqk,bnkhd->bnqhgd", p, vw)
    return o.reshape(b_sz, s_len, SWA_Q_W)

def memory_attention(q, mem_k, mem_v):
    s = jnp.einsum("bshd,bmhd->bhsm", q, mem_k).astype(jnp.float32) * (MEM_DH ** -0.5)
    p = jax.nn.softmax(s, axis=-1).astype(q.dtype)
    o = jnp.einsum("bhsm,bmhd->bshd", p, mem_v)
    return o.reshape(q.shape[0], q.shape[1], MEM_W)

def second_inputs(seed: int = 0) -> dict:
    key = jax.random.key(seed)
    ks = jax.random.split(key, 24)
    f32 = jnp.float32

    def dense(k, shape, fan_in):
        return jax.random.normal(k, shape, f32) * (fan_in ** -0.5)

    def gain(k, shape):
        return 1.0 + 0.02 * jax.random.normal(k, shape, f32)

    x = jax.random.normal(ks[0], (BATCH, SEQ, D_MODEL), f32)
    mem = jax.random.normal(ks[1], (BATCH, MEM_LEN, D_MODEL), f32)
    positions = (jnp.arange(SEQ, dtype=jnp.int32)[None, :]
                 + jax.random.randint(ks[2], (BATCH, 1), 0, 4096, dtype=jnp.int32))
    dt0 = jnp.exp(jax.random.uniform(ks[15], (N_A_LAYERS, GDN_HEADS), f32,
                                     math.log(1e-3), math.log(1e-1)))
    return {
        "x": x,
        "mem": mem,
        "positions": positions,
        "ln_mix": gain(ks[3], (DEPTH_2, D_MODEL)),
        "ln_ffn": gain(ks[4], (DEPTH_2, D_MODEL)),
        "ln_mem": gain(ks[5], (D_MODEL,)),
        "w_mem_kv": dense(ks[6], (DEPTH_2, D_MODEL, 2 * MEM_W), D_MODEL),
        "w_out": dense(ks[7], (DEPTH_2, D_MIX, D_MODEL), D_MIX),
        "w_gate_up": dense(ks[8], (DEPTH_2, D_MODEL, 2 * D_FF), D_MODEL),
        "w_down": dense(ks[9], (DEPTH_2, D_FF, D_MODEL), D_FF),
        "gdn_w_in": dense(ks[10], (N_A_LAYERS, D_MODEL, GDN_IN), D_MODEL),
        "gdn_conv": dense(ks[11], (N_A_LAYERS, CONV_K, 2 * GDN_QK_W + GDN_V_W), CONV_K),
        "gdn_A_log": jnp.log(jax.random.uniform(ks[12], (N_A_LAYERS, GDN_HEADS), f32, 1.0, 16.0)),
        "gdn_dt_bias": dt0 + jnp.log(-jnp.expm1(-dt0)),
        "gdn_norm": gain(ks[13], (N_A_LAYERS, GDN_DV)),
        "swa_w_q": dense(ks[14], (N_B_LAYERS, D_MODEL, SWA_IN), D_MODEL),
        "swa_sinks": 0.5 * jax.random.normal(ks[16], (N_B_LAYERS, SWA_HEADS), f32),
        "ln_kv": gain(ks[17], (D_MODEL,)),
        "w_kv": dense(ks[18], (D_MODEL, 2 * KV_W), D_MODEL),
        "ln_final": gain(ks[19], (D_MODEL,)),
    }

def second_block(x, mem, positions, ln_mix, ln_ffn, ln_mem, w_mem_kv, w_out, w_gate_up, w_down,
              gdn_w_in, gdn_conv, gdn_A_log, gdn_dt_bias, gdn_norm,
              swa_w_q, swa_sinks, ln_kv, w_kv, ln_final):
    b_sz, s_len, _ = x.shape
    cos, sin = rope_tables(positions)
    mem_n = rms_norm(mem, ln_mem)
    shared_k = None
    shared_v = None
    for layer in range(DEPTH_2):
        h = rms_norm(x, ln_mix[layer])
        mkv = mem_n @ w_mem_kv[layer]
        mem_k = mkv[..., :MEM_W].reshape(b_sz, MEM_LEN, MEM_HEADS, MEM_DH)
        mem_v = mkv[..., MEM_W:].reshape(b_sz, MEM_LEN, MEM_HEADS, MEM_DH)
        if layer < N_A_LAYERS:
            a = layer
            mix_out, mem_q = gated_deltanet_mixer(h, gdn_w_in[a], gdn_conv[a], gdn_A_log[a],
                                                  gdn_dt_bias[a], gdn_norm[a])
        else:
            bl = layer - N_A_LAYERS
            proj = h @ swa_w_q[bl]
            q = apply_partial_rope(proj[..., :SWA_Q_W].reshape(b_sz, s_len, SWA_HEADS, SWA_DH), cos, sin)
            mix_out = sliding_window_attention(q, shared_k, shared_v, swa_sinks[bl])
            mem_q = proj[..., SWA_Q_W:]
        mem_o = memory_attention(mem_q.reshape(b_sz, s_len, MEM_HEADS, MEM_DH), mem_k, mem_v)
        x = x + jnp.concatenate([mix_out.astype(x.dtype), mem_o.astype(x.dtype)], axis=-1) @ w_out[layer]
        x = x + swiglu(rms_norm(x, ln_ffn[layer]), w_gate_up[layer], w_down[layer])
        if layer == N_A_LAYERS - 1:
            kv = rms_norm(x, ln_kv) @ w_kv
            shared_k = apply_partial_rope(kv[..., :KV_W].reshape(b_sz, s_len, SWA_KV_HEADS, SWA_DH), cos, sin)
            shared_v = kv[..., KV_W:].reshape(b_sz, s_len, SWA_KV_HEADS, SWA_DH)
    return rms_norm(x, ln_final)


def setup_inputs(seed=0):
    out = dict(first_inputs(seed))
    for name, value in second_inputs(seed + 1).items():
        if name != "x":
            out[name + "_2"] = value
    return out


def reference(
    x, mem, positions, norm_mix_g, w_in, diff_lambda_q1, diff_lambda_k1, diff_lambda_q2,
    diff_lambda_k2, diff_out_g, mla_q_norm_g, w_mla_uq, mla_kv_norm_g, w_mla_ukv, mla_out_g,
    w_out, norm_cross_g, norm_mem_g, w_mem_q, w_mem_kv, w_mem_o, norm_ffn_g, w_group_router,
    b_group_router, w_expert_router, b_expert_router, w_expert_gate, w_expert_up, w_expert_down,
    norm_final_g, mem_2, positions_2, ln_mix_2, ln_ffn_2, ln_mem_2, w_mem_kv_2, w_out_2,
    w_gate_up_2, w_down_2, gdn_w_in_2, gdn_conv_2, gdn_A_log_2, gdn_dt_bias_2, gdn_norm_2,
    swa_w_q_2, swa_sinks_2, ln_kv_2, w_kv_2, ln_final_2,
):
    x = first_block(
        x, mem, positions, norm_mix_g, w_in, diff_lambda_q1, diff_lambda_k1, diff_lambda_q2,
        diff_lambda_k2, diff_out_g, mla_q_norm_g, w_mla_uq, mla_kv_norm_g, w_mla_ukv, mla_out_g,
        w_out, norm_cross_g, norm_mem_g, w_mem_q, w_mem_kv, w_mem_o, norm_ffn_g, w_group_router,
        b_group_router, w_expert_router, b_expert_router, w_expert_gate, w_expert_up,
        w_expert_down, norm_final_g,
    )
    return second_block(
        x, mem_2, positions_2, ln_mix_2, ln_ffn_2, ln_mem_2, w_mem_kv_2, w_out_2, w_gate_up_2,
        w_down_2, gdn_w_in_2, gdn_conv_2, gdn_A_log_2, gdn_dt_bias_2, gdn_norm_2, swa_w_q_2,
        swa_sinks_2, ln_kv_2, w_kv_2, ln_final_2,
    )


_drawn_inputs = setup_inputs


def setup_inputs(seed=0):
    import zlib

    import numpy as np

    out = dict(_drawn_inputs(seed))
    spreads = {}
    factors = {'diff_lambda_q2': 3.245,
     'diff_lambda_k2': 7.009,
     'norm_cross_g': 8.0,
     'norm_mem_g': 5.101,
     'b_group_router': 5.846,
     'b_expert_router': 3.158,
     'ln_mix_2': 3.029,
     'ln_ffn_2': 2.937,
     'ln_mem_2': 8.0,
     'gdn_norm_2': 5.245,
     'swa_sinks_2': 35.524,
     'ln_kv_2': 8.0}
    for name, (base, spread) in spreads.items():
        noise = np.random.default_rng([zlib.crc32(name.encode()), seed]).standard_normal(out[name].shape)
        drawn = base * np.exp(spread * noise) if base else spread * noise
        out[name] = jnp.asarray(drawn.astype(out[name].dtype))
    for name, factor in factors.items():
        out[name] = (out[name] * factor).astype(out[name].dtype)
    return out
```

```python
import math
from collections import defaultdict
from contextlib import ExitStack

import concourse.bass as bass
import numpy as np
from concourse import mybir

F32 = mybir.dt.float32
F32R = mybir.dt.float32r
I32 = mybir.dt.int32
U32 = mybir.dt.uint32
ALU = mybir.AluOpType
ACT = mybir.ActivationFunctionType
AX_X = mybir.AxisListType.X

P = 128
S = 512
D = 1024
KT = D // P
QT = S // P
NMEM = 256
EPS = 1e-6
NEG = -1e30

DIFF_HEADS, DIFF_HALF, DIFF_V = 8, 32, 64
MLA_HEADS, MLA_NOPE, MLA_ROPE, MLA_V = 8, 64, 32, 64
MLA_QK = MLA_NOPE + MLA_ROPE
MEM_HEADS, MEM_DH1, MEM_DH2 = 4, 128, 64
N_GROUPS, PER_GROUP = 4, 8
N_EXPERTS = N_GROUPS * PER_GROUP
EXPERT_FF = 256
SLOTS = 128
NB_MAX = -(-(2 * S + N_EXPERTS * (SLOTS - 1)) // SLOTS)
NBC = NB_MAX + 1
LAMBDA_INIT = 0.8 - 0.6 * math.exp(0.0)

GDN_HEADS, GDN_D = 6, 128
GDN_W = GDN_HEADS * GDN_D
CONV_K = 4
SWA_HEADS, SWA_KV, SWA_DH, SWA_ROT = 12, 2, 64, 16
D_FF = 2816
FF_TILES = D_FF // P
FF_PARTS = (8, 7, 7)
RING, SPLIT, BANKS = 6, 3, 2

CONST = {}
_w = 0
for _n, _k in (("ident", P), ("upper", P), ("lower", P), ("incl", P), ("causal", P), ("prev", P),
               ("ones", P), ("blk64", P), ("perm_mla", P), ("perm_swa", P), ("first_level", P),
               ("levels", 7 * P), ("iota", 48), ("cols", 8)):
    CONST[_n] = (_w, _k)
    _w += _k
CONST_W = _w
C_INV_MLA, C_SIGN_MLA, C_INV_SWA, C_SIGN_SWA, C_TOKEN, C_EPS = range(6)

VEC = {}
_w = 0
for _n, _k in (("norm_mix", KT), ("norm_cross", KT), ("norm_mem", KT), ("norm_ffn", KT), ("ln_mem", KT),
               ("ln_mix0", KT), ("ln_mix1", KT), ("ln_ffn0", KT), ("ln_ffn1", KT), ("ln_kv", KT),
               ("ln_final", KT), ("mla_q", 2), ("mla_kv", 1), ("mla_out", 4), ("diff_out", 1),
               ("gdn_norm", 1), ("conv", 18 * CONV_K), ("sinks", SWA_HEADS), ("lam", 4 * DIFF_HALF),
               ("a_log", 1), ("dt", 1), ("router_b", 36), ("norm_final", KT)):
    VEC[_n] = (_w, _k)
    _w += _k
VEC_W = _w

STAGES = [("in", 15, KT, P, S), ("kpe", 1, KT, MLA_ROPE, S), ("uq", MLA_HEADS, 2, MLA_QK, S),
          ("ukv", MLA_HEADS, 1, P, S), ("out", KT, KT, P, S),
          ("memkv", 8, KT, P, NMEM), ("memq", 4, KT, P, S), ("memo", KT, 4, P, S),
          ("mem2", 8, KT, P, NMEM),
          ("gdnin", 26, KT, P, S), ("ba", 2, KT, GDN_HEADS, S), ("out0", KT, KT, P, S)]
for _l in range(2):
    if _l == 1:
        STAGES += [("kv", 3, KT, P, S), ("swaq", 8, KT, P, S), ("out1", KT, KT, P, S)]
    for _p, _n in enumerate(FF_PARTS):
        STAGES += [(f"gu{_l}{_p}", 2 * _n, KT, P, S), (f"down{_l}{_p}", KT, _n, P, S)]
BASE = {}
_t = 0
for _s in STAGES:
    BASE[_s[0]] = _t
    _t += _s[1]
N_TILES = _t
MOE_AT = BASE["mem2"]
STAGE_OF = {_s[0]: _s for _s in STAGES}
TILE = [_s for _s in STAGES for _ in range(_s[1])]


class Events:

    def __init__(self, nc, ctx, plan):
        self.nc, self.ctx, self.plan = nc, ctx, plan
        self.sems, self.count, self.seen, self.waited = {}, {}, {}, {}

    def sem(self, name):
        if name not in self.sems:
            self.sems[name] = self.ctx.enter_context(self.nc.semaphore(name))
        return self.sems[name]

    def done(self, ins, name, label=None, by=1):
        ins.then_inc(self.sem(name), by)
        self.count[name] = self.count.get(name, 0) + by
        if label is not None:
            self.seen[name, label] = self.count[name]

    def wait(self, eng, name, value):
        if self.waited.get((id(eng), name), 0) < value:
            eng.wait_ge(self.sem(name), value)
            self.waited[id(eng), name] = value

    def need(self, eng, name, label):
        self.wait(eng, name, self.plan[name, label])

    def step(self, eng, ins, name, label=None):
        self.done(ins, name, label)
        self.wait(eng, name, self.count[name])


def program(nc, a, plan, stop=None):
    with ExitStack() as ctx:
        ev = Events(nc, ctx, plan)
        done, need, step = ev.done, ev.need, ev.step

        at = [16512]

        def place(name, shape, dt, where=None):
            size = int(np.prod(shape[1:])) * 4
            off = at[0] if where is None else where
            if where is None:
                at[0] += -(-size // 32) * 32
            return nc.alloc_sbuf_tensor_at(name, shape, dt, offset=off), off

        X, _ = place("x", [P, KT, S], F32)
        AR, ar_at = place("split_acts", [P, 32, S], F32R)
        AF, _ = place("split_acts_as_f32", [P, 32, S], F32, ar_at)
        WRAW, _ = place("w_raw", [P, RING, 1024], F32)
        WH, _ = place("w_high", [P, SPLIT, 1024], F32R)
        WL, _ = place("w_low", [P, SPLIT, 1024], F32R)
        H, _ = place("h", [P, 8, S], F32)
        SC, sc_at = place("scratch", [P, 2, S], F32)
        G, g_at = place("g", [P, 24, S], F32)
        GI, _ = place("g_as_int", [P, 24, S], I32, g_at)
        CB, _ = place("consts", [P, CONST_W], F32)
        VB, _ = place("vectors", [P, VEC_W], F32)
        COL, col_at = place("columns", [P, 96], F32)
        COLI, _ = place("columns_as_int", [P, 96], I32, col_at)
        COLU, _ = place("columns_as_uint", [P, 96], U32, col_at)

        ps = [ctx.enter_context(nc.psum_tensor(f"ps{i}", [P, 512], F32)) for i in range(8)]
        ps_lin, ps_s, ps_t, ps_o, ps_m = ps[0:2], ps[2:4], ps[4:6], ps[6], ps[7]

        def const(name, rows=P):
            o, w = CONST[name]
            return CB[0:rows, o:o + w]

        def col(i, rows=slice(0, P)):
            o = CONST["cols"][0] + i
            return CB[rows, o:o + 1]

        def vec(name, i=0, n=1, rows=slice(0, P)):
            o = VEC[name][0] + i
            return VB[rows, o:o + n]

        ident = const("ident")
        slot_tok = nc.dram_tensor("slot_tok", [P * NBC, 1], I32).ap()
        rows_h = nc.dram_tensor("rows_h", [S, D], F32).ap()
        rows_y = nc.dram_tensor("rows_y", [(NB_MAX + 2) * SLOTS, D], F32).ap()

        w_loaded = [ctx.enter_context(nc.semaphore(f"w_loaded{i}")) for i in range(RING)]
        high_ready, low_ready, tile_done = (ctx.enter_context(nc.semaphore(n))
                                            for n in ("high_ready", "low_ready", "tile_done"))
        evacuated = [ctx.enter_context(nc.semaphore(f"evacuated{i}")) for i in range(BANKS)]

        def wait_evac(eng, t):
            eng.wait_ge(evacuated[t % BANKS], t // BANKS + 1)

        def wait_stage_evac(eng, name, upto=None):
            last = BASE[name] + (STAGE_OF[name][1] if upto is None else upto) - 1
            for t in (last - 1, last):
                if t >= BASE[name]:
                    wait_evac(eng, t)

        def wait_products(eng, name):
            eng.wait_ge(tile_done, BASE[name] + STAGE_OF[name][1])

        def segment_end(t):
            return MOE_AT if t < MOE_AT else N_TILES

        def split_high(act, t):
            _, _, kt, m, _ = TILE[t]
            act.wait_ge(w_loaded[t % RING], 16 * (t // RING + 1))
            if t >= SPLIT:
                act.wait_ge(tile_done, t - SPLIT + 1)
            act.activation(WH[:, t % SPLIT, 0:kt * m], WRAW[:, t % RING, 0:kt * m],
                           ACT.Copy).then_inc(high_ready, 1)

        def split_low(dve, t):
            _, _, kt, m, _ = TILE[t]
            dve.wait_ge(high_ready, t + 1)
            dve.tensor_tensor(WL[:, t % SPLIT, 0:kt * m], WRAW[:, t % RING, 0:kt * m],
                              WH[:, t % SPLIT, 0:kt * m].bitcast(F32), ALU.subtract).then_inc(low_ready, 1)

        AHEAD = SPLIT - 1

        class Linear:

            def __init__(self, name, high, low, ready, take_act=None, take_dve=None, before=None):
                self.name, self.high, self.low, self.ready = name, high, low, ready
                self.take_act, self.take_dve, self.before = take_act, take_dve, before
                _, self.nt, self.kt, self.m, self.n = STAGE_OF[name]
                self.base = BASE[name]

            def tensor(self, pe):
                for j in range(self.nt):
                    t = self.base + j
                    pe.wait_ge(low_ready, t + 1)
                    if t >= BANKS:
                        wait_evac(pe, t - BANKS)
                    out = ps_lin[t % BANKS][0:self.m, 0:self.n]
                    w = slice(0, self.kt * self.m)
                    wh = WH[:, t % SPLIT, w].rearrange("p (k m) -> p k m", m=self.m)
                    wl = WL[:, t % SPLIT, w].rearrange("p (k m) -> p k m", m=self.m)
                    for k in range(self.kt):
                        if j == 0 and self.ready is not None:
                            need(pe, *self.ready(k))
                        pe.matmul(out, wh[:, k, :], self.high(k), start=(k == 0), stop=False)
                        pe.matmul(out, wh[:, k, :], self.low(k), start=False, stop=False)
                        last = pe.matmul(out, wl[:, k, :], self.high(k), start=False, stop=(k == self.kt - 1))
                    last.then_inc(tile_done, 1)

            def scalar(self, act):
                if self.before:
                    self.before(act)
                for j in range(self.nt):
                    t = self.base + j
                    if t + AHEAD < segment_end(t):
                        split_high(act, t + AHEAD)
                    if self.take_act:
                        self.take_act(act, j, t, ps_lin[t % BANKS][0:self.m, 0:self.n])

            def vector(self, dve):
                for j in range(self.nt):
                    t = self.base + j
                    if t + AHEAD < segment_end(t):
                        split_low(dve, t + AHEAD)
                    if self.take_dve:
                        self.take_dve(dve, j, t, ps_lin[t % BANKS][0:self.m, 0:self.n])

        class Prime:

            def __init__(self, t0):
                self.t0 = t0

            def tensor(self, pe):
                pass

            def scalar(self, act):
                for t in range(self.t0, self.t0 + AHEAD):
                    split_high(act, t)

            def vector(self, dve):
                for t in range(self.t0, self.t0 + AHEAD):
                    split_low(dve, t)

        def taker(dest, waits=None):
            def take(act, j, t, out):
                if j == 0 and waits:
                    waits(act)
                act.wait_ge(tile_done, t + 1)
                act.copy(dest(j), out).then_inc(evacuated[t % BANKS], 1)
            return take

        def add_to_x(dve, j, t, out):
            dve.wait_ge(tile_done, t + 1)
            dve.tensor_tensor(X[:, j, :], X[:, j, :], out, ALU.add).then_inc(evacuated[t % BANKS], 1)

        shared = {"n": 0}

        class Norm:

            def __init__(self, name, kt, width, src, gain, dst, high, low, wait_src, wait_dst=None, scale=1.0 / D, ones=None, squares=24):
                self.name, self.kt, self.width, self.src = name, kt, width, src
                self.gain, self.dst, self.high, self.low = gain, dst, high, low
                self.wait_src, self.wait_dst, self.scale, self.ones = wait_src, wait_dst, scale, ones
                self.squares = squares
                self.ones = const("ones") if ones is None else ones
                self.n = shared["n"]
                shared["n"] += 1
                self.sq = AF[:, squares:squares + 8, :].rearrange("p k s -> p (k s)")

            def scalar(self, act):
                w = self.width
                self.wait_src(act)
                for k in range(self.kt):
                    done(act.activation(self.sq[:, k * w:(k + 1) * w], self.src(k), ACT.Square),
                         "norm_act", (self.name, "sq", k))
                need(act, "norm_pe", (self.name, "sum"))
                done(act.activation(SC[:, 0, 0:w], ps_m[:, 0:w], ACT.Sqrt, bias=col(C_EPS), scale=self.scale),
                     "norm_act", (self.name, "root"))
                if self.high is None:
                    return
                for k in range(self.kt):
                    if k == 0 and self.wait_dst:
                        self.wait_dst(act)
                    need(act, "norm_dve", (self.name, "h", k))
                    done(act.activation(self.high(k), self.dst(k), ACT.Copy), "norm_act", (self.name, "high", k))

            def vector(self, dve):
                w = self.width
                for k in range(self.kt):
                    need(dve, "norm_act", (self.name, "sq", k))
                    if k:
                        step(dve, dve.tensor_tensor(self.sq[:, 0:w], self.sq[:, 0:w],
                                                    self.sq[:, k * w:(k + 1) * w], ALU.add),
                             "norm_dve", (self.name, "sum"))
                need(dve, "norm_act", (self.name, "root"))
                step(dve, dve.reciprocal(SC[:, 0, 0:w], SC[:, 0, 0:w]), "norm_dve", (self.name, "rstd"))
                for k in range(self.kt):
                    if k == 0 and self.wait_dst:
                        self.wait_dst(dve)
                    done(dve.scalar_tensor_tensor(out=self.dst(k), in0=self.src(k), scalar=self.gain(k),
                                                  in1=SC[:, 0, 0:w], op0=ALU.mult, op1=ALU.mult),
                         "norm_dve", (self.name, "h", k))
                    if self.high is not None and k:
                        self.lower(dve, k - 1)
                if self.high is not None:
                    self.lower(dve, self.kt - 1)

            def lower(self, dve, k):
                need(dve, "norm_act", (self.name, "high", k))
                done(dve.tensor_tensor(self.low(k), self.dst(k), self.high(k).bitcast(F32), ALU.subtract),
                     "norm_dve", (self.name, "low", k))

            def tensor(self, pe):
                w = self.width
                if self.kt > 1:
                    need(pe, "norm_dve", (self.name, "sum"))
                else:
                    need(pe, "norm_act", (self.name, "sq", 0))
                if (self.name, "free") in ps_m_free:
                    need(pe, *ps_m_free[self.name, "free"])
                done(pe.matmul(ps_m[:, 0:w], self.ones, self.sq[:, 0:w], start=True, stop=True),
                     "norm_pe", (self.name, "sum"))

            def ready(self, k):
                return "norm_dve", (self.name, "low", k)

        ps_m_free = {}

        class Split:

            def __init__(self, name, kt, src, high, low, waits):
                self.name, self.kt, self.src, self.high, self.low, self.waits = name, kt, src, high, low, waits

            def tensor(self, pe):
                pass

            def scalar(self, act):
                self.waits(act)
                for k in range(self.kt):
                    done(act.activation(self.high(k), self.src(k), ACT.Copy), "split_act", (self.name, k))

            def vector(self, dve):
                self.waits(dve)
                for k in range(self.kt):
                    need(dve, "split_act", (self.name, k))
                    done(dve.tensor_tensor(self.low(k), self.src(k), self.high(k).bitcast(F32), ALU.subtract),
                         "split_dve", (self.name, k))

            def ready(self, k):
                return "split_dve", (self.name, k)

        class On:

            def __init__(self, tensor=None, scalar=None, vector=None, gpsimd=None, sync=None):
                nothing = lambda eng: None
                self.tensor, self.scalar, self.vector = tensor or nothing, scalar or nothing, vector or nothing
                self.gpsimd, self.sync = gpsimd or nothing, sync or nothing

        turns = {"n": 0}

        class Transposes:

            def __init__(self, name, groups, wait_first=None):
                self.name, self.groups, self.wait_first = name, groups, wait_first
                self.t0 = turns["n"]
                turns["n"] += len(groups)

            def tensor(self, pe):
                if self.wait_first:
                    self.wait_first(pe)
                for g, (blocks, _, waits) in enumerate(self.groups):
                    if waits:
                        waits(pe)
                    n = self.t0 + g
                    if n >= 2:
                        need(pe, "turn_act", n - 2)
                    elif n == 0:
                        pass
                    last = None
                    for b, (src, at_) in enumerate(blocks):
                        rows = src.shape[0]
                        wid = src.shape[1]
                        last = pe.transpose(ps_t[n % 2][0:wid, at_:at_ + rows], src, ident[0:rows, 0:rows])
                    done(last, "turn_pe", n)

            def scalar(self, act):
                for g, (blocks, (dst, src_of), _) in enumerate(self.groups):
                    n = self.t0 + g
                    need(act, "turn_pe", n)
                    if g == 0 and self.wait_first:
                        self.wait_first(act)
                    done(act.copy(dst, src_of(ps_t[n % 2])), "turn_act", n)

            def vector(self, dve):
                pass

        att_m, att_h = {"n": 0}, {"n": 0}

        class Attention:

            def __init__(self, name, heads, kind, scale, scores, width, probs, turned, pv, out, wait_scores, wait_v, wait_out=None, keys=None):
                self.name, self.heads, self.kind, self.scale = name, heads, kind, scale
                self.scores, self.width, self.probs, self.turned = scores, width, probs, turned
                self.pv, self.out, self.wait_scores, self.wait_v = pv, out, wait_scores, wait_v
                self.wait_out, self.keys = wait_out, keys
                self.maps = 2 if kind == "alibi" else 1
                self.m0, self.u0, self.h0 = att_m["n"], turns["n"], att_h["n"]
                att_m["n"] += heads * QT * self.maps
                turns["n"] += heads * QT
                att_h["n"] += heads
                self.units = [(h, i) for h in range(heads) for i in range(QT)]

            def prob(self, m):
                return self.probs[m % len(self.probs)]

            def tensor(self, pe):
                self.wait_scores(pe)
                self.pe_scores(pe, 0)
                for n in range(len(self.units)):
                    if n + 1 < len(self.units):
                        self.pe_scores(pe, n + 1)
                    self.pe_turn(pe, n)
                    if n and self.units[n - 1][1] == QT - 1:
                        self.pe_values(pe, self.units[n - 1][0])
                self.pe_values(pe, self.heads - 1)

            def pe_scores(self, pe, n):
                h, i = self.units[n]
                for r in range(self.maps):
                    m = self.m0 + n * self.maps + r
                    if m >= 2:
                        need(pe, "att_act", ("exp", m - 2))
                    lhs, rhs = self.scores(h, i, r)
                    done(pe.matmul(ps_s[m % 2][:, 0:self.width(i)], lhs, rhs, start=True, stop=True),
                         "att_pe", ("scores", m))

            def pe_turn(self, pe, n):
                h, i = self.units[n]
                u = self.u0 + n
                need(pe, "att_dve", ("probs", u))
                if u >= 2:
                    need(pe, "turn_act", u - 2)
                src = self.prob(n * self.maps)
                nb = self.width(i) // P
                for b in range(nb):
                    last = pe.transpose(ps_t[u % 2][:, b * P:(b + 1) * P], src[:, b * P:(b + 1) * P], ident)
                done(last, "turn_pe", u)

            def pe_values(self, pe, h):
                g = self.h0 + h
                if h == 0:
                    self.wait_v(pe)
                need(pe, "turn_act", self.u0 + h * QT + QT - 1)
                if g:
                    need(pe, "att_act", ("out", g - 1))
                rows, plan_ = self.pv(h)
                for lhs, (slot, src, q0, q1), first, lastk in plan_:
                    last = pe.matmul(ps_o[rows, q0:q1], lhs, self.turned[h % 2][:, slot, src:src + q1 - q0],
                                     start=first, stop=lastk, skip_group_check=True)
                done(last, "att_pe", ("values", g))

            def scalar(self, act):
                self.act_exp(act, 0)
                for n in range(len(self.units)):
                    if n + 1 < len(self.units):
                        self.act_exp(act, n + 1)
                    self.act_turn(act, n)
                    if n and self.units[n - 1][1] == QT - 1:
                        self.act_out(act, self.units[n - 1][0])
                self.act_out(act, self.heads - 1)

            def act_exp(self, act, n):
                h, i = self.units[n]
                w = self.width(i)
                for r in range(self.maps):
                    lm = n * self.maps + r
                    m = self.m0 + lm
                    need(act, "att_dve", ("max", m))
                    if lm >= 4:
                        need(act, "turn_pe", self.u0 + (lm - 4) // self.maps)
                    src = self.prob(lm)[:, 0:w] if self.kind == "alibi" else ps_s[m % 2][:, 0:w]
                    if self.kind == "window":
                        done(act.activation(COL[:, 24 + m % 8:25 + m % 8], vec("sinks", h), ACT.Exp,
                                            bias=COL[:, m % 8:m % 8 + 1]), "att_act", ("sink", m))
                    done(act.activation(self.prob(lm)[:, 0:w], src, ACT.Exp, bias=COL[:, m % 8:m % 8 + 1],
                                        scale=self.scale, accum_out=COL[:, 8 + m % 8:9 + m % 8]),
                         "att_act", ("exp", m))

            def act_turn(self, act, n):
                h, i = self.units[n]
                u, nb = self.u0 + n, self.width(i) // P
                need(act, "turn_pe", u)
                if n == 0 and self.wait_out:
                    self.wait_out(act)
                if i == 0 and h >= 2:
                    need(act, "att_pe", ("values", self.h0 + h - 2))
                done(act.copy(self.turned[h % 2][:, 0:nb, i * P:(i + 1) * P],
                              ps_t[u % 2][:, 0:nb * P].rearrange("p (b q) -> p b q", q=P)), "turn_act", u)

            def act_out(self, act, h):
                g = self.h0 + h
                rows, _ = self.pv(h)
                need(act, "att_pe", ("values", g))
                done(act.copy(self.out(h), ps_o[rows, :]), "att_act", ("out", g))

            def vector(self, dve):
                self.dve_max(dve, 0)
                for n in range(len(self.units)):
                    if n + 1 < len(self.units):
                        self.dve_max(dve, n + 1)
                    self.dve_probs(dve, n)

            def dve_max(self, dve, n):
                h, i = self.units[n]
                w = self.width(i)
                for r in range(self.maps):
                    lm = n * self.maps + r
                    m = self.m0 + lm
                    need(dve, "att_pe", ("scores", m))
                    s = ps_s[m % 2][:, 0:w]
                    if self.kind == "alibi":
                        if lm >= 4:
                            need(dve, "turn_pe", self.u0 + (lm - 4) // self.maps)
                        slope = 2.0 ** (-8.0 * (h + 1) / DIFF_HEADS)
                        s = self.prob(lm)[:, 0:w]
                        step(dve, dve.scalar_tensor_tensor(out=s, in0=minus_dist(i), scalar=slope / self.scale,
                                                           in1=ps_s[m % 2][:, 0:w], op0=ALU.mult, op1=ALU.add),
                             "att_dve")
                    elif self.kind == "causal":
                        diag = ps_s[m % 2][:, i * P:(i + 1) * P]
                        step(dve, dve.tensor_tensor(diag, diag, const("causal"), ALU.add), "att_dve")
                    elif self.kind == "window":
                        mask = CB[:, CONST["causal"][0]:CONST["causal"][0] + 2 * P]
                        if i == 0:
                            step(dve, dve.tensor_tensor(s, s, mask[:, 0:P], ALU.add), "att_dve")
                        else:
                            step(dve, dve.tensor_tensor(s[:, 0:P], s[:, 0:P], mask[:, P:2 * P], ALU.add), "att_dve")
                            step(dve, dve.tensor_tensor(s[:, P:2 * P], s[:, P:2 * P], mask[:, 0:P], ALU.add),
                                 "att_dve")
                    c = COL[:, m % 8:m % 8 + 1]
                    step(dve, dve.tensor_reduce(c, s, AX_X, ALU.max), "att_dve")
                    if self.kind == "window":
                        step(dve, dve.tensor_scalar(c, c, self.scale, vec("sinks", h), ALU.mult, ALU.max), "att_dve")
                        step(dve, dve.tensor_scalar(c, c, -1.0, None, ALU.mult), "att_dve", ("max", m))
                    else:
                        step(dve, dve.tensor_scalar(c, c, -self.scale, None, ALU.mult), "att_dve", ("max", m))

            def dve_probs(self, dve, n):
                h, i = self.units[n]
                w, m = self.width(i), self.m0 + n * self.maps
                need(dve, "att_act", ("exp", m + self.maps - 1))
                inv = []
                for r in range(self.maps):
                    tot = COL[:, 8 + (m + r) % 8:9 + (m + r) % 8]
                    inv.append(COL[:, 16 + (m + r) % 8:17 + (m + r) % 8])
                    if self.kind == "window":
                        step(dve, dve.tensor_tensor(tot, tot, COL[:, 24 + m % 8:25 + m % 8], ALU.add), "att_dve")
                    step(dve, dve.reciprocal(inv[r], tot), "att_dve")
                p0 = self.prob(n * self.maps)[:, 0:w]
                if self.kind == "alibi":
                    p1 = self.prob(n * self.maps + 1)[:, 0:w]
                    step(dve, dve.tensor_scalar(p1, p1, inv[1], LAM, ALU.mult, ALU.mult), "att_dve")
                    done(dve.scalar_tensor_tensor(out=p0, in0=p0, scalar=inv[0], in1=p1, op0=ALU.mult,
                                                  op1=ALU.subtract), "att_dve", ("probs", self.u0 + n))
                else:
                    done(dve.tensor_scalar(p0, p0, inv[0], None, ALU.mult), "att_dve", ("probs", self.u0 + n))

        LAM = COL[:, 32:33]
        DIST_OFF = [P * (i * (i + 1) // 2) for i in range(QT + 1)]
        dist = AF[:, 20:23, :].rearrange("p k s -> p (k s)")

        def minus_dist(i):
            return dist[:, DIST_OFF[i]:DIST_OFF[i + 1]]

        class HeadNorm:

            def __init__(self, name, tiles, src, ones, scale, finish, wait_src):
                self.name, self.tiles, self.src, self.ones = name, tiles, src, ones
                self.scale, self.finish, self.wait_src = scale, finish, wait_src

            def tensor(self, pe):
                for k in range(self.tiles):
                    need(pe, "hn_act", (self.name, "sq", k))
                    if k:
                        need(pe, "hn_act", (self.name, "root", k - 1))
                    elif (self.name, "free") in ps_m_free:
                        need(pe, *ps_m_free[self.name, "free"])
                    done(pe.matmul(ps_m[:, :], self.ones, SC[:, k % 2, :], start=True, stop=True),
                         "hn_pe", (self.name, k))

            def scalar(self, act):
                self.wait_src(act)
                for k in range(self.tiles + 1):
                    if k < self.tiles:
                        if k >= 2:
                            need(act, "hn_dve", (self.name, k - 2))
                        done(act.activation(SC[:, k % 2, :], self.src(k), ACT.Square), "hn_act",
                             (self.name, "sq", k))
                    if k:
                        need(act, "hn_pe", (self.name, k - 1))
                        done(act.activation(SC[:, (k - 1) % 2, :], ps_m[:, :], ACT.Sqrt, bias=col(C_EPS),
                                            scale=self.scale), "hn_act", (self.name, "root", k - 1))

            def vector(self, dve):
                for k in range(self.tiles):
                    need(dve, "hn_act", (self.name, "root", k))
                    s = SC[:, k % 2, :]
                    step(dve, dve.reciprocal(s, s), "hn_dve")
                    self.finish(dve, k, s, (self.name, k))

        def g(k, n=None):
            return G[:, k, :] if n is None else G[:, k:k + n, :]

        def load_waits(eng, *names):
            for n in names:
                ev.wait(eng, "ld_" + n, 16)

        lam_v = VEC["lam"][0]

        def early_vector(dve):
            load_waits(dve, "const", "vec", "pos", "posc")
            for i in range(2):
                step(dve, dve.tensor_tensor_reduce(out=SC[:, 0, 32 * i:32 * i + 32],
                                                   in0=vec("lam", 64 * i, 32), in1=vec("lam", 64 * i + 32, 32),
                                                   scale=1.0, scalar=0.0, op0=ALU.mult, op1=ALU.add,
                                                   accum_out=COL[:, 34 + i:35 + i]), "early_dve", ("lam", i))
            step(dve, dve.tensor_copy(g(18), GI[:, 16, :]), "early_dve")
            step(dve, dve.tensor_copy(COL[:, 36:40], COLI[:, 40:44]), "early_dve")
            for i in range(QT):
                w = (i + 1) * P
                step(dve, dve.tensor_scalar(minus_dist(i), G[:, 18, 0:w], COL[:, 36 + i:37 + i], None,
                                            ALU.subtract), "early_dve")
                step(dve, dve.scalar_tensor_tensor(out=minus_dist(i), in0=minus_dist(i), scalar=-1.0,
                                                   in1=minus_dist(i), op0=ALU.mult, op1=ALU.min), "early_dve")
                diag = minus_dist(i)[:, i * P:w]
                step(dve, dve.tensor_tensor(diag, diag, const("causal"), ALU.add), "early_dve")
            need(dve, "early_act", "lam")
            step(dve, dve.tensor_tensor(LAM, COL[:, 34:35], COL[:, 35:36], ALU.subtract), "early_dve")
            step(dve, dve.tensor_scalar(LAM, LAM, LAMBDA_INIT, None, ALU.add), "early_dve")
            step(dve, dve.tensor_scalar(COL[:, 33:34], vec("diff_out"), 1.0 - LAMBDA_INIT, None, ALU.mult),
                 "early_dve")

        def early_scalar(act):
            need(act, "early_dve", ("lam", 1))
            for i in range(2):
                done(act.activation(COL[:, 34 + i:35 + i], COL[:, 34 + i:35 + i], ACT.Exp), "early_act", "lam")

        TWO_PI_PARTS = (6.28125, 0.0019350051879882812, 2 * math.pi - 6.28125 - 0.0019350051879882812)

        class Angles:

            def __init__(self, name, pos, inv, sign, cos, sin, wait):
                self.name, self.pos, self.inv, self.sign = name, pos, inv, sign
                self.cos, self.sin, self.wait = cos, sin, wait

            def tensor(self, pe):
                pass

            def vector(self, dve):
                st = lambda ins, label=None: step(dve, ins, "angle_dve", label)
                self.wait(dve)
                pos_i, ang, k, ki = self.pos, g(18), g(19), GI[:, 19, :]
                st(dve.tensor_copy(ang, pos_i))
                st(dve.tensor_scalar(ang, ang, self.inv, None, ALU.mult))
                for out, turn, shift in ((self.sin, 0.0, 0.0), (self.cos, 0.25, math.pi / 2)):
                    st(dve.tensor_scalar(ki, ang, 1.0 / (2 * math.pi), turn, ALU.mult, ALU.add))
                    st(dve.tensor_copy(k, ki))
                    st(dve.tensor_copy(out, ang))
                    for c in TWO_PI_PARTS:
                        st(dve.scalar_tensor_tensor(out=out, in0=k, scalar=-c, in1=out, op0=ALU.mult, op1=ALU.add))
                    if shift:
                        st(dve.tensor_scalar(out, out, shift, None, ALU.add))
                    for sgn, cmp in ((1.0, ALU.is_gt), (-1.0, ALU.is_lt)):
                        st(dve.tensor_scalar(k, out, sgn * math.pi, -sgn * 2 * math.pi, cmp, ALU.mult))
                        st(dve.tensor_tensor(out, out, k, ALU.add))
                    st(dve.tensor_scalar(out, out, 3.1415925, -3.1415925, ALU.min, ALU.max),
                       (self.name, "arg", shift > 0))
                need(dve, "angle_act", self.name)
                st(dve.tensor_scalar(self.sin, self.sin, self.sign, None, ALU.mult), (self.name, "table"))

            def scalar(self, act):
                for out, shift in ((self.sin, False), (self.cos, True)):
                    need(act, "angle_dve", (self.name, "arg", shift))
                    done(act.activation(out, out, ACT.Sin), "angle_act", self.name)

        ropes = {"n": 0}

        class Rope:

            def __init__(self, name, tiles, rows, perm, cos, sin, waits):
                self.name, self.tiles, self.rows, self.perm = name, tiles, rows, perm
                self.cos, self.sin, self.waits = cos, sin, waits

            def tensor(self, pe):
                for k in range(len(self.tiles)):
                    if k == 0:
                        self.waits(pe)
                    need_n = ("rope_dve", (self.name, "swap", k - 1))
                    if k:
                        need(pe, *need_n)
                    done(pe.matmul(ps_m[0:self.rows, :], self.perm[0:self.rows, 0:self.rows],
                                   self.tiles[k], start=True, stop=True), "rope_pe", (self.name, k))

            def scalar(self, act):
                pass

            def vector(self, dve):
                r = slice(0, self.rows)
                for k, x in enumerate(self.tiles):
                    need(dve, "rope_pe", (self.name, k))
                    s = SC[r, k % 2, :]
                    step(dve, dve.tensor_tensor(s, ps_m[r, :], self.sin[r, :], ALU.mult), "rope_dve",
                         (self.name, "swap", k))
                    step(dve, dve.tensor_tensor(x, x, self.cos[r, :], ALU.mult), "rope_dve")
                    step(dve, dve.tensor_tensor(x, x, s, ALU.add), "rope_dve", (self.name, k))

        hi = lambda k: AR[:, k, :]
        lo = lambda k: AR[:, 8 + k, :]
        x_tile = lambda k: X[:, k, :]
        h_tile = lambda k: H[:, k, :]
        fl = []

        cos_m, sin_m = g(20), g(21)
        fl.append(On(scalar=early_scalar, vector=early_vector))
        fl.append(Angles("mla", GI[:, 16, :], col(C_INV_MLA), col(C_SIGN_MLA), cos_m, sin_m,
                         lambda e: load_waits(e, "pos")))
        n_mix = Norm("mix", KT, S, x_tile, lambda k: vec("norm_mix", k), h_tile, hi, lo,
                     lambda e: load_waits(e, "x", "const", "vec"))
        fl += [Prime(0), n_mix]
        in_dest = lambda j: (g(j) if j < 8 else AF[:, 16 + j - 8, :] if j < 12 else g(j))
        fl.append(Linear("in", hi, lo, n_mix.ready, taker(in_dest)))
        fl.append(Linear("kpe", hi, lo, None, taker(lambda j: G[0:MLA_ROPE, 15, :])))
        fl.append(Transposes("diff_v", [
            ([(AF[:, 16 + c, i * P:(i + 1) * P], c * P) for c in range(4)],
             (g(8 + i), lambda b: b[:, :]), None) for i in range(QT)],
            wait_first=lambda e: wait_stage_evac(e, "in", 12)))

        def diff_scores(h, i, r):
            p0 = 64 * (h % 2) + 32 * r
            return (G[p0:p0 + 32, h // 2, i * P:(i + 1) * P], G[p0:p0 + 32, 4 + h // 2, 0:(i + 1) * P])

        def causal_pv(v, heads_per_tile=2):
            def pv(h):
                rows = slice(64 * (h % 2), 64 * (h % 2) + 64)
                return rows, [(v(h, j), (j, j * P, j * P, S), j == 0, j == QT - 1) for j in range(QT)]
            return pv

        turned4 = (AF[:, 8:12, :], AF[:, 12:16, :])
        grow = lambda i: (i + 1) * P
        probs4 = [g(16 + k) for k in range(4)]
        out_rows = lambda h: slice(64 * (h % 2), 64 * (h % 2) + 64)
        diff = Attention("diff", DIFF_HEADS, "alibi", DIFF_HALF ** -0.5, diff_scores, grow, probs4, turned4,
                         causal_pv(lambda h, j: G[:, 8 + j, h * 64:(h + 1) * 64]),
                         lambda h: H[out_rows(h), h // 2, :],
                         lambda e: wait_stage_evac(e, "in", 8), lambda e: None,
                         wait_out=lambda e: wait_products(e, "kpe"))
        fl.append(diff)
        last_head = lambda att: (lambda e: need(e, "att_act", ("out", att.h0 + att.heads - 1)))

        n_cq = Norm("cq", 2, S, lambda k: g(12 + k), lambda k: vec("mla_q", k), lambda k: g(12 + k),
                    lambda k: AR[:, k, :], lambda k: AR[:, 2 + k, :], lambda e: wait_stage_evac(e, "in"),
                    scale=1.0 / 256)
        n_ckv = Norm("ckv", 1, S, lambda k: g(14), lambda k: vec("mla_kv"), lambda k: g(14),
                     lambda k: AR[:, 4, :], lambda k: AR[:, 5, :], lambda e: None, scale=1.0 / 128)
        fl += [n_cq, n_ckv]
        fl.append(Linear("uq", lambda k: AR[:, k, :], lambda k: AR[:, 2 + k, :], n_cq.ready,
                         taker(lambda h: AF[0:MLA_QK, 16 + h, :])))
        fl.append(Linear("ukv", lambda k: AR[:, 4, :], lambda k: AR[:, 5, :], n_ckv.ready,
                         taker(lambda h: AF[:, 24 + h, :])))

        def kpe_tile(dve):
            wait_evac(dve, BASE["kpe"])
            step(dve, dve.memset(G[0:64, 2, :], 0.0), "mla_dve")
            step(dve, dve.tensor_copy(G[64:96, 2, :], G[0:32, 15, :]), "mla_dve", "kpe")

        fl.append(On(vector=kpe_tile))
        mla_v = Transposes("mla_v", [
            ([(AF[:, 24 + h, i * P:(i + 1) * P], i * P) for i in range(QT)],
             (G[:, 4:8, h * 64:(h + 1) * 64],
              lambda b: b[:, :].rearrange("p (i c) -> p i c", c=P)[:, :, 64:128]), None)
            for h in range(MLA_HEADS)], wait_first=lambda e: wait_stage_evac(e, "ukv"))
        fl.append(mla_v)
        rope_q = Rope("mla_q", [AF[0:96, 16 + h, :] for h in range(MLA_HEADS)] + [G[0:96, 2, :]], 96,
                      const("perm_mla"), cos_m, sin_m,
                      lambda e: (wait_stage_evac(e, "uq"), need(e, "mla_dve", "kpe")))
        fl.append(rope_q)

        def spread_kpe(act):
            need(act, "rope_dve", ("mla_q", MLA_HEADS))
            need(act, "turn_act", mla_v.t0 + MLA_HEADS - 1)
            for h in range(MLA_HEADS):
                done(act.copy(AF[64:96, 24 + h, :], G[64:96, 2, :]), "mla_act", "keys")

        fl.append(On(scalar=spread_kpe))
        mla = Attention("mla", MLA_HEADS, "causal", MLA_QK ** -0.5,
                        lambda h, i, r: (AF[0:96, 16 + h, i * P:(i + 1) * P], AF[0:96, 24 + h, 0:(i + 1) * P]),
                        grow, probs4, turned4, causal_pv(lambda h, j: G[:, 4 + j, h * 64:(h + 1) * 64]),
                        lambda h: H[out_rows(h), 4 + h // 2, :],
                        lambda e: (need(e, "mla_act", "keys"), need(e, "rope_dve", ("mla_q", MLA_HEADS - 1))),
                        lambda e: None)
        fl.append(mla)

        def diff_gain(dve, k, s, label):
            done(dve.scalar_tensor_tensor(out=h_tile(k), in0=h_tile(k), scalar=COL[:, 33:34], in1=s,
                                          op0=ALU.mult, op1=ALU.mult), "hn_dve", label)

        fl.append(HeadNorm("diff", 4, h_tile, const("blk64"), 1.0 / DIFF_V, diff_gain, last_head(diff)))
        s_diff = Split("diff", 4, h_tile, hi, lo, lambda e: need(e, "hn_dve", ("diff", 3)))
        n_mo = Norm("mla_out", 4, S, lambda k: h_tile(4 + k), lambda k: vec("mla_out", k),
                    lambda k: h_tile(4 + k), lambda k: hi(4 + k), lambda k: lo(4 + k), last_head(mla),
                    scale=1.0 / S)
        fl += [s_diff, n_mo]
        fl.append(Linear("out", hi, lo, lambda k: s_diff.ready(k) if k < 4 else n_mo.ready(k - 4),
                         None, add_to_x))

        cuts = {"mix": (len(fl), lambda e: wait_stage_evac(e, "out"), BASE["memkv"])}

        memv = lambda k0: G[:, k0:k0 + 4, :].rearrange("p k (a s) -> p (k a) s", a=2)
        raw1 = memv(20)
        mh = AR[:, 16:20, :].rearrange("p k (a s) -> p (k a) s", a=2)
        ml = AR[:, 20:24, :].rearrange("p k (a s) -> p (k a) s", a=2)
        n_mem = Norm("mem", KT, NMEM, lambda k: raw1[:, k, :], lambda k: vec("norm_mem", k),
                     lambda k: raw1[:, k, :], lambda k: mh[:, k, :], lambda k: ml[:, k, :],
                     lambda e: (load_waits(e, "mem"), last_head(mla)(e)))
        n_mem.sq = H[:, 0:4, :].rearrange("p k s -> p (k s)")
        n_mem.wait_src = lambda e: (load_waits(e, "mem"), need(e, *n_mo.ready(3)), need(e, *s_diff.ready(3)))
        n_cross = Norm("cross", KT, S, x_tile, lambda k: vec("norm_cross", k), h_tile, hi, lo,
                       lambda e: wait_stage_evac(e, "out"),
                       wait_dst=lambda e: (wait_products(e, "out")))
        mk = memv(8)
        fl += [n_mem, Linear("memkv", lambda k: mh[:, k, :], lambda k: ml[:, k, :], n_mem.ready,
                             taker(lambda j: mk[:, j, :])), n_cross]
        fl.append(Linear("memq", hi, lo, n_cross.ready, taker(lambda j: g(4 + j))))
        mem_v = Transposes("mem_v", [
            ([(mk[:, 4 + c, i * P:(i + 1) * P], c * P) for c in range(4)], (g(12 + i), lambda b: b[:, :]), None)
            for i in range(2)], wait_first=lambda e: wait_stage_evac(e, "memkv"))
        fl.append(mem_v)
        cross = Attention("cross", MEM_HEADS, "full", MEM_DH1 ** -0.5,
                          lambda h, i, r: (G[:, 4 + h, i * P:(i + 1) * P], mk[:, h, :]),
                          lambda i: NMEM, probs4, (AF[:, 16:18, :], AF[:, 18:20, :]),
                          lambda h: (slice(0, P), [(G[:, 12 + j, h * P:(h + 1) * P], (j, 0, 0, S), j == 0, j == 1)
                                                   for j in range(2)]),
                          h_tile, lambda e: wait_stage_evac(e, "memq"), lambda e: None,
                          wait_out=lambda e: (wait_products(e, "memkv"), wait_products(e, "memq")))
        fl.append(cross)
        s_cross = Split("cross", 4, h_tile, hi, lo, last_head(cross))
        fl += [s_cross, Linear("memo", hi, lo, s_cross.ready, None, add_to_x)]
        cuts["cross"] = (len(fl), lambda e: wait_stage_evac(e, "memo"), MOE_AT)

        n_ffn = Norm("ffn", KT, S, x_tile, lambda k: vec("norm_ffn", k), h_tile, None, None,
                     lambda e: wait_stage_evac(e, "memo"))
        fl.append(n_ffn)
        GU32, _ = place("g_as_uint", [P, 24, S], U32, g_at)
        RW = G[:, 0, 0:KT * 36].rearrange("p (k c) -> p k c", c=36)
        LG = G[:, 1, 0:QT * 36].rearrange("p (t c) -> p t c", c=36)
        GL = G[:, 1, 160:192].rearrange("p (t c) -> p t c", c=8)
        SEL = G[:, 1, 192:224].rearrange("p (t c) -> p t c", c=8)
        TOP = G[:, 1, 256:512].rearrange("p (t c) -> p t c", c=64)
        TOPU = GU32[:, 1, 256:512].rearrange("p (t c) -> p t c", c=64)
        HOT = G[:, 2, 0:256].rearrange("p (t k e) -> p t k e", k=2, e=32)
        BOTH = G[:, 2, 256:384].rearrange("p (t e) -> p t e", e=32)
        BEG, NBF, END, NBI, POS, JUNK = (G[:, 3, 32 * k:32 * k + 32] for k in range(6))
        NBI = GI[:, 3, 96:128]
        DEST = G[:, 3, 256:264]
        DESTI, DBLK, DROW = (GI[:, 3, 264 + 8 * k:272 + 8 * k] for k in range(3))
        FBLK, FROW = G[:, 3, 288:296], G[:, 3, 296:304]
        IDX, YIDX = GU32[:, 3, 304:312], GU32[:, 17, 128:136]
        TOKI = GI[:, 3, 320:324]
        WTS = G[:, 17, 160:168].rearrange("p (t k) -> p t k", k=2)
        IDS, ID_COL = GI[:, 17, 0:NBC], GI[:, 18, 0:1]
        BLK_E, N_BLK = GI[0:1, 19, 0:NBC], GI[0:1, 19, 48:49]
        iota = const("iota")

        def router_tensor(pe):
            ev.wait(pe, "ld_router", 16)
            for i in range(QT):
                for k in range(KT):
                    need(pe, "norm_dve", ("ffn", "h", k))
                    last = pe.matmul(ps_m[:, i * 36:(i + 1) * 36], H[:, k, i * P:(i + 1) * P], RW[:, k, :],
                                     start=(k == 0), stop=(k == KT - 1))
            done(last, "route_pe", "logits")
            need(pe, "route_dve", "both")
            for i in range(QT):
                for j in range(i + 1):
                    pe.matmul(ps_m[:, 32 * i:32 * i + 32], const("upper") if j == i else const("ones"),
                              BOTH[:, j, :], start=(j == 0), stop=(j == i))
            for j in range(QT):
                last = pe.matmul(ps_m[:, 128:160], const("ones"), BOTH[:, j, :], start=(j == 0), stop=(j == QT - 1))
            done(last, "route_pe", "ranks")

        def router_scalar(act):
            for i in range(QT):
                need(act, "route_dve", ("neg", i))
                done(act.activation(TOP[:, i, 40:44], GL[:, i, 0:4], ACT.Exp, bias=TOP[:, i, 32:33],
                                    accum_out=TOP[:, i, 34:35]), "route_act")
                done(act.activation(TOP[:, i, 35:36], TOP[:, i, 17:18], ACT.Exp, bias=TOP[:, i, 33:34]),
                     "route_act", ("exp", i))

        def router_vector(dve):
            st = lambda ins, label=None: step(dve, ins, "route_dve", label)
            ts, tt = dve.tensor_scalar, dve.tensor_tensor
            load_waits(dve, "router")
            st(dve.memset(GL[:, :, :], -3e38))
            need(dve, "route_pe", "logits")
            for i in range(QT):
                st(tt(LG[:, i, :], ps_m[:, i * 36:(i + 1) * 36], vec("router_b", 0, 36), ALU.add))
            st(dve.tensor_copy(GL[:, :, 0:4], LG[:, :, 0:4]))
            for i in range(QT):
                st(dve.max(TOP[:, i, 0:8], GL[:, i, :]))
                st(dve.max_index(TOPU[:, i, 8:16], TOP[:, i, 0:8], GL[:, i, :]))
                st(dve.tensor_copy(TOP[:, i, 36:37], TOPU[:, i, 8:9]))
                st(ts(TOP[:, i, 48:52], iota[:, 0:4], TOP[:, i, 36:37], None, ALU.is_equal))
                st(ts(SEL[:, i, :], LG[:, i, 4:12], TOP[:, i, 48:49], None, ALU.mult))
                for q in range(1, 4):
                    st(dve.scalar_tensor_tensor(out=SEL[:, i, :], in0=LG[:, i, 4 + 8 * q:12 + 8 * q],
                                                scalar=TOP[:, i, 48 + q:49 + q], in1=SEL[:, i, :],
                                                op0=ALU.mult, op1=ALU.add))
                st(dve.max(TOP[:, i, 16:24], SEL[:, i, :]))
                st(dve.max_index(TOPU[:, i, 24:32], TOP[:, i, 16:24], SEL[:, i, :]))
                st(ts(TOP[:, i, 32:33], TOP[:, i, 0:1], -1.0, None, ALU.mult))
                st(ts(TOP[:, i, 33:34], TOP[:, i, 16:17], -1.0, None, ALU.mult), ("neg", i))
                st(dve.tensor_copy(TOP[:, i, 38:40], TOPU[:, i, 24:26]))
                st(ts(TOP[:, i, 37:38], TOP[:, i, 36:37], float(PER_GROUP), None, ALU.mult))
                st(ts(TOP[:, i, 38:40], TOP[:, i, 38:40], TOP[:, i, 37:38], None, ALU.add))
                for q in range(2):
                    st(ts(HOT[:, i, q, :], iota[:, 0:32], TOP[:, i, 38 + q:39 + q], None, ALU.is_equal))
                st(tt(BOTH[:, i, :], HOT[:, i, 0, :], HOT[:, i, 1, :], ALU.add), "both")
            for i in range(QT):
                need(dve, "route_act", ("exp", i))
                st(dve.reciprocal(TOP[:, i, 44:45], TOP[:, i, 34:35]))
                st(ts(TOP[:, i, 45:46], TOP[:, i, 35:36], 1.0, None, ALU.add))
                st(dve.reciprocal(TOP[:, i, 46:47], TOP[:, i, 45:46]))
                st(tt(WTS[:, i, 0:1], TOP[:, i, 44:45], TOP[:, i, 46:47], ALU.mult))
                st(tt(WTS[:, i, 1:2], WTS[:, i, 0:1], TOP[:, i, 35:36], ALU.mult))
            need(dve, "route_pe", "ranks")
            st(ts(NBI, ps_m[:, 128:160], float(SLOTS - 1), None, ALU.add))
            st(ts(NBI, NBI, 7, None, ALU.arith_shift_right))
            st(dve.tensor_copy(NBF, NBI))
            st(dve.tensor_tensor_scan(END, const("ones")[:, 0:32], NBF, 0.0, ALU.mult, ALU.add))
            st(tt(BEG, END, NBF, ALU.subtract))
            st(ts(BEG, BEG, float(SLOTS), None, ALU.mult))
            for i in range(QT):
                st(tt(POS, BEG, ps_m[:, 32 * i:32 * i + 32], ALU.add), "ranks_read")
                for q in range(2):
                    st(dve.tensor_tensor_reduce(out=JUNK, in0=HOT[:, i, q, :], in1=POS, scale=1.0, scalar=0.0,
                                                op0=ALU.mult, op1=ALU.add,
                                                accum_out=DEST[:, 2 * i + q:2 * i + q + 1]))
            st(dve.tensor_copy(YIDX, DEST))
            st(dve.tensor_copy(DESTI, DEST))
            st(ts(DBLK, DESTI, 7, None, ALU.arith_shift_right))
            st(ts(DROW, DESTI, SLOTS - 1, None, ALU.bitwise_and))
            st(dve.tensor_copy(FBLK, DBLK))
            st(dve.tensor_copy(FROW, DROW))
            st(dve.scalar_tensor_tensor(out=FROW, in0=FROW, scalar=float(NBC), in1=FBLK, op0=ALU.mult, op1=ALU.add))
            st(dve.tensor_copy(IDX, FROW))
            for i in range(QT):
                st(ts(TOKI[:, i:i + 1], col(C_TOKEN), float(i * P), None, ALU.add), "slots")
            table = AF[0:1, 16:19, :].rearrange("p k s -> p (k s)")[:, 0:NBC * 32].rearrange(
                "p (b e) -> p b e", e=32)
            st(tt(table, END[0:1, :].unsqueeze(1).to_broadcast([1, NBC, 32]),
                  iota[0:1, 0:NBC].unsqueeze(2).to_broadcast([1, NBC, 32]), ALU.is_le))
            st(dve.tensor_reduce(G[0:1, 19, 64:64 + NBC], table, AX_X, ALU.add))
            st(ts(BLK_E, G[0:1, 19, 64:64 + NBC], float(N_EXPERTS - 1), None, ALU.min))
            st(dve.tensor_copy(N_BLK, END[0:1, 31:32]), "plan")

        fl.append(On(tensor=router_tensor, scalar=router_scalar, vector=router_vector))
        rows_out = Transposes("rows", [
            ([(H[:, 4 * half + c, i * P:(i + 1) * P], c * P) for c in range(4)],
             (g(4 + 2 * i + half), lambda b: b[:, :]), None) for i in range(QT) for half in range(2)],
            wait_first=lambda e: need(e, "norm_dve", ("ffn", "h", KT - 1)))
        fl.append(rows_out)

        msem = lambda n: ctx.enter_context(nc.semaphore(n))
        m_load = [msem(f"m_load{p}") for p in range(6)]
        m_high, m_low, m_done = msem("m_high"), msem("m_low"), msem("m_done")
        x_ids, x_rows, x_turned, x_high, x_low = (msem(n) for n in ("x_ids", "x_rows", "x_turned", "x_high", "x_low"))
        m_silu, m_hidden, h_turned, h_high, h_low = (msem(n) for n in ("m_silu", "m_hidden", "h_turned", "h_high",
                                                                       "h_low"))
        y_taken, y_stored, y_all, y_over, x_go, w_over = (msem(n) for n in ("y_taken", "y_stored", "y_all", "y_over", "x_go", "w_over"))
        XB = G[:, 12:14, :].rearrange("p k s -> p (k s)")
        YB = G[:, 14:16, :]
        SG, HID = G[:, 16, 0:256], G[:, 16, 256:512]
        XH = AR[:, 0:2, :].rearrange("p k s -> p (k s)")
        XL = AR[:, 2:4, :].rearrange("p k s -> p (k s)")
        HH, HL = AR[:, 4, 0:256], AR[:, 5, 0:256]
        ps_gu, ps_y = ps_s[0], (ps_o, ps_s[1])
        whm = lambda p: WH[:, p % SPLIT, :]
        wlm = lambda p: WL[:, p % SPLIT, :]

        def n_blocks(eng):
            need(eng, "route_dve", "plan")
            return eng.value_load(N_BLK, min_val=2 * S // SLOTS, max_val=NB_MAX)

        def moe_sync(sp):
            cnt = n_blocks(sp)

            def load(b, e, p):
                sp.wait_ge(m_low, 6 * b + p + 1)
                sp.dma_start(WRAW[:, p, :], a["w_experts"][bass.ds(e, 1), p, :, :].rearrange("a p n -> (a p) n")
                             ).then_inc(m_load[p], 16)

            expert = lambda b: sp.value_load(BLK_E[:, bass.ds(b, 1)], min_val=0, max_val=N_EXPERTS - 1)
            e0 = sp.value_load(BLK_E[:, 0:1], min_val=0, max_val=N_EXPERTS - 1)
            sp.wait_ge(low_ready, MOE_AT)
            load(0, e0, 0)
            load(0, e0, 1)
            with sp.Fori(cnt, NB_MAX + 1) as b:
                sp.dma_start(rows_y[bass.ds(b * SLOTS, SLOTS), :],
                               G[:, 4:6, :].rearrange("p k s -> p (k s)")).then_inc(y_all, 16)
            with sp.Fori(0, cnt) as b:
                sp.sem_inc(y_all, 16)
                e = expert(b)
                for p in range(2, 6):
                    load(b, e, p)
                e = expert(b + 1)
                for p in range(2):
                    load(b + 1, e, p)
            sp.wait_ge(m_low, 6 * cnt + 8)

        def moe_high(act, b, p):
            act.wait_ge(m_load[p], 16 * b + 16)
            act.wait_ge(m_done, 6 * b + p + 1)
            act.activation(whm(p), WRAW[:, p, :], ACT.Copy).then_inc(m_high, 1)

        def moe_low(dve, b, p):
            dve.wait_ge(m_high, 6 * b + p + 1)
            dve.tensor_tensor(wlm(p), WRAW[:, p, :], whm(p).bitcast(F32), ALU.subtract).then_inc(m_low, 1)

        def x_split_high(act, b):
            for q in range(2):
                act.wait_ge(x_turned, 2 * b + q + 1)
                act.activation(XH[:, q * 512:(q + 1) * 512], ps_t[q][:, :], ACT.Copy).then_inc(x_high, 1)

        def x_split_low(dve, b):
            for q in range(2):
                dve.wait_ge(x_high, 2 * b + q + 1)
                dve.tensor_tensor(XL[:, q * 512:(q + 1) * 512], ps_t[q][:, :],
                                  XH[:, q * 512:(q + 1) * 512].bitcast(F32), ALU.subtract).then_inc(x_low, 1)

        def x_turn(pe, b):
            pe.wait_ge(x_rows, 16 * b + 16)
            for q in range(2):
                for c in range(4):
                    k = 4 * q + c
                    last = pe.transpose(ps_t[q][:, c * P:(c + 1) * P], XB[:, k * P:(k + 1) * P], ident)
                last.then_inc(x_turned, 1)

        def moe_tensor(pe):
            cnt = n_blocks(pe)
            pe.wait_ge(tile_done, MOE_AT)
            need(pe, "turn_act", rows_out.t0 + 2 * QT - 1)
            pe.sem_inc(m_done, SPLIT)
            x_turn(pe, 0)
            with pe.Fori(0, cnt) as b:
                pe.wait_ge(x_low, 2 * b + 2)
                for p in range(4):
                    pe.wait_ge(m_low, 6 * b + p + 7)
                    for kk in range(2):
                        k = 2 * p + kk
                        xs, w = slice(k * P, (k + 1) * P), slice(kk * 512, kk * 512 + 512)
                        pe.matmul(ps_gu[:, :], XH[:, xs], whm(p)[:, w], start=(k == 0), stop=False)
                        pe.matmul(ps_gu[:, :], XH[:, xs], wlm(p)[:, w], start=False, stop=False)
                        last = pe.matmul(ps_gu[:, :], XL[:, xs], whm(p)[:, w], start=False, stop=(k == 7))
                    last.then_inc(m_done, 1)
                x_turn(pe, b + 1)
                pe.wait_ge(m_hidden, b + 1)
                for q in range(2):
                    last = pe.transpose(ps_m[:, q * P:(q + 1) * P], HID[:, q * P:(q + 1) * P], ident)
                last.then_inc(h_turned, 1)
                pe.wait_ge(h_low, b + 1)
                for k in range(2):
                    pe.wait_ge(m_low, 6 * b + k + 11)
                    hs = slice(k * P, (k + 1) * P)
                    for n in range(2):
                        w = slice(n * 512, n * 512 + 512)
                        pe.matmul(ps_y[n][:, :], HH[:, hs], whm(4 + k)[:, w], start=(k == 0), stop=False)
                        pe.matmul(ps_y[n][:, :], HH[:, hs], wlm(4 + k)[:, w], start=False, stop=False)
                        last = pe.matmul(ps_y[n][:, :], HL[:, hs], whm(4 + k)[:, w], start=False, stop=(k == 1))
                    last.then_inc(m_done, 1)

        def moe_scalar(act):
            cnt = n_blocks(act)
            act.wait_ge(tile_done, MOE_AT)
            moe_high(act, 0, 0)
            moe_high(act, 0, 1)
            x_split_high(act, 0)
            with act.Fori(0, cnt) as b:
                for p in range(2, 6):
                    moe_high(act, b, p)
                act.wait_ge(m_done, 6 * b + 7)
                act.activation(SG, ps_gu[:, 0:256], ACT.Silu).then_inc(m_silu, 1)
                x_split_high(act, b + 1)
                act.wait_ge(h_turned, b + 1)
                act.activation(HH, ps_m[:, 0:256], ACT.Copy).then_inc(h_high, 1)
                moe_high(act, b + 1, 0)
                moe_high(act, b + 1, 1)
                act.wait_ge(m_done, 6 * b + 9)
                act.wait_ge(y_stored, 16 * b + 16)
                act.copy(YB[:, 0, :], ps_y[0][:, :]).then_inc(y_taken, 1)
            act.wait_ge(m_done, 6 * cnt + 3)
            act.wait_ge(m_low, 6 * cnt + 8)
            act.sem_inc(w_over, 1)

        def moe_vector(dve):
            cnt = n_blocks(dve)
            dve.sem_inc(m_low, 6)
            moe_low(dve, 0, 0)
            moe_low(dve, 0, 1)
            x_split_low(dve, 0)
            with dve.Fori(0, cnt) as b:
                for p in range(2, 6):
                    moe_low(dve, b, p)
                dve.wait_ge(m_silu, b + 1)
                dve.tensor_tensor(HID, SG, ps_gu[:, 256:512], ALU.mult).then_inc(m_hidden, 1)
                x_split_low(dve, b + 1)
                dve.wait_ge(h_high, b + 1)
                dve.tensor_tensor(HL, ps_m[:, 0:256], HH.bitcast(F32), ALU.subtract).then_inc(h_low, 1)
                moe_low(dve, b + 1, 0)
                moe_low(dve, b + 1, 1)
                dve.wait_ge(m_done, 6 * b + 9)
                dve.wait_ge(y_stored, 16 * b + 16)
                dve.tensor_copy(YB[:, 1, :], ps_y[1][:, :]).then_inc(y_taken, 1)

        def gather_rows(pool, ids):
            pool.indirect_dma_start(out=XB, out_offset=None, in_=rows_h,
                                    in_offset=bass.IndirectOffsetOnAxis(ap=ids, axis=0)).then_inc(x_rows, 16)

        def moe_gpsimd(pool):
            need(pool, "route_dve", "slots")
            step(pool, pool.memset(IDS, 0), "slots_pool")
            done(pool.dma_start(slot_tok.rearrange("(p b) a -> p (b a)", b=NBC), IDS), "st_zero", by=16)
            ev.wait(pool, "st_zero", 16)
            for c in range(2 * QT):
                done(pool.indirect_dma_start(out=slot_tok, out_offset=bass.IndirectOffsetOnAxis(
                    ap=IDX[:, c:c + 1], axis=0), in_=TOKI[:, c // 2:c // 2 + 1], in_offset=None,
                    bounds_check=P * NBC - 1), "st_slots", by=16)
            ev.wait(pool, "st_slots", 2 * QT * 16)
            done(pool.dma_start(IDS, slot_tok.rearrange("(p b) a -> p (b a)", b=NBC)), "ld_slots", by=16)
            ev.wait(pool, "ld_slots", 16)
            ev.wait(pool, "st_rows", 16 * QT)
            cnt = n_blocks(pool)
            pool.tensor_copy(ID_COL, IDS[:, 0:1]).then_inc(x_ids, 1)
            pool.wait_ge(x_ids, 1)
            gather_rows(pool, ID_COL)
            pool.dma_start(rows_y[(NB_MAX + 1) * SLOTS:(NB_MAX + 2) * SLOTS, :],
                           G[:, 4:6, :].rearrange("p k s -> p (k s)")).then_inc(y_stored, 16)
            with pool.Fori(0, cnt) as b:
                pool.wait_ge(x_rows, 16 * b + 16)
                pool.tensor_copy(ID_COL, IDS[:, bass.ds(b + 1, 1)]).then_inc(x_ids, 1)
                pool.wait_ge(x_ids, b + 2)
                pool.wait_ge(x_turned, 2 * b + 2)
                pool.sem_inc(x_go, 1)
                gather_rows(pool, ID_COL)
                pool.wait_ge(y_taken, 2 * b + 2)
                pool.dma_start(rows_y[bass.ds(b * SLOTS, SLOTS), :],
                               YB.rearrange("p k s -> p (k s)")).then_inc(y_stored, 16)
            pool.wait_ge(y_stored, 16 * cnt + 16)
            pool.sem_inc(y_over, 1)
            pool.wait_ge(y_all, 16 * (NB_MAX + 1))
            for i in range(QT):
                for q in range(2):
                    if i >= 2:
                        need(pool, "comb_dve", ("sum", i - 2))
                        need(pool, "comb_pe", (i - 2, 1))
                    done(pool.indirect_dma_start(
                        out=YG(i, q), out_offset=None, in_=rows_y[0:NB_MAX * SLOTS, :], in_offset=bass.IndirectOffsetOnAxis(
                            ap=YIDX[:, 2 * i + q:2 * i + q + 1], axis=0), bounds_check=NB_MAX * SLOTS - 1),
                        f"ld_y{i}", by=16)

        YG = lambda i, q: G[:, 4 * (i % 2) + 2 * q:4 * (i % 2) + 2 * q + 2, :].rearrange("p k s -> p (k s)")
        fl.append(On(tensor=moe_tensor, scalar=moe_scalar, vector=moe_vector, gpsimd=moe_gpsimd))

        def combine_vector(dve):
            for i in range(QT):
                ev.wait(dve, f"ld_y{i}", 32)
                step(dve, dve.tensor_scalar(YG(i, 0), YG(i, 0), WTS[:, i, 0:1], None, ALU.mult), "comb_dve")
                step(dve, dve.scalar_tensor_tensor(out=YG(i, 0), in0=YG(i, 1), scalar=WTS[:, i, 1:2],
                                                   in1=YG(i, 0), op0=ALU.mult, op1=ALU.add),
                     "comb_dve", ("sum", i))
                for q in range(2):
                    need(dve, "comb_pe", (i, q))
                    xs = X[:, 4 * q:4 * q + 4, i * P:(i + 1) * P]
                    done(dve.tensor_tensor(xs, xs, ps_s[q][:, :].rearrange("p (c t) -> p c t", t=P), ALU.add),
                         "comb_dve", ("x", i, q))

        def combine_tensor(pe):
            for i in range(QT):
                need(pe, "comb_dve", ("sum", i))
                for q in range(2):
                    if i:
                        need(pe, "comb_dve", ("x", i - 1, q))
                    for c in range(4):
                        k = 4 * q + c
                        last = pe.transpose(ps_s[q][:, c * P:(c + 1) * P], YG(i, 0)[:, k * P:(k + 1) * P], ident)
                    done(last, "comb_pe", (i, q))

        fl.append(On(tensor=combine_tensor, vector=combine_vector))
        moe_through = lambda e: need(e, "comb_dve", ("x", QT - 1, 1))
        cuts["moe"] = (len(fl), moe_through, MOE_AT)
        n_final1 = Norm("final1", KT, S, x_tile, lambda k: vec("norm_final", k), x_tile, None, None, moe_through)
        fl.append(n_final1)
        cuts["first"] = (len(fl), lambda e: need(e, "norm_dve", ("final1", "h", KT - 1)), MOE_AT)

        x_final1 = lambda e: need(e, "norm_dve", ("final1", "h", KT - 1))
        fl.append(Prime(MOE_AT))
        mh2 = AR[:, 24:28, :].rearrange("p k (a s) -> p (k a) s", a=2)
        ml2 = AR[:, 28:32, :].rearrange("p k (a s) -> p (k a) s", a=2)
        n_mem2 = Norm("mem2", KT, NMEM, lambda k: raw1[:, k, :], lambda k: vec("ln_mem", k),
                      lambda k: raw1[:, k, :], lambda k: mh2[:, k, :], lambda k: ml2[:, k, :],
                      lambda e: (load_waits(e, "mem2"), moe_through(e)), wait_dst=x_final1)
        n_mem2.sq = H[:, 0:4, :].rearrange("p k s -> p (k s)")
        k2 = lambda l: G[:, 20 + l, :].rearrange("p (c m) -> p c m", c=2)
        v2f = lambda l: G[:, l, :].rearrange("p (c m) -> p c m", c=2)
        v2 = lambda l: G[:, 22 + l, :].rearrange("p (t f) -> p t f", t=2)
        fl += [n_mem2, Linear("mem2", lambda k: mh2[:, k, :], lambda k: ml2[:, k, :], n_mem2.ready,
                              taker(lambda j: (k2 if j % 4 < 2 else v2f)(j // 4)[:, j % 2, :]))]
        fl.append(Transposes("mem2_v", [
            ([(v2f(l)[:, c, t * P:(t + 1) * P], (2 * t + c) * P) for t in range(2) for c in range(2)],
             (G[:, 22 + l, :], lambda b: b[:, :]), None) for l in range(2)],
            wait_first=lambda e: wait_stage_evac(e, "mem2")))
        mem2_turned = fl[-1]

        n_mix0 = Norm("mix0", KT, S, x_tile, lambda k: vec("ln_mix0", k), h_tile, hi, lo, x_final1,
                      wait_dst=lambda e: (wait_products(e, "mem2"), need(e, *n_mem2.ready(KT - 1))))
        fl.append(n_mix0)
        cbuf = lambda j: AF[:, 24:27, :].rearrange("p k s -> p (k s)")[:, 516 * (j % 2):516 * (j % 2) + 515]
        PAD = CONV_K - 1
        N_CONV = 3 * GDN_HEADS

        def gdn_act(act, j, t, out):
            act.wait_ge(tile_done, t + 1)
            if j < N_CONV:
                if j == 0:
                    need(act, "conv_dve", "pad")
                elif j >= 2:
                    need(act, "conv_dve", j - 2)
                act.copy(cbuf(j)[:, PAD:PAD + S], out).then_inc(evacuated[t % BANKS], 1)
            elif j < N_CONV + GDN_HEADS:
                act.activation(AF[:, 16 + j - N_CONV, :], out, ACT.Silu).then_inc(evacuated[t % BANKS], 1)
            else:
                act.copy(AF[:, 22 + j - N_CONV - GDN_HEADS, :], out).then_inc(evacuated[t % BANKS], 1)
            if 1 <= j <= N_CONV:
                need(act, "conv_dve", j - 1)
                if j == 1:
                    need(act, "turn_act", mem2_turned.t0 + 1)
                done(act.activation(g(j - 1), SC[:, (j - 1) % 2, :], ACT.Silu), "conv_act", j - 1)

        def gdn_dve(dve, j, t, out):
            if j == 0:
                need(dve, "norm_dve", ("mix0", "low", KT - 1))
                for q in range(2):
                    step(dve, dve.memset(cbuf(q)[:, 0:PAD], 0.0), "conv_dve", "pad")
            if j < N_CONV:
                wait_evac(dve, t)
                if j >= 2:
                    need(dve, "conv_act", j - 2)
                acc = SC[:, j % 2, :]
                step(dve, dve.tensor_scalar(acc, cbuf(j)[:, 0:S], vec("conv", 4 * j), None, ALU.mult), "conv_dve")
                for q in range(1, CONV_K):
                    step(dve, dve.scalar_tensor_tensor(out=acc, in0=cbuf(j)[:, q:q + S],
                                                       scalar=vec("conv", 4 * j + q), in1=acc,
                                                       op0=ALU.mult, op1=ALU.add), "conv_dve", j)

        fl.append(Linear("gdnin", hi, lo, n_mix0.ready, gdn_act, gdn_dve))
        BETA, GC = G[0:GDN_HEADS, 18, :], G[0:GDN_HEADS, 19, :]
        fl.append(Linear("ba", hi, lo, None, taker(lambda j: G[0:GDN_HEADS, 18 + j, :])))

        def l2_scale(dve, k, s, label):
            if k < GDN_HEADS:
                done(dve.scalar_tensor_tensor(out=g(k), in0=g(k), scalar=GDN_D ** -0.5, in1=s, op0=ALU.mult,
                                              op1=ALU.mult), "hn_dve", label)
            else:
                done(dve.tensor_tensor(g(k), g(k), s, ALU.mult), "hn_dve", label)

        fl.append(HeadNorm("qk", 2 * GDN_HEADS, g, const("ones"), 1.0, l2_scale,
                           lambda e: need(e, "conv_act", 2 * GDN_HEADS - 1)))

        def gates_vector(dve):
            st = lambda ins, label=None: step(dve, ins, "gate_dve", label)
            r = slice(0, GDN_HEADS)
            ts = dve.tensor_scalar
            wait_stage_evac(dve, "ba")
            need(dve, "gate_act", "beta")
            st(ts(BETA, BETA, 1.0, None, ALU.add))
            st(dve.reciprocal(BETA, BETA), "beta")
            sp_, ab = SC[r, 0, :], SC[r, 1, :]
            st(ts(GC, GC, vec("dt", rows=r), None, ALU.add))
            st(dve.scalar_tensor_tensor(out=ab, in0=GC, scalar=-1.0, in1=GC, op0=ALU.mult, op1=ALU.min), "ab")
            need(dve, "gate_act", "exp")
            st(ts(ab, ab, 1.0, None, ALU.add), "ab1")
            st(ts(GC, GC, 0.0, None, ALU.max))
            need(dve, "gate_act", "ln")
            st(dve.tensor_tensor(GC, GC, ab, ALU.add))
            st(ts(GC, GC, COL[r, 46:47], -1.0, ALU.mult, ALU.mult))
            for c in range(QT):
                cs = slice(c * P, (c + 1) * P)
                st(dve.tensor_tensor_scan(sp_[:, cs], const("ones", GDN_HEADS), GC[:, cs], 0.0, ALU.mult, ALU.add))
            st(dve.tensor_copy(GC, sp_), "gc")

        def gates_scalar(act):
            r = slice(0, GDN_HEADS)
            ab = SC[r, 1, :]
            need(act, "hn_dve", ("qk", 2 * GDN_HEADS - 1))
            done(act.activation(COL[r, 46:47], vec("a_log", rows=r), ACT.Exp), "gate_act")
            done(act.activation(BETA, BETA, ACT.Exp, scale=-1.0), "gate_act", "beta")
            need(act, "gate_dve", "ab")
            done(act.activation(ab, ab, ACT.Exp), "gate_act", "exp")
            need(act, "gate_dve", "ab1")
            done(act.activation(ab, ab, ACT.Ln), "gate_act", "ln")

        fl.append(On(scalar=gates_scalar, vector=gates_vector))
        gate_cols = Transposes("gate_cols", [
            ([(G[0:GDN_HEADS, 18 + q, c * P:(c + 1) * P], 24 * q + GDN_HEADS * c) for q in range(2)
              for c in range(QT)], (COL[:, 48:96], lambda b: b[:, 0:48]), None)],
            wait_first=lambda e: need(e, "gate_dve", "gc"))
        fl.append(gate_cols)
        flat = lambda a, k, n: a[:, k:k + n, :].rearrange("p k s -> p (k s)")
        heads_of = lambda f, at_=0: f[:, at_:at_ + GDN_W].rearrange("p (h c) -> p h c", c=P)
        VROW, KROW = flat(AF, 0, 6), flat(AF, 6, 6)

        def row_groups(first, dest):
            out = []
            for c in range(QT):
                for h0, n in ((0, 4), (4, 2)):
                    at_ = c * GDN_W + h0 * P
                    out.append(([(G[:, first + h0 + h, c * P:(c + 1) * P], h * P) for h in range(n)],
                                (dest[:, at_:at_ + n * P], (lambda n: lambda b: b[:, 0:n * P])(n)), None))
            return out

        v_rows = Transposes("v_rows", row_groups(12, VROW), wait_first=lambda e: (
            need(e, "conv_act", N_CONV - 1), wait_products(e, "ba")))
        k_rows = Transposes("k_rows", row_groups(6, KROW),
                            wait_first=lambda e: need(e, "hn_dve", ("qk", 2 * GDN_HEADS - 1)))
        fl += [v_rows, k_rows]

        def gcb_tensor(pe):
            for h in range(GDN_HEADS):
                if h:
                    need(pe, "gcb_act", h - 1)
                else:
                    need(pe, "hn_act", ("qk", "root", 2 * GDN_HEADS - 1))
                done(pe.matmul(ps_m[:, :], ident[0:GDN_HEADS, h:h + 1].to_broadcast([GDN_HEADS, P]), GC,
                               start=True, stop=True), "gcb_pe", h)

        def gcb_scalar(act):
            need(act, "turn_pe", k_rows.t0 - 1)
            for h in range(GDN_HEADS):
                need(act, "gcb_pe", h)
                done(act.copy(g(12 + h), ps_m[:, :]), "gcb_act", h)
            need(act, "cc_dve", "args")
            done(act.activation(CC[:, 0:24], COL[:, 72:96], ACT.Exp), "cc_act")
            done(act.activation(CC[:, 24:72], CC[:, 24:72], ACT.Exp), "cc_act", "exp")

        CC = SC[:, 1, :]
        BG, KGC, GLAST = CC[:, 0:24], CC[:, 24:48], CC[:, 48:72]
        gc_last = G[:, 12:18, :].rearrange("p h (c j) -> p c h j", j=P)[:, :, :, P - 1]

        def cols_vector(dve):
            st = lambda ins, label=None: step(dve, ins, "cc_dve", label)
            need(dve, "gcb_act", GDN_HEADS - 1)
            need(dve, "turn_act", gate_cols.t0)
            need(dve, "gate_act", "ln")
            as_ch = lambda f: f.rearrange("p (c h) -> p c h", h=GDN_HEADS)
            st(dve.tensor_copy(as_ch(GLAST), gc_last))
            st(dve.tensor_tensor(KGC, GLAST, COL[:, 72:96], ALU.subtract), "args")
            need(dve, "cc_act", "exp")
            st(dve.tensor_tensor(BG, BG, COL[:, 48:72], ALU.mult), "cols")
            st(dve.memset(flat(AF, 12, 2)[:, 0:GDN_W], 0.0), "state0")

        fl.append(On(tensor=gcb_tensor, scalar=gcb_scalar, vector=cols_vector))
        k0_of = lambda l, h: k2(l)[64 * (h % 2):64 * (h % 2) + 64, h // 2, :]

        def mem2_attention(name, l, q, out, probs, turned, wait_scores, wait_out):
            return Attention(
                name, MEM_HEADS, "full", MEM_DH2 ** -0.5,
                lambda h, i, r: (q(h)[:, i * P:(i + 1) * P], k0_of(l, h)), lambda i: NMEM, probs, turned,
                lambda h: (out_rows(h), [(v2(l)[:, j, h * 64:(h + 1) * 64], (j, 0, 0, S), j == 0, j == 1)
                                         for j in range(2)]), out, wait_scores, lambda e: None,
                wait_out=wait_out)

        att_mem0 = mem2_attention("mem0", 0, lambda h: AF[out_rows(h), 22 + h // 2, :],
                                  lambda h: AF[out_rows(h), 22 + h // 2, :], [AF[:, 24 + k, :] for k in range(4)],
                                  (AF[:, 28:30, :], AF[:, 30:32, :]),
                                  lambda e: (wait_stage_evac(e, "gdnin"), need(e, "conv_dve", N_CONV - 1)), None)
        fl.append(att_mem0)

        W4 = flat(AF, 24, 8)
        LT, TT, RR, UU, INT = (heads_of(W4, q * GDN_W) for q in range(5))
        DEC, CM, WT = heads_of(flat(G, 18, 2)), heads_of(flat(H, 6, 2)), heads_of(flat(AF, 14, 2))
        ST = heads_of(flat(AF, 12, 2))
        KBG = DEC
        halves = ((0, 3), (3, 6))
        wide = lambda c_: c_.unsqueeze(1).to_broadcast([P, GDN_HEADS, P])
        pair = lambda banks, q: banks[q][:, 0:3 * P].rearrange("p (h c) -> p h c", c=P)
        bank_a, bank_b, bank_c = ps_s, ps_t, (ps_o, ps_m)
        level = lambda l: CB[:, CONST["levels"][0] + l * P:CONST["levels"][0] + (l + 1) * P]
        LEVELS = 7
        by_col = lambda cols, c: cols[:, 6 * c:6 * c + 6].unsqueeze(2).to_broadcast([P, GDN_HEADS, P])
        rows_of = lambda f, c: heads_of(f, c * GDN_W)
        BETA_C, GC_C = COL[:, 48:72], COL[:, 72:96]

        def six(pe, banks, lhs, rhs, name, label, waits=lambda q: None, more=None):
            for q, (h0, h1) in enumerate(halves):
                waits(q)
                for h in range(h0, h1):
                    out = pair(banks, q)[:, h - h0, :]
                    last = pe.matmul(out, lhs(h), rhs(h), start=True, stop=more is None)
                    if more:
                        last = pe.matmul(out, more[0](h), more[1](h), start=False, stop=True)
                done(last, name, (label, q))

        def gdn_tensor(pe):
            N = "gdn_pe"
            for c in range(QT):
                cs = slice(c * P, (c + 1) * P)
                kT, qT = (lambda h: G[:, 6 + h, cs]), (lambda h: G[:, h, cs])
                if c == 0:
                    need(pe, "att_act", ("out", att_mem0.h0 + MEM_HEADS - 1))
                else:
                    need(pe, "gdn_act", (c - 1, "o", 1))
                    need(pe, "gdn_dve", (c - 1, "v", 1))
                six(pe, bank_a, kT, kT, N, (c, "kk"))
                six(pe, bank_c, qT, kT, N, (c, "qk"))
                need(pe, "gdn_dve", (c, "L"))
                if c:
                    need(pe, "gdn_dve", (c - 1, "S"))
                for q, (h0, h1) in enumerate(halves):
                    for h in range(h0, h1):
                        last = pe.transpose(pair(bank_b, q)[:, h - h0, :], TT[:, h, :], ident)
                    done(last, N, ((c, "Lt"), q))
                need(pe, "gdn_dve", (c, "intra", 1))
                for q, (h0, h1) in enumerate(halves):
                    need(pe, "gdn_act", (c, "Lt", q))
                    for h in range(h0, h1):
                        last = pe.transpose(pair(bank_b, q)[:, h - h0, :], UU[:, h, :], ident)
                    done(last, N, ((c, "It"), q))
                for l in range(1, LEVELS):
                    need(pe, "gdn_pool", (c, "C", l))
                    six(pe, bank_a, lambda h: CM[:, h, :], lambda h: TT[:, h, :], N, (c, "U", l),
                        waits=lambda q: need(pe, "gdn_dve", (c, "T", l - 1, q)))
                    if l < LEVELS - 1:
                        six(pe, bank_b, lambda h: RR[:, h, :], lambda h: UU[:, h, :], N, (c, "TU", l),
                            waits=lambda q: (need(pe, "gdn_act", (c, "U", l, q)),
                                             need(pe, "gdn_dve", (c, "R", l - 1, q)),
                                             need(pe, "gdn_act", (c, "It", q))))
                    six(pe, bank_c, lambda h: UU[:, h, :], lambda h: RR[:, h, :], N, (c, "UR", l),
                        waits=lambda q: (need(pe, "gdn_act", (c, "U", l, q)),
                                         need(pe, "gdn_dve", (c, "R", l - 1, q))))
                last_r = lambda q: need(pe, "gdn_dve", (c, "R", LEVELS - 1, q))
                need(pe, "gdn_dve", (c, "kbg"))
                six(pe, bank_a, lambda h: KBG[:, h, :], lambda h: RR[:, h, :], N, (c, "w"), waits=last_r)
                six(pe, bank_b, lambda h: RR[:, h, :], lambda h: rows_of(VROW, c)[:, h, :], N, (c, "u"),
                    waits=lambda q: need(pe, "gdn_dve", (c, "T", LEVELS - 2, q)))
                six(pe, bank_c, lambda h: WT[:, h, :], lambda h: ST[:, h, :], N, (c, "wS"),
                    waits=lambda q: (need(pe, "gdn_act", (c, "w", q)),
                                     need(pe, "gdn_dve", (c - 1, "S") if c else (0, "kbg"))))
                six(pe, bank_a, lambda h: ST[:, h, :], qT, N, (c, "o"),
                    waits=lambda q: need(pe, "gdn_dve", (c, "v", q)),
                    more=(lambda h: TT[:, h, :], lambda h: INT[:, h, :]))
                need(pe, "gdn_dve", (c, "kg"))
                six(pe, bank_b, lambda h: LT[:, h, :], lambda h: TT[:, h, :], N, (c, "kv"),
                    waits=lambda q: need(pe, "gdn_act", (c, "u", q)))

        def gdn_scalar(act):
            A = "gdn_act"

            def take(dest, banks, c, label, as_=None):
                for q, (h0, h1) in enumerate(halves):
                    need(act, "gdn_pe", (label, q))
                    done(act.copy(dest(h0, h1), pair(banks, q)), A, label + (q,))

            for c in range(QT):
                cs = slice(c * P, (c + 1) * P)
                need(act, "gdn_dve", (c, "dec"))
                done(act.activation(DEC, DEC, ACT.Exp, scale=-1.0), A, (c, "dec"))
                take(lambda a_, b_: LT[:, a_:b_, :], bank_b, c, (c, "Lt"))
                take(lambda a_, b_: INT[:, a_:b_, :], bank_b, c, (c, "It"))
                need(act, "gdn_dve", (c, "intra", 1))
                done(act.activation(DEC, G[:, 12:18, cs], ACT.Exp), A, (c, "eg"))
                for l in range(1, LEVELS):
                    for q, (h0, h1) in enumerate(halves):
                        need(act, "gdn_pe", ((c, "U", l), q))
                        done(act.copy(UU[:, h0:h1, :], pair(bank_a, q)), A, (c, "U", l, q))
                take(lambda a_, b_: WT[:, a_:b_, :], bank_a, c, (c, "w"))
                take(lambda a_, b_: UU[:, a_:b_, :], bank_b, c, (c, "u"))
                take(lambda a_, b_: H[:, a_:b_, cs], bank_a, c, (c, "o"))

        def gdn_vector(dve):
            N = "gdn_dve"
            st = lambda ins, label=None: step(dve, ins, N, label)
            tt = dve.tensor_tensor
            for c in range(QT):
                cs = slice(c * P, (c + 1) * P)
                if c == 0:
                    need(dve, "turn_act", k_rows.t0 + 7)
                    need(dve, "att_act", ("out", att_mem0.h0 + MEM_HEADS - 1))
                    need(dve, "norm_dve", ("mix0", "low", KT - 1))
                else:
                    need(dve, "gdn_pe", ((c - 1, "kv"), 1))
                st(tt(DEC, G[:, 12:18, cs], by_col(GC_C, c), ALU.subtract))
                st(dve.tensor_scalar(DEC, DEC, 0.0, None, ALU.max), (c, "dec"))
                need(dve, "gdn_act", (c, "dec"))
                st(tt(CM, DEC, wide(const("lower")), ALU.mult))
                for q, (h0, h1) in enumerate(halves):
                    need(dve, "gdn_pe", ((c, "kk"), q))
                    for h in range(h0, h1):
                        done(dve.scalar_tensor_tensor(out=TT[:, h, :], in0=pair(bank_a, q)[:, h - h0, :],
                                                      scalar=BETA_C[:, 6 * c + h:6 * c + h + 1], in1=CM[:, h, :],
                                                      op0=ALU.mult, op1=ALU.mult), N, (c, "L"))
                st(tt(DEC, DEC, wide(const("incl")), ALU.mult))
                for q, (h0, h1) in enumerate(halves):
                    need(dve, "gdn_pe", ((c, "qk"), q))
                    st(tt(UU[:, h0:h1, :], pair(bank_c, q), DEC[:, h0:h1, :], ALU.mult), (c, "intra", q))
                need(dve, "gdn_pe", ((c, "Lt"), 1))
                st(tt(TT, TT, wide(const("first_level")), ALU.mult))
                st(tt(TT, wide(ident), TT, ALU.subtract), (c, "T", 0, 0))
                ev.seen[N, (c, "T", 0, 1)] = ev.seen[N, (c, "T", 0, 0)]
                need(dve, "gdn_act", (c, "Lt", 1))
                st(tt(RR, LT, wide(level(0)), ALU.mult))
                st(tt(RR, wide(ident), RR, ALU.subtract), (c, "R", 0, 0))
                ev.seen[N, (c, "R", 0, 1)] = ev.seen[N, (c, "R", 0, 0)]
                need(dve, "gdn_act", (c, "eg"))
                st(tt(G[:, 0:6, cs], G[:, 0:6, cs], DEC, ALU.mult), (c, "qg"))
                st(tt(KBG, rows_of(KROW, c), by_col(BG, c), ALU.mult))
                st(tt(rows_of(VROW, c), rows_of(VROW, c), by_col(BETA_C, c), ALU.mult), (c, "kbg"))
                for l in range(1, LEVELS):
                    for q, (h0, h1) in enumerate(halves):
                        if l < LEVELS - 1:
                            need(dve, "gdn_pe", ((c, "TU", l), q))
                            done(tt(TT[:, h0:h1, :], TT[:, h0:h1, :], pair(bank_b, q), ALU.subtract), N,
                                 (c, "T", l, q))
                    for q, (h0, h1) in enumerate(halves):
                        need(dve, "gdn_pe", ((c, "UR", l), q))
                        done(tt(RR[:, h0:h1, :], RR[:, h0:h1, :], pair(bank_c, q), ALU.subtract), N,
                             (c, "R", l, q))
                need(dve, "gdn_pool", (c, "C", LEVELS - 1))
                done(tt(LT, rows_of(KROW, c), by_col(KGC, c), ALU.mult), N, (c, "kg"))
                for q, (h0, h1) in enumerate(halves):
                    need(dve, "gdn_act", (c, "u", q))
                    need(dve, "gdn_pe", ((c, "wS"), q))
                    st(tt(TT[:, h0:h1, :], UU[:, h0:h1, :], pair(bank_c, q), ALU.subtract), (c, "v", q))
                for q, (h0, h1) in enumerate(halves):
                    need(dve, "gdn_pe", ((c, "kv"), q))
                    for h in range(h0, h1):
                        done(dve.scalar_tensor_tensor(out=ST[:, h, :], in0=ST[:, h, :],
                                                      scalar=GLAST[:, 6 * c + h:6 * c + h + 1],
                                                      in1=pair(bank_b, q)[:, h - h0, :], op0=ALU.mult,
                                                      op1=ALU.add), N, (c, "S"))

        def gdn_gpsimd(pool):
            for c in range(QT):
                for l in range(1, LEVELS):
                    if l == 1:
                        need(pool, "gdn_act", (c, "Lt", 1))
                        need(pool, "gdn_dve", (c, "intra", 1))
                    else:
                        need(pool, "gdn_pe", ((c, "U", l - 1), 1))
                    done(pool.tensor_tensor(CM, LT, wide(level(l)), ALU.mult), "gdn_pool", (c, "C", l))

        fl.append(On(tensor=gdn_tensor, scalar=gdn_scalar, vector=gdn_vector, gpsimd=gdn_gpsimd))

        def gdn_gain(dve, k, s, label):
            step(dve, dve.scalar_tensor_tensor(out=h_tile(k), in0=h_tile(k), scalar=vec("gdn_norm"), in1=s,
                                               op0=ALU.mult, op1=ALU.mult), "hn_dve")
            done(dve.tensor_tensor(h_tile(k), h_tile(k), AF[:, 16 + k, :], ALU.mult), "hn_dve", label)

        gdn_out = lambda e: (need(e, "gdn_act", (QT - 1, "o", 1)), need(e, "gdn_dve", (QT - 1, "S")))
        fl.append(HeadNorm("gdn", GDN_HEADS, h_tile, const("ones"), 1.0 / GDN_D, gdn_gain, gdn_out))
        s_gdn = Split("gdn", 8, lambda k: h_tile(k) if k < 6 else AF[:, 16 + k, :], hi, lo,
                      lambda e: need(e, "hn_dve", ("gdn", GDN_HEADS - 1)))
        fl += [s_gdn, Linear("out0", hi, lo, s_gdn.ready, None, add_to_x)]
        cuts["s1"] = (len(fl), lambda e: wait_stage_evac(e, "out0"), BASE["gu00"])

        def swiglu(l, x_done):
            n = Norm(f"ffn{l}", KT, S, x_tile, lambda k: vec(f"ln_ffn{l}", k), h_tile, hi, lo, x_done,
                     wait_dst=x_done)
            fl.append(n)
            for p, width in enumerate(FF_PARTS):
                name = f"gu{l}{p}"
                ready = {}

                def take_act(act, j, t, out, name=name, width=width, p=p):
                    i, up = j // 2, j % 2
                    if not up:
                        act.wait_ge(tile_done, t + 1)
                        if i >= 2:
                            wait_evac(act, t - 3)
                        act.activation(H[:, i % 2, :], out, ACT.Silu).then_inc(evacuated[t % BANKS], 1)
                    else:
                        wait_evac(act, t)
                        if i == 0 and p:
                            wait_products(act, f"down{l}{p - 1}")
                        done(act.activation(AR[:, 16 + i, :], H[:, 2 + i % 2, :], ACT.Copy), "ff_act", (name, i))

                def take_dve(dve, j, t, out, name=name, width=width, p=p):
                    i, up = j // 2, j % 2
                    if up:
                        wait_evac(dve, t - 1)
                        dve.wait_ge(tile_done, t + 1)
                        dve.tensor_tensor(H[:, 2 + i % 2, :], H[:, i % 2, :], out,
                                          ALU.mult).then_inc(evacuated[t % BANKS], 1)
                        need(dve, "ff_act", (name, i))
                        done(dve.tensor_tensor(AR[:, 24 + i, :], H[:, 2 + i % 2, :],
                                               AR[:, 16 + i, :].bitcast(F32), ALU.subtract), "ff_dve", (name, i))

                fl.append(Linear(name, hi, lo, n.ready if p == 0 else None, take_act, take_dve))
                fl.append(Linear(f"down{l}{p}", lambda k: AR[:, 16 + k, :], lambda k: AR[:, 24 + k, :],
                                 (lambda name: lambda k: ("ff_dve", (name, k)))(name), None, add_to_x))
            return lambda e: wait_stage_evac(e, f"down{l}{len(FF_PARTS) - 1}")

        x_ff0 = swiglu(0, lambda e: wait_stage_evac(e, "out0"))
        cuts["s2"] = (len(fl), x_ff0, BASE["kv"])

        n_kv = Norm("kv", KT, S, x_tile, lambda k: vec("ln_kv", k), h_tile, hi, lo, x_ff0, wait_dst=x_ff0)
        cos_s, sin_s = g(3), g(4)
        fl.append(Angles("swa", GI[:, 16, :], col(C_INV_SWA), col(C_SIGN_SWA), cos_s, sin_s,
                         lambda e: load_waits(e, "pos2")))
        fl += [n_kv, Linear("kv", hi, lo, n_kv.ready, taker(lambda j: g(j) if j < 2 else g(5)))]
        swa_v = Transposes("swa_v", [([(G[:, 5, i * P:(i + 1) * P], i * P) for i in range(QT)],
                                      (g(2), lambda b: b[:, :]), None)],
                           wait_first=lambda e: wait_stage_evac(e, "kv"))
        fl.append(swa_v)
        fl.append(Rope("swa_k", [g(0), g(1)], P, const("perm_swa"), cos_s, sin_s,
                       lambda e: wait_stage_evac(e, "kv")))

        n_mix1 = Norm("mix1", KT, S, x_tile, lambda k: vec("ln_mix1", k), h_tile, hi, lo, x_ff0,
                      wait_dst=lambda e: (wait_products(e, "kv"), need(e, "rope_dve", ("swa_k", 1)),
                                          need(e, *n_kv.ready(KT - 1))))
        fl += [n_mix1, Linear("swaq", hi, lo, n_mix1.ready, taker(lambda j: g(5 + j), lambda e: need(
            e, "turn_pe", swa_v.t0)))]
        fl.append(Rope("swa_q", [g(5 + k) for k in range(6)], P, const("perm_swa"), cos_s, sin_s,
                       lambda e: wait_stage_evac(e, "swaq")))
        per_kv = SWA_HEADS // SWA_KV

        def swa_scores(h, i, r):
            rows = out_rows(h)
            return G[rows, 5 + h // 2, i * P:(i + 1) * P], G[rows, h // per_kv, max(i - 1, 0) * P:(i + 1) * P]

        def swa_pv(h):
            plan_ = []
            for i in range(QT):
                tiles = [i] if i == 0 else [i - 1, i]
                for b, j in enumerate(tiles):
                    v = G[:, 2, j * P + 64 * (h // per_kv):j * P + 64 * (h // per_kv) + 64]
                    plan_.append((v, (b, i * P, i * P, (i + 1) * P), b == 0, b == len(tiles) - 1))
            return out_rows(h), plan_

        probs_s = [g(14 + k) for k in range(4)]
        turned_s = (AF[:, 16:18, :], AF[:, 18:20, :])
        swa = Attention("swa", SWA_HEADS, "window", SWA_DH ** -0.5, swa_scores, lambda i: P if i == 0 else 2 * P,
                        probs_s, turned_s, swa_pv, lambda h: H[out_rows(h), h // 2, :],
                        lambda e: need(e, "rope_dve", ("swa_q", 5)), lambda e: need(e, "turn_act", swa_v.t0),
                        wait_out=lambda e: (wait_products(e, "swaq"), need(e, *n_mix1.ready(KT - 1))))
        att_mem1 = mem2_attention("mem1", 1, lambda h: G[out_rows(h), 11 + h // 2, :],
                                  lambda h: H[out_rows(h), 6 + h // 2, :], probs_s, turned_s,
                                  lambda e: wait_stage_evac(e, "swaq"), None)
        s_swa = Split("swa", 8, h_tile, hi, lo, last_head(att_mem1))
        fl += [swa, att_mem1, s_swa, Linear("out1", hi, lo, s_swa.ready, None, add_to_x)]
        cuts["s4"] = (len(fl), lambda e: wait_stage_evac(e, "out1"), BASE["gu10"])
        x_ff1 = swiglu(1, lambda e: wait_stage_evac(e, "out1"))
        n_final = Norm("final", KT, S, x_tile, lambda k: vec("ln_final", k), x_tile, None, None, x_ff1)
        fl.append(n_final)
        cuts["final"] = (len(fl), lambda e: need(e, "norm_dve", ("final", "h", KT - 1)), N_TILES)

        def load_tile(sp, t):
            name, _, kt, m, _ = TILE[t]
            if t >= RING:
                sp.wait_ge(low_ready, t - RING + 1)
            sp.dma_start(WRAW[:, t % RING, 0:kt * m], a["w_" + name][t - BASE[name]]).then_inc(w_loaded[t % RING], 16)

        if stop:
            fl = fl[:cuts[stop][0]]
        last_tile = cuts[stop or "final"][2]
        block = ctx.enter_context(nc.Block())

        @block.sync
        def _(sp):
            done(sp.dma_start(CB[:, :], a["consts"]), "ld_const", by=16)
            done(sp.dma_start(VB[:, :], a["vectors"]), "ld_vec", by=16)
            done(sp.dma_start(X[:, :, :], a["x_t"]), "ld_x", by=16)
            for t in range(MOE_AT):
                load_tile(sp, t)
            for i in range(QT):
                need(sp, "turn_act", rows_out.t0 + 2 * i + 1)
                done(sp.dma_start(rows_h[i * P:(i + 1) * P, :],
                                  G[:, 4 + 2 * i:6 + 2 * i, :].rearrange("p k s -> p (k s)")), "st_rows", by=16)
            moe_sync(sp)
            for t in range(MOE_AT, min(last_tile + 2, N_TILES)):
                load_tile(sp, t)
            cuts[stop or "final"][1](sp)
            done(sp.dma_start(a["out"], X[:, :, :]), "st_out", by=16)
            ev.wait(sp, "st_out", 16)

        @block.gpsimd
        def _(pool):
            done(pool.dma_start(GI[:, 16, :], a["pos"].partition_broadcast(P)), "ld_pos", by=16)
            done(pool.dma_start(COLI[:, 40:44], a["pos_col"]), "ld_posc", by=16)
            need(pool, "rope_dve", ("mla_q", MLA_HEADS))
            done(pool.dma_start(raw1, a["mem_t"]), "ld_mem", by=16)
            done(pool.dma_start(RW, a["router_w"]), "ld_router", by=16)
            need(pool, *n_mem.ready(KT - 1))
            done(pool.dma_start(raw1, a["mem2_t"]), "ld_mem2", by=16)
            moe_gpsimd(pool)
            if not stop or stop not in ("moe", "first"):
                gdn_gpsimd(pool)
                need(pool, "gdn_dve", (QT - 1, "S"))
                done(pool.dma_start(GI[:, 16, :], a["pos2"].partition_broadcast(P)), "ld_pos2", by=16)

        @block.tensor
        def _(pe):
            load_waits(pe, "const")
            for stage in fl:
                stage.tensor(pe)

        @block.scalar
        def _(act):
            for stage in fl:
                stage.scalar(act)

        @block.vector
        def _(dve):
            for stage in fl:
                stage.vector(dve)
    return ev.seen


def _feature_major(x):
    return np.ascontiguousarray(x.T.reshape(-1, P, x.shape[0]).transpose(1, 0, 2))


def _tiles(w, cols):
    k = w.shape[0] // P
    return np.ascontiguousarray(
        np.stack([w[:, c].reshape(k, P, len(c)).transpose(1, 0, 2).reshape(P, k * len(c)) for c in cols]))


def _blocks(n, width=P, at=0):
    return [np.arange(at + i * width, at + (i + 1) * width) for i in range(n)]


def _constants():
    p, f = np.arange(P)[:, None], np.arange(P)[None, :]
    c = {"ident": p == f, "upper": p < f, "lower": p > f, "incl": p >= f, "ones": p + f >= 0,
         "causal": np.where(f <= p, 0.0, NEG), "prev": np.where(f > p, 0.0, NEG),
         "blk64": p // 64 == f // 64}
    rope = np.where(f >= 64, 64 + (f - 64 + 16) % 32, -1)
    c["perm_mla"] = (p == rope) & (f >= 64) & (f < 96)
    d = f % 64
    c["perm_swa"] = (p == f - d + (d + SWA_ROT // 2) % SWA_ROT) & (d < SWA_ROT)
    pair = lambda i, j, s: (i // (2 * s) == j // (2 * s)) & ((i // s) % 2 == 1) & ((j // s) % 2 == 0)
    c["first_level"] = pair(p, f, 1)
    c["levels"] = np.concatenate([pair(f, p, 1 << k) for k in range(7)], axis=1)
    c["iota"] = np.broadcast_to(np.arange(48), (P, 48))
    q = np.arange(P)
    cols = np.zeros((P, 8), np.float64)
    r = (q - 64) % 32
    cols[:, C_INV_MLA] = np.where((q >= 64) & (q < 96), 10000.0 ** (-(2.0 * (r % 16)) / 32), 0)
    cols[:, C_SIGN_MLA] = np.where(r < 16, -1, 1)
    e = q % 64
    cols[:, C_INV_SWA] = np.where(e < 16, 500000.0 ** (-(2.0 * (e % 8)) / 16), 0)
    cols[:, C_SIGN_SWA] = np.where(e < 8, -1, 1)
    cols[:, C_TOKEN] = q
    cols[:, C_EPS] = EPS
    c["cols"] = cols
    return np.ascontiguousarray(np.concatenate([np.asarray(c[n], np.float32) for n in CONST], axis=1))


def _vectors(i):
    col = lambda v: v.reshape(-1, P).T
    row = lambda v: np.broadcast_to(v.reshape(1, -1), (P, v.size))
    few = lambda v: np.concatenate([v.reshape(-1, 1), np.zeros((P - v.size, 1), v.dtype)])
    v = {"norm_mix": col(i["norm_mix_g"]), "norm_cross": col(i["norm_cross_g"]), "norm_mem": col(i["norm_mem_g"]),
         "norm_ffn": col(i["norm_ffn_g"]), "ln_mem": col(i["ln_mem_2"]), "ln_kv": col(i["ln_kv_2"]),
         "ln_final": col(i["ln_final_2"]), "mla_q": col(i["mla_q_norm_g"]), "mla_kv": col(i["mla_kv_norm_g"]),
         "mla_out": col(i["mla_out_g"]), "diff_out": np.concatenate([i["diff_out_g"].reshape(-1, 1)] * 2),
         "gdn_norm": col(i["gdn_norm_2"]), "sinks": row(i["swa_sinks_2"]),
         "conv": i["gdn_conv_2"][0].reshape(CONV_K, 18, P).transpose(2, 1, 0).reshape(P, -1),
         "lam": row(np.concatenate([i[f"diff_lambda_{n}"].reshape(-1) for n in ("q1", "k1", "q2", "k2")])),
         "a_log": few(i["gdn_A_log_2"]), "dt": few(i["gdn_dt_bias_2"]),
         "router_b": row(np.concatenate([i["b_group_router"].reshape(-1), i["b_expert_router"].reshape(-1)])),
         "norm_final": col(i["norm_final_g"])}
    for l in range(2):
        v[f"ln_mix{l}"], v[f"ln_ffn{l}"] = col(i["ln_mix_2"][l]), col(i["ln_ffn_2"][l])
    return np.ascontiguousarray(np.concatenate([v[n] for n in VEC], axis=1))


def _arrays(i):
    w_in, w_gdn = i["w_in"][0], i["gdn_w_in_2"][0]
    a = {"x_t": _feature_major(i["x"][0]), "mem_t": _feature_major(i["mem"][0]),
         "mem2_t": _feature_major(i["mem_2"][0]), "consts": _constants(), "vectors": _vectors(i),
         "pos": i["positions"].reshape(S), "pos2": i["positions_2"].reshape(S),
         "pos_col": np.ascontiguousarray(i["positions"].reshape(QT, P).T)}
    a["router_w"] = np.ascontiguousarray(
        np.concatenate([i["w_group_router"][0], i["w_expert_router"][0]], axis=1)
        .reshape(KT, P, 36).transpose(1, 0, 2))
    a["w_in"] = _tiles(w_in, _blocks(15))
    a["w_kpe"] = _tiles(w_in, [np.arange(15 * P, 15 * P + MLA_ROPE)])
    a["w_uq"] = _tiles(i["w_mla_uq"][0], _blocks(MLA_HEADS, MLA_QK))
    a["w_ukv"] = _tiles(i["w_mla_ukv"][0], _blocks(MLA_HEADS))
    a["w_out"] = _tiles(i["w_out"][0], _blocks(KT))
    a["w_memkv"] = _tiles(i["w_mem_kv"][0], _blocks(8))
    a["w_memq"] = _tiles(i["w_mem_q"][0], _blocks(4))
    a["w_memo"] = _tiles(i["w_mem_o"][0], _blocks(KT))
    gu = np.concatenate([i["w_expert_gate"][0], i["w_expert_up"][0]], axis=2)
    gu = gu.reshape(N_EXPERTS, 4, 2, P, 512).transpose(0, 1, 3, 2, 4).reshape(N_EXPERTS, 4, P, 1024)
    a["w_experts"] = np.ascontiguousarray(
        np.concatenate([gu, i["w_expert_down"][0].reshape(N_EXPERTS, 2, P, 1024)], axis=1))
    a["w_mem2"] = np.concatenate([_tiles(i["w_mem_kv_2"][l], _blocks(4)) for l in range(2)])
    z0 = 3 * GDN_W
    ba = z0 + GDN_W
    a["w_gdnin"] = _tiles(w_gdn, _blocks(24) + _blocks(2, P, ba + 2 * GDN_HEADS))
    a["w_ba"] = _tiles(w_gdn, _blocks(2, GDN_HEADS, ba))
    kv = _blocks(4, 64)
    a["w_kv"] = _tiles(i["w_kv_2"], [np.tile(kv[0], 2), np.tile(kv[1], 2), np.concatenate(kv[2:])])
    a["w_swaq"] = _tiles(i["swa_w_q_2"][0], _blocks(8))
    for l in range(2):
        a[f"w_out{l}"] = _tiles(i["w_out_2"][l], _blocks(KT))
        at = 0
        for p, n in enumerate(FF_PARTS):
            gate, up = _blocks(n, P, at * P), _blocks(n, P, D_FF + at * P)
            a[f"w_gu{l}{p}"] = _tiles(i["w_gate_up_2"][l], [c for pair in zip(gate, up) for c in pair])
            a[f"w_down{l}{p}"] = _tiles(i["w_down_2"][l][at * P:(at + n) * P], _blocks(KT))
            at += n
    return a


def _described(nc, shapes):
    aps = {n: nc.dram_tensor(n, list(shape), mybir.dt.from_np(dtype), kind="ExternalInput").ap()
           for n, (shape, dtype) in shapes.items()}
    aps["out"] = nc.dram_tensor("out", [P, KT, S], F32, kind="ExternalOutput").ap()
    return aps


def kernel(**inputs):
    import concourse.bacc as _bacc
    from concourse.bass_utils import run_bass_kernel_spmd as _run

    arrays = _arrays({k: np.asarray(v) for k, v in inputs.items()})
    shapes = {n: (v.shape, v.dtype) for n, v in arrays.items()}
    counting = _bacc.Bacc("TRN2", target_bir_lowering=False, num_devices=1)
    counted = program(counting, _described(counting, shapes), defaultdict(lambda: 1))
    nc = _bacc.Bacc("TRN2", target_bir_lowering=False, num_devices=1)
    program(nc, _described(nc, shapes), counted)
    r = _run(nc, [arrays], core_ids=[0])
    out = r.results[0]["out"]
    return out.transpose(1, 0, 2).reshape(D, S).T.reshape(1, S, D)
```

```python
import math
from collections import defaultdict
from contextlib import ExitStack

import concourse.bass as bass
import numpy as np
from concourse import mybir

F32 = mybir.dt.float32
F32R = mybir.dt.float32r
I32 = mybir.dt.int32
U32 = mybir.dt.uint32
ALU = mybir.AluOpType
ACT = mybir.ActivationFunctionType
AX_X = mybir.AxisListType.X

P = 128
S = 512
D = 1024
KT = D // P
QT = S // P
NMEM = 256
EPS = 1e-6
NEG = -1e30

DIFF_HEADS, DIFF_HALF, DIFF_V = 8, 32, 64
MLA_HEADS, MLA_NOPE, MLA_ROPE, MLA_V = 8, 64, 32, 64
MLA_QK = MLA_NOPE + MLA_ROPE
MEM_HEADS, MEM_DH1, MEM_DH2 = 4, 128, 64
N_GROUPS, PER_GROUP = 4, 8
N_EXPERTS = N_GROUPS * PER_GROUP
EXPERT_FF = 256
SLOTS = 64
NB_MAX = -(-(2 * S + N_EXPERTS * (SLOTS - 1)) // SLOTS)
NB_MIN = 2 * S // SLOTS
SLOT_BITS = SLOTS.bit_length() - 1
NBC = NB_MAX + 1
LAMBDA_INIT = 0.8 - 0.6 * math.exp(0.0)

GDN_HEADS, GDN_D = 6, 128
GDN_W = GDN_HEADS * GDN_D
CONV_K = 4
SWA_HEADS, SWA_KV, SWA_DH, SWA_ROT = 12, 2, 64, 16
D_FF = 2816
FF_TILES = D_FF // P
FF_PARTS = (8, 7, 7)
RING, SPLIT, BANKS = 6, 3, 2

CONST = {}
_w = 0
for _n, _k in (("ident", P), ("upper", P), ("lower", P), ("incl", P), ("causal", P), ("prev", P),
               ("ones", P), ("blk64", P), ("perm_mla", P), ("perm_swa", P), ("first_level", P),
               ("levels", 7 * P), ("iota", 56), ("cols", 8)):
    CONST[_n] = (_w, _k)
    _w += _k
CONST_W = _w
C_INV_MLA, C_SIGN_MLA, C_INV_SWA, C_SIGN_SWA, C_TOKEN, C_EPS = range(6)

VEC = {}
_w = 0
for _n, _k in (("norm_mix", KT), ("norm_cross", KT), ("norm_mem", KT), ("norm_ffn", KT), ("ln_mem", KT),
               ("ln_mix0", KT), ("ln_mix1", KT), ("ln_ffn0", KT), ("ln_ffn1", KT), ("ln_kv", KT),
               ("ln_final", KT), ("mla_q", 2), ("mla_kv", 1), ("mla_out", 4), ("diff_out", 1),
               ("gdn_norm", 1), ("conv", 18 * CONV_K), ("sinks", SWA_HEADS), ("lam", 4 * DIFF_HALF),
               ("a_log", 1), ("dt", 1), ("router_b", 36), ("norm_final", KT)):
    VEC[_n] = (_w, _k)
    _w += _k
VEC_W = _w

STAGES = [("in", 15, KT, P, S), ("kpe", 1, KT, MLA_ROPE, S), ("uq", MLA_HEADS, 2, MLA_QK, S),
          ("ukv", MLA_HEADS, 1, P, S), ("out", KT, KT, P, S),
          ("memkv", 8, KT, P, NMEM), ("memq", 4, KT, P, S), ("memo", KT, 4, P, S),
          ("mem2", 8, KT, P, NMEM),
          ("gdnin", 26, KT, P, S), ("ba", 2, KT, GDN_HEADS, S), ("out0", KT, KT, P, S)]
for _l in range(2):
    if _l == 1:
        STAGES += [("kv", 3, KT, P, S), ("swaq", 8, KT, P, S), ("out1", KT, KT, P, S)]
    for _p, _n in enumerate(FF_PARTS):
        STAGES += [(f"gu{_l}{_p}", 2 * _n, KT, P, S), (f"down{_l}{_p}", KT, _n, P, S)]
BASE = {}
_t = 0
for _s in STAGES:
    BASE[_s[0]] = _t
    _t += _s[1]
N_TILES = _t
MOE_AT = BASE["mem2"]
STAGE_OF = {_s[0]: _s for _s in STAGES}
TILE = [_s for _s in STAGES for _ in range(_s[1])]


class Events:

    def __init__(self, nc, ctx, plan):
        self.nc, self.ctx, self.plan = nc, ctx, plan
        self.sems, self.count, self.seen, self.waited = {}, {}, {}, {}

    def sem(self, name):
        if name not in self.sems:
            self.sems[name] = self.ctx.enter_context(self.nc.semaphore(name))
        return self.sems[name]

    def done(self, ins, name, label=None, by=1):
        ins.then_inc(self.sem(name), by)
        self.count[name] = self.count.get(name, 0) + by
        if label is not None:
            self.seen[name, label] = self.count[name]

    def wait(self, eng, name, value):
        if self.waited.get((id(eng), name), 0) < value:
            eng.wait_ge(self.sem(name), value)
            self.waited[id(eng), name] = value

    def need(self, eng, name, label):
        self.wait(eng, name, self.plan[name, label])

    def step(self, eng, ins, name, label=None):
        self.done(ins, name, label)
        self.wait(eng, name, self.count[name])


def program(nc, a, plan, stop=None):
    with ExitStack() as ctx:
        ev = Events(nc, ctx, plan)
        done, need, step = ev.done, ev.need, ev.step

        at = [16512]

        def place(name, shape, dt, where=None):
            size = int(np.prod(shape[1:])) * 4
            off = at[0] if where is None else where
            if where is None:
                at[0] += -(-size // 32) * 32
            return nc.alloc_sbuf_tensor_at(name, shape, dt, offset=off), off

        X, _ = place("x", [P, KT, S], F32)
        AR, ar_at = place("split_acts", [P, 32, S], F32R)
        AF, _ = place("split_acts_as_f32", [P, 32, S], F32, ar_at)
        WRAW, _ = place("w_raw", [P, RING, 1024], F32)
        WH, _ = place("w_high", [P, SPLIT, 1024], F32R)
        WL, _ = place("w_low", [P, SPLIT, 1024], F32R)
        H, _ = place("h", [P, 8, S], F32)
        SC, sc_at = place("scratch", [P, 2, S], F32)
        G, g_at = place("g", [P, 24, S], F32)
        GI, _ = place("g_as_int", [P, 24, S], I32, g_at)
        CB, _ = place("consts", [P, CONST_W], F32)
        VB, _ = place("vectors", [P, VEC_W], F32)
        ROOTS, _ = place("roots", [P, 64], F32)
        COL, col_at = place("columns", [P, 96], F32)
        COLI, _ = place("columns_as_int", [P, 96], I32, col_at)
        COLU, _ = place("columns_as_uint", [P, 96], U32, col_at)

        pairs = [ctx.enter_context(nc.psum_tensor(f"ps_pair{i}", [P, 2, 512], F32)) for i in range(2)]
        ps_t = [ctx.enter_context(nc.psum_tensor(f"ps_turn{i}", [P, 512], F32)) for i in range(2)]
        ps_o, ps_m = (ctx.enter_context(nc.psum_tensor(n, [P, 512], F32)) for n in ("ps_out", "ps_shared"))
        ps_lin, ps_s = ([q[:, i, :] for i in range(2)] for q in pairs)

        def const(name, rows=P):
            o, w = CONST[name]
            return CB[0:rows, o:o + w]

        def col(i, rows=slice(0, P)):
            o = CONST["cols"][0] + i
            return CB[rows, o:o + 1]

        def vec(name, i=0, n=1, rows=slice(0, P)):
            o = VEC[name][0] + i
            return VB[rows, o:o + n]

        ident = const("ident")
        slot_tok = nc.dram_tensor("slot_tok", [SLOTS * NBC, 1], I32).ap()
        rows_h = nc.dram_tensor("rows_h", [S, D], F32).ap()
        rows_y = nc.dram_tensor("rows_y", [(NB_MAX + 1) * SLOTS, D], F32).ap()

        w_loaded = [ctx.enter_context(nc.semaphore(f"w_loaded{i}")) for i in range(RING)]
        high_ready, low_ready, tile_done = (ctx.enter_context(nc.semaphore(n))
                                            for n in ("high_ready", "low_ready", "tile_done"))
        evacuated = [ctx.enter_context(nc.semaphore(f"evacuated{i}")) for i in range(BANKS)]

        def wait_evac(eng, t):
            eng.wait_ge(evacuated[t % BANKS], t // BANKS + 1)

        def wait_stage_evac(eng, name, upto=None):
            last = BASE[name] + (STAGE_OF[name][1] if upto is None else upto) - 1
            for t in (last - 1, last):
                if t >= BASE[name]:
                    wait_evac(eng, t)

        def wait_products(eng, name):
            eng.wait_ge(tile_done, BASE[name] + STAGE_OF[name][1])

        def segment_end(t):
            return MOE_AT if t < MOE_AT else N_TILES

        def split_high(act, t):
            _, _, kt, m, _ = TILE[t]
            act.wait_ge(w_loaded[t % RING], 16 * (t // RING + 1))
            if t >= SPLIT:
                act.wait_ge(tile_done, t - SPLIT + 1)
            act.activation(WH[:, t % SPLIT, 0:kt * m], WRAW[:, t % RING, 0:kt * m],
                           ACT.Copy).then_inc(high_ready, 1)

        def split_low(dve, t):
            _, _, kt, m, _ = TILE[t]
            dve.wait_ge(high_ready, t + 1)
            dve.tensor_tensor(WL[:, t % SPLIT, 0:kt * m], WRAW[:, t % RING, 0:kt * m],
                              WH[:, t % SPLIT, 0:kt * m].bitcast(F32), ALU.subtract).then_inc(low_ready, 1)

        AHEAD = SPLIT - 1
        scores_read = []

        class Linear:

            def __init__(self, name, high, low, ready, take_act=None, take_dve=None, before=None):
                self.name, self.high, self.low, self.ready = name, high, low, ready
                self.take_act, self.take_dve, self.before = take_act, take_dve, before
                _, self.nt, self.kt, self.m, self.n = STAGE_OF[name]
                self.base = BASE[name]

            def tensor(self, pe):
                while scores_read:
                    need(pe, *scores_read.pop())
                for j in range(self.nt):
                    t = self.base + j
                    pe.wait_ge(low_ready, t + 1)
                    if t >= BANKS:
                        wait_evac(pe, t - BANKS)
                    out = ps_lin[t % BANKS][0:self.m, 0:self.n]
                    w = slice(0, self.kt * self.m)
                    wh = WH[:, t % SPLIT, w].rearrange("p (k m) -> p k m", m=self.m)
                    wl = WL[:, t % SPLIT, w].rearrange("p (k m) -> p k m", m=self.m)
                    for k in range(self.kt):
                        if j == 0 and self.ready is not None:
                            need(pe, *self.ready(k))
                        pe.matmul(out, wh[:, k, :], self.high(k), start=(k == 0), stop=False)
                        pe.matmul(out, wh[:, k, :], self.low(k), start=False, stop=False)
                        last = pe.matmul(out, wl[:, k, :], self.high(k), start=False, stop=(k == self.kt - 1))
                    last.then_inc(tile_done, 1)

            def scalar(self, act):
                if self.before:
                    self.before(act)
                for j in range(self.nt):
                    t = self.base + j
                    if t + AHEAD < segment_end(t):
                        split_high(act, t + AHEAD)
                    if self.take_act:
                        self.take_act(act, j, t, ps_lin[t % BANKS][0:self.m, 0:self.n])

            def vector(self, dve):
                for j in range(self.nt):
                    t = self.base + j
                    if t + AHEAD < segment_end(t):
                        split_low(dve, t + AHEAD)
                    if self.take_dve:
                        self.take_dve(dve, j, t, ps_lin[t % BANKS][0:self.m, 0:self.n])

        class Prime:

            def __init__(self, t0):
                self.t0 = t0

            def tensor(self, pe):
                pass

            def scalar(self, act):
                for t in range(self.t0, self.t0 + AHEAD):
                    split_high(act, t)

            def vector(self, dve):
                for t in range(self.t0, self.t0 + AHEAD):
                    split_low(dve, t)

        def taker(dest, waits=None):
            def take(act, j, t, out):
                if j == 0 and waits:
                    waits(act)
                act.wait_ge(tile_done, t + 1)
                act.copy(dest(j), out).then_inc(evacuated[t % BANKS], 1)
            return take

        def add_to_x(dve, j, t, out):
            dve.wait_ge(tile_done, t + 1)
            dve.tensor_tensor(X[:, j, :], X[:, j, :], out, ALU.add).then_inc(evacuated[t % BANKS], 1)

        held = []

        def claim(pe):
            while held:
                need(pe, *held.pop())

        ones_col = const("ones")[:, 0:1]

        class Norm:

            def __init__(self, name, kt, width, src, gain, dst, high, low, wait_src, wait_dst=None, scale=1.0 / D,
                         early=False, roots_of=None):
                self.name, self.kt, self.width, self.src = name, kt, width, src
                self.gain, self.dst, self.high, self.low = gain, dst, high, low
                self.wait_src, self.wait_dst, self.scale = wait_src, wait_dst, scale
                self.early, self.roots_of = early, roots_of
                self.sq = AF[:, 24:32, :].rearrange("p k s -> p (k s)")
                self.total = H[:, 6, :] if early else self.sq
                self.columns = width // P

            def square(self, act, k):
                if k >= 2:
                    need(act, "norm_dve", (self.name, "part", k - 2))
                dst = H[:, 6, :] if k == 0 else H[:, 4 + k % 2, :]
                done(act.activation(dst, self.src(k), ACT.Square), "norm_act", (self.name, "sq", k))

            def add_square(self, dve, k):
                need(dve, "norm_act", (self.name, "sq", k))
                if k:
                    step(dve, dve.tensor_tensor(H[:, 6, :], H[:, 6, :], H[:, 4 + k % 2, :], ALU.add),
                         "norm_dve", (self.name, "sum"))
                    ev.seen["norm_dve", (self.name, "part", k)] = ev.seen["norm_dve", (self.name, "sum")]
                else:
                    ev.seen["norm_dve", (self.name, "part", 0)] = 0

            def scalar(self, act):
                w = self.width
                if not self.roots_of:
                    ev.wait(act, "ld_const", 16)
                    act.activation(ROOTS[:, 63:64], col(C_EPS), ACT.Sqrt)
                    if not self.early:
                        self.wait_src(act)
                        for k in range(self.kt):
                            done(act.activation(self.sq[:, k * w:(k + 1) * w], self.src(k), ACT.Square),
                                 "norm_act", (self.name, "sq", k))
                    need(act, "norm_pe", (self.name, "sum"))
                    done(act.activation(ROOTS[:, 0:self.columns], ps_m[:, 0:self.columns], ACT.Sqrt,
                                        bias=col(C_EPS), scale=self.scale), "norm_act", (self.name, "root"))
                if self.high is None:
                    return
                for k in range(self.kt):
                    if k == 0 and self.wait_dst:
                        self.wait_dst(act)
                    need(act, "norm_dve", (self.name, "h", k))
                    done(act.activation(self.high(k), self.dst(k), ACT.Copy), "norm_act", (self.name, "high", k))

            def vector(self, dve):
                w = self.width
                if self.early:
                    self.add_square(dve, self.kt - 1)
                elif not self.roots_of:
                    for k in range(self.kt):
                        need(dve, "norm_act", (self.name, "sq", k))
                        if k:
                            step(dve, dve.tensor_tensor(self.sq[:, 0:w], self.sq[:, 0:w],
                                                        self.sq[:, k * w:(k + 1) * w], ALU.add),
                                 "norm_dve", (self.name, "sum"))
                if not self.roots_of:
                    need(dve, "norm_act", (self.name, "root"))
                    rs = ROOTS[:, 0:self.columns]
                    step(dve, dve.reciprocal(rs, rs), "norm_dve", (self.name, "rstd"))
                need(dve, "norm_pe", (self.name, "spread"))
                for k in range(self.kt):
                    if k == 0 and self.wait_dst:
                        self.wait_dst(dve)
                    done(dve.scalar_tensor_tensor(out=self.dst(k), in0=self.src(k), scalar=self.gain(k),
                                                  in1=ps_m[:, 0:w], op0=ALU.mult, op1=ALU.mult),
                         "norm_dve", (self.name, "h", k))
                    if self.high is not None and k:
                        self.lower(dve, k - 1)
                if self.high is not None:
                    self.lower(dve, self.kt - 1)

            def lower(self, dve, k):
                need(dve, "norm_act", (self.name, "high", k))
                done(dve.tensor_tensor(self.low(k), self.dst(k), self.high(k).bitcast(F32), ALU.subtract),
                     "norm_dve", (self.name, "low", k))

            def tensor(self, pe):
                claim(pe)
                if not self.roots_of:
                    if self.kt > 1:
                        need(pe, "norm_dve", (self.name, "sum"))
                    else:
                        need(pe, "norm_act", (self.name, "sq", 0))
                    for i in range(self.columns):
                        last = pe.matmul(ps_m[:, i:i + 1], self.total[:, i * P:(i + 1) * P], ones_col,
                                         start=True, stop=True)
                    done(last, "norm_pe", (self.name, "sum"))
                    need(pe, "norm_dve", (self.name, "rstd"))
                for i in range(self.columns):
                    last = pe.matmul(ps_m[:, i * P:(i + 1) * P], ROOTS[:, i:i + 1].to_broadcast([P, P]), ident,
                                     start=True, stop=True)
                done(last, "norm_pe", (self.name, "spread"))
                held.append(("norm_dve", (self.name, "h", self.kt - 1)))

            def ready(self, k):
                return "norm_dve", (self.name, "low", k)

        def add_and_square(norm):
            def take_act(act, j, t, out):
                wait_evac(act, t)
                norm.square(act, j)

            def take_dve(dve, j, t, out):
                add_to_x(dve, j, t, out)
                if j:
                    norm.add_square(dve, j - 1)
            return take_act, take_dve

        class Split:

            def __init__(self, name, kt, src, high, low, waits):
                self.name, self.kt, self.src, self.high, self.low, self.waits = name, kt, src, high, low, waits

            def tensor(self, pe):
                pass

            def scalar(self, act):
                self.waits(act)
                for k in range(self.kt):
                    done(act.activation(self.high(k), self.src(k), ACT.Copy), "split_act", (self.name, k))

            def vector(self, dve):
                self.waits(dve)
                for k in range(self.kt):
                    need(dve, "split_act", (self.name, k))
                    done(dve.tensor_tensor(self.low(k), self.src(k), self.high(k).bitcast(F32), ALU.subtract),
                         "split_dve", (self.name, k))

            def ready(self, k):
                return "split_dve", (self.name, k)

        class On:

            def __init__(self, tensor=None, scalar=None, vector=None, gpsimd=None, sync=None):
                nothing = lambda eng: None
                self.tensor, self.scalar, self.vector = tensor or nothing, scalar or nothing, vector or nothing
                self.gpsimd, self.sync = gpsimd or nothing, sync or nothing

        turns = {"n": 0}

        class Transposes:

            def __init__(self, name, groups, wait_first=None):
                self.name, self.groups, self.wait_first = name, groups, wait_first
                self.t0 = turns["n"]
                turns["n"] += len(groups)

            def tensor(self, pe):
                if self.wait_first:
                    self.wait_first(pe)
                for g, (blocks, _, waits) in enumerate(self.groups):
                    if waits:
                        waits(pe)
                    n = self.t0 + g
                    if n >= 2:
                        need(pe, "turn_act", n - 2)
                    elif n == 0:
                        pass
                    last = None
                    for b, (src, at_) in enumerate(blocks):
                        rows = src.shape[0]
                        wid = src.shape[1]
                        last = pe.transpose(ps_t[n % 2][0:wid, at_:at_ + rows], src, ident[0:rows, 0:rows])
                    done(last, "turn_pe", n)

            def scalar(self, act):
                for g, (blocks, (dst, src_of), _) in enumerate(self.groups):
                    n = self.t0 + g
                    need(act, "turn_pe", n)
                    if g == 0 and self.wait_first:
                        self.wait_first(act)
                    done(act.copy(dst, src_of(ps_t[n % 2])), "turn_act", n)

            def vector(self, dve):
                pass

        seen_groups, seen_heads, seen_outs = {"n": 0}, {"n": 0}, {"n": 0}

        class Attention:

            def __init__(self, name, heads, kind, scale, scores, probs, turned, pv, out, wait_scores, wait_v,
                         next_tile, wait_out=None, per_tile=2):
                self.name, self.heads, self.kind, self.scale = name, heads, kind, scale
                self.scores, self.probs, self.turned, self.per_tile = scores, probs, turned, per_tile
                self.pv, self.out, self.wait_scores, self.wait_v = pv, out, wait_scores, wait_v
                self.wait_out, self.next_tile = wait_out, next_tile
                wide_ = [(h, i) for h in range(heads) for i in range(QT)]
                if kind == "alibi":
                    self.groups = [([(h, i, 0), (h, i, 1)], (i + 1) * P,
                                    [(h, i, [(0, b) for b in range(i + 1)])], [h] if i == QT - 1 else [])
                                   for h, i in wide_]
                elif kind == "causal":
                    self.groups = [([(h, i, 0), (h + 1, i, 0)], (i + 1) * P,
                                    [(h + r, i, [(r, b) for b in range(i + 1)]) for r in range(2)],
                                    [h, h + 1] if i == QT - 1 else []) for h, i in wide_ if h % 2 == 0]
                else:
                    self.groups = [([(h, i, 0) for i in range(QT)], 2 * P,
                                    [(h, b, [(i, b) for i in range(QT)]) for b in range(2)], [h])
                                   for h in range(heads)]
                self.m0, self.h0, self.o0 = seen_groups["n"], seen_heads["n"], seen_outs["n"]
                self.u0, u = [], turns["n"]
                for group in self.groups:
                    self.u0.append(u)
                    u += len(group[2])
                seen_groups["n"] += len(self.groups)
                seen_heads["n"] += heads
                seen_outs["n"] += heads // per_tile
                turns["n"] = u
                self.last = ("att_act", ("out", seen_outs["n"] - 1))

            def member(self, buf, j, w):
                return buf[:, j // 2, (j % 2) * w:(j % 2 + 1) * w] if self.kind in ("full", "window") \
                    else buf[:, j, 0:w]

            def all_members(self, buf, w):
                if self.kind in ("full", "window"):
                    return buf[:, :, :].rearrange("p b (a w) -> p (b a) w", w=w)
                return buf[:, :, 0:w]

            def bank(self, m):
                return pairs[m % 2]

            def prob(self, n):
                return self.probs[n % len(self.probs)]

            def place_turned(self, h, i, nb):
                t = self.turned[h % len(self.turned)]
                if self.kind in ("full", "window"):
                    return t[:, i, :], lambda b: b[:, :]
                return (t[:, 0:nb, i * P:(i + 1) * P],
                        lambda b: b[:, 0:nb * P].rearrange("p (b q) -> p b q", q=P))

            def tensor(self, pe):
                self.wait_scores(pe)
                claim(pe)
                for t in (self.next_tile - 2, self.next_tile - 1):
                    wait_evac(pe, t)
                self.pe_scores(pe, 0)
                for n in range(len(self.groups)):
                    if n + 1 < len(self.groups):
                        self.pe_scores(pe, n + 1)
                    self.pe_turn(pe, n)
                    if n:
                        self.pe_values(pe, n - 1)
                self.pe_values(pe, len(self.groups) - 1)
                held.append(self.last)
                scores_read.append(self.last)

            def pe_scores(self, pe, n):
                members, w, _, _ = self.groups[n]
                m = self.m0 + n
                if m >= 2:
                    need(pe, "att_act", ("exp", m - 2))
                for j, (h, i, r) in enumerate(members):
                    lhs, rhs = self.scores(h, i, r)
                    last = pe.matmul(self.member(self.bank(m), j, w), lhs, rhs, start=True, stop=True,
                                     skip_group_check=True)
                done(last, "att_pe", ("scores", m))

            def pe_turn(self, pe, n):
                _, w, turns_, _ = self.groups[n]
                need(pe, "att_dve", ("probs", self.m0 + n))
                for q, (_, _, blocks) in enumerate(turns_):
                    u = self.u0[n] + q
                    if u >= 2:
                        need(pe, "turn_act", u - 2)
                    for at_, (j, b) in enumerate(blocks):
                        src = self.member(self.prob(n), j, w)[:, b * P:(b + 1) * P]
                        last = pe.transpose(ps_t[u % 2][:, at_ * P:(at_ + 1) * P], src, ident)
                    done(last, "turn_pe", u)

            def pe_values(self, pe, n):
                _, _, turns_, closes = self.groups[n]
                for h in closes:
                    o = self.o0 + h // self.per_tile
                    if h == 0:
                        self.wait_v(pe)
                    need(pe, "turn_act", self.u0[n] + len(turns_) - 1)
                    if o >= 2 and h % self.per_tile == 0:
                        need(pe, "att_act", ("out", o - 2))
                    rows, plan_ = self.pv(h)
                    for lhs, (slot, src, q0, q1), first, lastk in plan_:
                        last = pe.matmul((ps_o, ps_m)[o % 2][rows, q0:q1], lhs,
                                         self.turned[h % len(self.turned)][:, slot, src:src + q1 - q0],
                                         start=first, stop=lastk, skip_group_check=True)
                    done(last, "att_pe", ("values", self.h0 + h))

            def scalar(self, act):
                self.act_exp(act, 0)
                for n in range(len(self.groups)):
                    if n + 1 < len(self.groups):
                        self.act_exp(act, n + 1)
                    self.act_turn(act, n)
                    if n:
                        self.act_out(act, n - 1)
                self.act_out(act, len(self.groups) - 1)

            def act_exp(self, act, n):
                members, w, _, _ = self.groups[n]
                m, a_ = self.m0 + n, len(members)
                need(act, "att_dve", ("max", m))
                if n >= 2:
                    need(act, "turn_pe", self.u0[n - 1] - 1)
                c = 4 * (m % 2)
                if self.kind == "window":
                    done(act.activation(COL[:, 24 + c:24 + c + a_], COL[:, 24 + c:24 + c + a_], ACT.Exp),
                         "att_act", ("sink", m))
                for j in range(a_):
                    last = act.activation(self.member(self.prob(n), j, w), self.member(self.bank(m), j, w),
                                          ACT.Exp, bias=COL[:, c + j:c + j + 1], scale=self.scale,
                                          accum_out=COL[:, 8 + c + j:9 + c + j])
                done(last, "att_act", ("exp", m))

            def act_turn(self, act, n):
                for q, (h, i, blocks) in enumerate(self.groups[n][2]):
                    u = self.u0[n] + q
                    need(act, "turn_pe", u)
                    if n == 0 and q == 0 and self.wait_out:
                        self.wait_out(act)
                    if i == 0 and h >= len(self.turned):
                        need(act, "att_pe", ("values", self.h0 + h - len(self.turned)))
                    dst, src = self.place_turned(h, i, len(blocks))
                    done(act.copy(dst, src(ps_t[u % 2])), "turn_act", u)

            def act_out(self, act, n):
                closes = self.groups[n][3]
                if closes and closes[-1] % self.per_tile == self.per_tile - 1:
                    o = closes[-1] // self.per_tile
                    need(act, "att_pe", ("values", self.h0 + closes[-1]))
                    done(act.copy(self.out(o), (ps_o, ps_m)[(self.o0 + o) % 2][:, :]), "att_act",
                         ("out", self.o0 + o))

            def vector(self, dve):
                self.dve_max(dve, 0)
                for n in range(len(self.groups)):
                    if n + 1 < len(self.groups):
                        self.dve_max(dve, n + 1)
                    self.dve_probs(dve, n)

            def dve_max(self, dve, n):
                members, w, _, _ = self.groups[n]
                m, a_, c = self.m0 + n, len(members), 4 * ((self.m0 + n) % 2)
                h, i, _ = members[0]
                need(dve, "att_pe", ("scores", m))
                s = self.all_members(self.bank(m), w)
                if self.kind == "alibi":
                    slope = 2.0 ** (-8.0 * (h + 1) / DIFF_HEADS)
                    step(dve, dve.scalar_tensor_tensor(
                        out=s, in0=minus_dist(i).unsqueeze(1).to_broadcast([P, 2, w]), scalar=slope / self.scale,
                        in1=s, op0=ALU.mult, op1=ALU.add), "att_dve")
                elif self.kind == "causal":
                    diag = s[:, :, i * P:w]
                    step(dve, dve.tensor_tensor(diag, diag, const("causal").unsqueeze(1).to_broadcast([P, 2, P]),
                                                ALU.add), "att_dve")
                elif self.kind == "window":
                    step(dve, dve.tensor_tensor(s, s, WINDOW, ALU.add), "att_dve")
                top = COL[:, c:c + a_]
                step(dve, dve.tensor_reduce(top, s, AX_X, ALU.max), "att_dve")
                if self.kind == "window":
                    step(dve, dve.tensor_scalar(top, top, self.scale, vec("sinks", h), ALU.mult, ALU.max), "att_dve")
                    step(dve, dve.tensor_scalar(top, top, -1.0, None, ALU.mult), "att_dve")
                    step(dve, dve.tensor_scalar(COL[:, 24 + c:24 + c + a_], top, vec("sinks", h), None, ALU.add),
                         "att_dve", ("max", m))
                else:
                    step(dve, dve.tensor_scalar(top, top, -self.scale, None, ALU.mult), "att_dve", ("max", m))

            def dve_probs(self, dve, n):
                members, w, _, _ = self.groups[n]
                m, a_, c = self.m0 + n, len(members), 4 * ((self.m0 + n) % 2)
                need(dve, "att_act", ("exp", m))
                tot, inv = COL[:, 8 + c:8 + c + a_], COL[:, 16 + c:16 + c + a_]
                if self.kind == "window":
                    step(dve, dve.tensor_tensor(tot, tot, COL[:, 24 + c:24 + c + a_], ALU.add), "att_dve")
                step(dve, dve.reciprocal(inv, tot), "att_dve")
                part = lambda j: self.member(self.prob(n), j, w)
                col_ = lambda j: COL[:, 16 + c + j:17 + c + j]
                if self.kind == "alibi":
                    step(dve, dve.tensor_scalar(part(1), part(1), col_(1), LAM, ALU.mult, ALU.mult), "att_dve")
                    done(dve.scalar_tensor_tensor(out=part(0), in0=part(0), scalar=col_(0), in1=part(1),
                                                  op0=ALU.mult, op1=ALU.subtract), "att_dve", ("probs", m))
                else:
                    for j in range(a_):
                        last = dve.tensor_scalar(part(j), part(j), col_(j), None, ALU.mult)
                    done(last, "att_dve", ("probs", m))

        WINDOW = AF[:, 22:24, :].rearrange("p b (a w) -> p (b a) w", w=2 * P)

        LAM = COL[:, 32:33]
        DIST_OFF = [P * (i * (i + 1) // 2) for i in range(QT + 1)]
        dist = AF[:, 20:23, :].rearrange("p k s -> p (k s)")

        def minus_dist(i):
            return dist[:, DIST_OFF[i]:DIST_OFF[i + 1]]

        class HeadNorm:

            def __init__(self, name, tiles, src, parts, scale, finish, wait_src):
                self.name, self.tiles, self.src, self.parts = name, tiles, src, parts
                self.scale, self.finish, self.wait_src = scale, finish, wait_src
                o = CONST["blk64"][0]
                self.members = ones_col if parts == 1 else CB[:, o:o + P:P // 2]
                self.bank = lambda k: (ps_m, ps_o)[k % 2]

            def tensor(self, pe):
                n = self.parts
                claim(pe)
                for k in range(self.tiles):
                    need(pe, "hn_act", (self.name, "sq", k))
                    for i in range(QT):
                        c = (k * QT + i) * n
                        last = pe.matmul(ps_m[:, c:c + n], SC[:, k % 2, i * P:(i + 1) * P], self.members,
                                         start=True, stop=True)
                    done(last, "hn_pe", (self.name, "sum", k))
                need(pe, "hn_dve", (self.name, "rstd"))
                for k in range(self.tiles):
                    if k >= 2:
                        need(pe, "hn_dve", (self.name, k - 2))
                    for i in range(QT):
                        for r in range(n):
                            c, w = 4 + (k * QT + i) * n + r, P // n
                            last = pe.matmul(self.bank(k)[r * w:(r + 1) * w, i * P:(i + 1) * P],
                                             ROOTS[:, c:c + 1].to_broadcast([P, w]), ident,
                                             start=True, stop=True)
                    done(last, "hn_pe", (self.name, "spread", k))
                held.append(("hn_dve", (self.name, self.tiles - 1)))

            def scalar(self, act):
                act.activation(ROOTS[:, 63:64], col(C_EPS), ACT.Sqrt)
                self.wait_src(act)
                for k in range(self.tiles):
                    if k >= 2:
                        need(act, "hn_pe", (self.name, "sum", k - 2))
                    done(act.activation(SC[:, k % 2, :], self.src(k), ACT.Square), "hn_act",
                         (self.name, "sq", k))
                need(act, "hn_pe", (self.name, "sum", self.tiles - 1))
                n = self.tiles * QT * self.parts
                done(act.activation(ROOTS[:, 4:4 + n], ps_m[:, 0:n], ACT.Sqrt, bias=col(C_EPS),
                                    scale=self.scale), "hn_act", (self.name, "root"))

            def vector(self, dve):
                n = self.tiles * QT * self.parts
                need(dve, "hn_act", (self.name, "root"))
                step(dve, dve.reciprocal(ROOTS[:, 4:4 + n], ROOTS[:, 4:4 + n]), "hn_dve", (self.name, "rstd"))
                for k in range(self.tiles):
                    need(dve, "hn_pe", (self.name, "spread", k))
                    self.finish(dve, k, self.bank(k)[:, :], (self.name, k))

        def g(k, n=None):
            return G[:, k, :] if n is None else G[:, k:k + n, :]

        def load_waits(eng, *names):
            for n in names:
                ev.wait(eng, "ld_" + n, 16)

        lam_v = VEC["lam"][0]

        def early_vector(dve):
            load_waits(dve, "const", "vec", "pos", "posc")
            for i in range(2):
                step(dve, dve.tensor_tensor_reduce(out=SC[:, 0, 32 * i:32 * i + 32],
                                                   in0=vec("lam", 64 * i, 32), in1=vec("lam", 64 * i + 32, 32),
                                                   scale=1.0, scalar=0.0, op0=ALU.mult, op1=ALU.add,
                                                   accum_out=COL[:, 34 + i:35 + i]), "early_dve", ("lam", i))
            step(dve, dve.tensor_copy(g(18), GI[:, 16, :]), "early_dve")
            step(dve, dve.tensor_copy(COL[:, 36:40], COLI[:, 40:44]), "early_dve")
            for i in range(QT):
                w = (i + 1) * P
                step(dve, dve.tensor_scalar(minus_dist(i), G[:, 18, 0:w], COL[:, 36 + i:37 + i], None,
                                            ALU.subtract), "early_dve")
                step(dve, dve.scalar_tensor_tensor(out=minus_dist(i), in0=minus_dist(i), scalar=-1.0,
                                                   in1=minus_dist(i), op0=ALU.mult, op1=ALU.min), "early_dve")
                diag = minus_dist(i)[:, i * P:w]
                step(dve, dve.tensor_tensor(diag, diag, const("causal"), ALU.add), "early_dve")
            need(dve, "early_act", "lam")
            step(dve, dve.tensor_tensor(LAM, COL[:, 34:35], COL[:, 35:36], ALU.subtract), "early_dve")
            step(dve, dve.tensor_scalar(LAM, LAM, LAMBDA_INIT, None, ALU.add), "early_dve")
            step(dve, dve.tensor_scalar(COL[:, 33:34], vec("diff_out"), 1.0 - LAMBDA_INIT, None, ALU.mult),
                 "early_dve")

        def early_scalar(act):
            need(act, "early_dve", ("lam", 1))
            for i in range(2):
                done(act.activation(COL[:, 34 + i:35 + i], COL[:, 34 + i:35 + i], ACT.Exp), "early_act", "lam")

        TWO_PI_PARTS = (6.28125, 0.0019350051879882812, 2 * math.pi - 6.28125 - 0.0019350051879882812)

        class Angles:

            def __init__(self, name, pos, inv, sign, cos, sin, wait):
                self.name, self.pos, self.inv, self.sign = name, pos, inv, sign
                self.cos, self.sin, self.wait = cos, sin, wait

            def tensor(self, pe):
                pass

            def vector(self, dve):
                st = lambda ins, label=None: step(dve, ins, "angle_dve", label)
                self.wait(dve)
                pos_i, ang, k, ki = self.pos, g(18), g(19), GI[:, 19, :]
                st(dve.tensor_copy(ang, pos_i))
                st(dve.tensor_scalar(ang, ang, self.inv, None, ALU.mult))
                for out, turn, shift in ((self.sin, 0.0, 0.0), (self.cos, 0.25, math.pi / 2)):
                    st(dve.tensor_scalar(ki, ang, 1.0 / (2 * math.pi), turn, ALU.mult, ALU.add))
                    st(dve.tensor_copy(k, ki))
                    st(dve.tensor_copy(out, ang))
                    for c in TWO_PI_PARTS:
                        st(dve.scalar_tensor_tensor(out=out, in0=k, scalar=-c, in1=out, op0=ALU.mult, op1=ALU.add))
                    if shift:
                        st(dve.tensor_scalar(out, out, shift, None, ALU.add))
                    for sgn, cmp in ((1.0, ALU.is_gt), (-1.0, ALU.is_lt)):
                        st(dve.tensor_scalar(k, out, sgn * math.pi, -sgn * 2 * math.pi, cmp, ALU.mult))
                        st(dve.tensor_tensor(out, out, k, ALU.add))
                    st(dve.tensor_scalar(out, out, 3.1415925, -3.1415925, ALU.min, ALU.max),
                       (self.name, "arg", shift > 0))
                need(dve, "angle_act", self.name)
                st(dve.tensor_scalar(self.sin, self.sin, self.sign, None, ALU.mult), (self.name, "table"))

            def scalar(self, act):
                for out, shift in ((self.sin, False), (self.cos, True)):
                    need(act, "angle_dve", (self.name, "arg", shift))
                    done(act.activation(out, out, ACT.Sin), "angle_act", self.name)

        ropes = {"n": 0}

        class Rope:

            def __init__(self, name, tiles, rows, perm, cos, sin, waits):
                self.name, self.tiles, self.rows, self.perm = name, tiles, rows, perm
                self.cos, self.sin, self.waits = cos, sin, waits

            def tensor(self, pe):
                for k in range(len(self.tiles)):
                    if k == 0:
                        self.waits(pe)
                        claim(pe)
                    need_n = ("rope_dve", (self.name, "swap", k - 1))
                    if k:
                        need(pe, *need_n)
                    done(pe.matmul(ps_m[0:self.rows, :], self.perm[0:self.rows, 0:self.rows],
                                   self.tiles[k], start=True, stop=True), "rope_pe", (self.name, k))
                held.append(("rope_dve", (self.name, "swap", len(self.tiles) - 1)))

            def scalar(self, act):
                pass

            def vector(self, dve):
                r = slice(0, self.rows)
                for k, x in enumerate(self.tiles):
                    need(dve, "rope_pe", (self.name, k))
                    s = SC[r, k % 2, :]
                    step(dve, dve.tensor_tensor(s, ps_m[r, :], self.sin[r, :], ALU.mult), "rope_dve",
                         (self.name, "swap", k))
                    step(dve, dve.tensor_tensor(x, x, self.cos[r, :], ALU.mult), "rope_dve")
                    step(dve, dve.tensor_tensor(x, x, s, ALU.add), "rope_dve", (self.name, k))

        hi = lambda k: AR[:, k, :]
        lo = lambda k: AR[:, 8 + k, :]
        x_tile = lambda k: X[:, k, :]
        h_tile = lambda k: H[:, k, :]
        fl = []

        cos_m, sin_m = g(20), g(21)
        fl.append(On(scalar=early_scalar, vector=early_vector))
        fl.append(Angles("mla", GI[:, 16, :], col(C_INV_MLA), col(C_SIGN_MLA), cos_m, sin_m,
                         lambda e: load_waits(e, "pos")))
        n_mix = Norm("mix", KT, S, x_tile, lambda k: vec("norm_mix", k), h_tile, hi, lo,
                     lambda e: load_waits(e, "x", "const", "vec"))
        fl += [Prime(0), n_mix]
        in_dest = lambda j: (g(j) if j < 8 else AF[:, 16 + j - 8, :] if j < 12 else g(j))
        fl.append(Linear("in", hi, lo, n_mix.ready, taker(in_dest)))
        fl.append(Linear("kpe", hi, lo, None, taker(lambda j: G[0:MLA_ROPE, 15, :])))
        fl.append(Transposes("diff_v", [
            ([(AF[:, 16 + c, i * P:(i + 1) * P], c * P) for c in range(4)],
             (g(8 + i), lambda b: b[:, :]), None) for i in range(QT)],
            wait_first=lambda e: wait_stage_evac(e, "in", 12)))

        def diff_scores(h, i, r):
            p0 = 64 * (h % 2) + 32 * r
            return (G[p0:p0 + 32, h // 2, i * P:(i + 1) * P], G[p0:p0 + 32, 4 + h // 2, 0:(i + 1) * P])

        def causal_pv(v, heads_per_tile=2):
            def pv(h):
                rows = slice(64 * (h % 2), 64 * (h % 2) + 64)
                return rows, [(v(h, j), (j, j * P, j * P, S), j == 0, j == QT - 1) for j in range(QT)]
            return pv

        turned4 = (AF[:, 8:12, :], AF[:, 12:16, :])
        probs4 = (G[:, 16:18, :], G[:, 18:20, :])
        out_rows = lambda h: slice(64 * (h % 2), 64 * (h % 2) + 64)
        diff = Attention("diff", DIFF_HEADS, "alibi", DIFF_HALF ** -0.5, diff_scores, probs4, turned4,
                         causal_pv(lambda h, j: G[:, 8 + j, h * 64:(h + 1) * 64]),
                         h_tile, lambda e: wait_stage_evac(e, "in", 8), lambda e: None, BASE["uq"],
                         wait_out=lambda e: wait_products(e, "kpe"))
        fl.append(diff)
        last_head = lambda att: (lambda e: need(e, *att.last))

        n_cq = Norm("cq", 2, S, lambda k: g(12 + k), lambda k: vec("mla_q", k), lambda k: g(12 + k),
                    lambda k: AR[:, k, :], lambda k: AR[:, 2 + k, :], lambda e: wait_stage_evac(e, "in"),
                    scale=1.0 / 256)
        n_ckv = Norm("ckv", 1, S, lambda k: g(14), lambda k: vec("mla_kv"), lambda k: g(14),
                     lambda k: AR[:, 4, :], lambda k: AR[:, 5, :], lambda e: None, scale=1.0 / 128)
        fl += [n_cq, n_ckv]
        fl.append(Linear("uq", lambda k: AR[:, k, :], lambda k: AR[:, 2 + k, :], n_cq.ready,
                         taker(lambda h: AF[0:MLA_QK, 16 + h, :])))
        fl.append(Linear("ukv", lambda k: AR[:, 4, :], lambda k: AR[:, 5, :], n_ckv.ready,
                         taker(lambda h: AF[:, 24 + h, :])))

        def kpe_tile(dve):
            wait_evac(dve, BASE["kpe"])
            step(dve, dve.memset(G[0:64, 2, :], 0.0), "mla_dve")
            step(dve, dve.tensor_copy(G[64:96, 2, :], G[0:32, 15, :]), "mla_dve", "kpe")

        fl.append(On(vector=kpe_tile))
        mla_v = Transposes("mla_v", [
            ([(AF[:, 24 + h, i * P:(i + 1) * P], i * P) for i in range(QT)],
             (G[:, 4:8, h * 64:(h + 1) * 64],
              lambda b: b[:, :].rearrange("p (i c) -> p i c", c=P)[:, :, 64:128]), None)
            for h in range(MLA_HEADS)], wait_first=lambda e: wait_stage_evac(e, "ukv"))
        fl.append(mla_v)
        rope_q = Rope("mla_q", [AF[0:96, 16 + h, :] for h in range(MLA_HEADS)] + [G[0:96, 2, :]], 96,
                      const("perm_mla"), cos_m, sin_m,
                      lambda e: (wait_stage_evac(e, "uq"), need(e, "mla_dve", "kpe")))
        fl.append(rope_q)

        def spread_kpe(act):
            need(act, "rope_dve", ("mla_q", MLA_HEADS))
            need(act, "turn_act", mla_v.t0 + MLA_HEADS - 1)
            for h in range(MLA_HEADS):
                done(act.copy(AF[64:96, 24 + h, :], G[64:96, 2, :]), "mla_act", "keys")

        fl.append(On(scalar=spread_kpe))
        mla = Attention("mla", MLA_HEADS, "causal", MLA_QK ** -0.5,
                        lambda h, i, r: (AF[0:96, 16 + h, i * P:(i + 1) * P], AF[0:96, 24 + h, 0:(i + 1) * P]),
                        probs4, tuple(AF[:, 4 * k:4 * k + 4, :] for k in range(4)),
                        causal_pv(lambda h, j: G[:, 4 + j, h * 64:(h + 1) * 64]), lambda o: h_tile(4 + o),
                        lambda e: (need(e, "mla_act", "keys"), need(e, "rope_dve", ("mla_q", MLA_HEADS - 1))),
                        lambda e: None, BASE["out"], wait_out=lambda e: wait_products(e, "ukv"))
        fl.append(mla)

        def diff_gain(dve, k, s, label):
            done(dve.scalar_tensor_tensor(out=h_tile(k), in0=h_tile(k), scalar=COL[:, 33:34], in1=s,
                                          op0=ALU.mult, op1=ALU.mult), "hn_dve", label)

        fl.append(HeadNorm("diff", 4, h_tile, 2, 1.0 / DIFF_V, diff_gain, last_head(diff)))
        s_diff = Split("diff", 4, h_tile, hi, lo, lambda e: need(e, "hn_dve", ("diff", 3)))
        n_mo = Norm("mla_out", 4, S, lambda k: h_tile(4 + k), lambda k: vec("mla_out", k),
                    lambda k: h_tile(4 + k), lambda k: hi(4 + k), lambda k: lo(4 + k), last_head(mla),
                    scale=1.0 / S)
        fl += [s_diff, n_mo]
        n_cross = Norm("cross", KT, S, x_tile, lambda k: vec("norm_cross", k), h_tile, hi, lo,
                       lambda e: wait_stage_evac(e, "out"),
                       wait_dst=lambda e: (wait_products(e, "out")), early=True)
        fl.append(Linear("out", hi, lo, lambda k: s_diff.ready(k) if k < 4 else n_mo.ready(k - 4),
                         *add_and_square(n_cross)))

        cuts = {"mix": (len(fl), lambda e: wait_stage_evac(e, "out"), BASE["memkv"])}

        memv = lambda k0: G[:, k0:k0 + 4, :].rearrange("p k (a s) -> p (k a) s", a=2)
        raw1 = memv(20)
        mh = AR[:, 16:20, :].rearrange("p k (a s) -> p (k a) s", a=2)
        ml = AR[:, 20:24, :].rearrange("p k (a s) -> p (k a) s", a=2)
        n_mem = Norm("mem", KT, NMEM, lambda k: raw1[:, k, :], lambda k: vec("norm_mem", k),
                     lambda k: raw1[:, k, :], lambda k: mh[:, k, :], lambda k: ml[:, k, :],
                     lambda e: (load_waits(e, "mem"), last_head(mla)(e)))
        n_mem.sq = n_mem.total = H[:, 0:4, :].rearrange("p k s -> p (k s)")
        n_mem.wait_src = lambda e: (load_waits(e, "mem"), need(e, *n_mo.ready(3)), need(e, *s_diff.ready(3)))
        mk = memv(8)
        fl += [n_mem, Linear("memkv", lambda k: mh[:, k, :], lambda k: ml[:, k, :], n_mem.ready,
                             taker(lambda j: mk[:, j, :])), n_cross]
        fl.append(Linear("memq", hi, lo, n_cross.ready, taker(lambda j: g(4 + j))))
        mem_v = Transposes("mem_v", [
            ([(mk[:, 4 + c, i * P:(i + 1) * P], c * P) for c in range(4)], (g(12 + i), lambda b: b[:, :]), None)
            for i in range(2)], wait_first=lambda e: wait_stage_evac(e, "memkv"))
        fl.append(mem_v)
        cross = Attention("cross", MEM_HEADS, "full", MEM_DH1 ** -0.5,
                          lambda h, i, r: (G[:, 4 + h, i * P:(i + 1) * P], mk[:, h, :]),
                          probs4, (AF[:, 16:18, :], AF[:, 18:20, :]),
                          lambda h: (slice(0, P), [(G[:, 12 + j, h * P:(h + 1) * P], (j, 0, 0, S), j == 0, j == 1)
                                                   for j in range(2)]),
                          h_tile, lambda e: wait_stage_evac(e, "memq"), lambda e: None, BASE["memo"],
                          per_tile=1,
                          wait_out=lambda e: (wait_products(e, "memkv"), wait_products(e, "memq")))
        fl.append(cross)
        s_cross = Split("cross", 4, h_tile, hi, lo, last_head(cross))
        n_ffn = Norm("ffn", KT, S, x_tile, lambda k: vec("norm_ffn", k), h_tile, None, None,
                     lambda e: wait_stage_evac(e, "memo"), early=True)
        fl += [s_cross, Linear("memo", hi, lo, s_cross.ready, *add_and_square(n_ffn))]
        cuts["cross"] = (len(fl), lambda e: wait_stage_evac(e, "memo"), MOE_AT)

        fl.append(n_ffn)
        GU32, _ = place("g_as_uint", [P, 24, S], U32, g_at)
        RW = G[:, 0, 0:KT * 36].rearrange("p (k c) -> p k c", c=36)
        LG = G[:, 1, 0:QT * 36].rearrange("p (t c) -> p t c", c=36)
        GL = G[:, 1, 160:192].rearrange("p (t c) -> p t c", c=8)
        SEL = G[:, 1, 192:224].rearrange("p (t c) -> p t c", c=8)
        TOP = G[:, 1, 256:512].rearrange("p (t c) -> p t c", c=64)
        TOPU = GU32[:, 1, 256:512].rearrange("p (t c) -> p t c", c=64)
        HOT = G[:, 2, 0:256].rearrange("p (t k e) -> p t k e", k=2, e=32)
        BOTH = G[:, 2, 256:384].rearrange("p (t e) -> p t e", e=32)
        BEG, NBF, END, NBI, POS, JUNK = (G[:, 3, 32 * k:32 * k + 32] for k in range(6))
        NBI = GI[:, 3, 96:128]
        DEST = G[:, 3, 256:264]
        DESTI, DBLK, DROW = (GI[:, 3, 264 + 8 * k:272 + 8 * k] for k in range(3))
        FBLK, FROW = G[:, 3, 288:296], G[:, 3, 296:304]
        IDX, YIDX = GU32[:, 3, 304:312], GU32[:, 17, 128:136]
        TOKI = GI[:, 3, 320:324]
        WTS = G[:, 17, 160:168].rearrange("p (t k) -> p t k", k=2)
        IDS, ID_COL = GI[0:SLOTS, 17, 0:NBC], GI[0:SLOTS, 18, 0:1]
        BLK_E, N_BLK = GI[0:1, 19, 0:NBC], GI[0:1, 19, 60:61]
        iota = const("iota")

        def router_tensor(pe):
            ev.wait(pe, "ld_router", 16)
            claim(pe)
            for i in range(QT):
                for k in range(KT):
                    need(pe, "norm_dve", ("ffn", "h", k))
                    last = pe.matmul(ps_m[:, i * 36:(i + 1) * 36], H[:, k, i * P:(i + 1) * P], RW[:, k, :],
                                     start=(k == 0), stop=(k == KT - 1))
            done(last, "route_pe", "logits")
            need(pe, "route_dve", "both")
            for i in range(QT):
                for j in range(i + 1):
                    pe.matmul(ps_m[:, 32 * i:32 * i + 32], const("upper") if j == i else const("ones"),
                              BOTH[:, j, :], start=(j == 0), stop=(j == i))
            for j in range(QT):
                last = pe.matmul(ps_m[:, 128:160], const("ones"), BOTH[:, j, :], start=(j == 0), stop=(j == QT - 1))
            done(last, "route_pe", "ranks")

        def router_scalar(act):
            for i in range(QT):
                need(act, "route_dve", ("neg", i))
                done(act.activation(TOP[:, i, 40:44], GL[:, i, 0:4], ACT.Exp, bias=TOP[:, i, 32:33],
                                    accum_out=TOP[:, i, 34:35]), "route_act")
                done(act.activation(TOP[:, i, 35:36], TOP[:, i, 17:18], ACT.Exp, bias=TOP[:, i, 33:34]),
                     "route_act", ("exp", i))

        def router_vector(dve):
            st = lambda ins, label=None: step(dve, ins, "route_dve", label)
            ts, tt = dve.tensor_scalar, dve.tensor_tensor
            load_waits(dve, "router")
            st(dve.memset(GL[:, :, :], -3e38))
            need(dve, "route_pe", "logits")
            for i in range(QT):
                st(tt(LG[:, i, :], ps_m[:, i * 36:(i + 1) * 36], vec("router_b", 0, 36), ALU.add))
            st(dve.tensor_copy(GL[:, :, 0:4], LG[:, :, 0:4]))
            for i in range(QT):
                st(dve.max(TOP[:, i, 0:8], GL[:, i, :]))
                st(dve.max_index(TOPU[:, i, 8:16], TOP[:, i, 0:8], GL[:, i, :]))
                st(dve.tensor_copy(TOP[:, i, 36:37], TOPU[:, i, 8:9]))
                st(ts(TOP[:, i, 48:52], iota[:, 0:4], TOP[:, i, 36:37], None, ALU.is_equal))
                st(ts(SEL[:, i, :], LG[:, i, 4:12], TOP[:, i, 48:49], None, ALU.mult))
                for q in range(1, 4):
                    st(dve.scalar_tensor_tensor(out=SEL[:, i, :], in0=LG[:, i, 4 + 8 * q:12 + 8 * q],
                                                scalar=TOP[:, i, 48 + q:49 + q], in1=SEL[:, i, :],
                                                op0=ALU.mult, op1=ALU.add))
                st(dve.max(TOP[:, i, 16:24], SEL[:, i, :]))
                st(dve.max_index(TOPU[:, i, 24:32], TOP[:, i, 16:24], SEL[:, i, :]))
                st(ts(TOP[:, i, 32:33], TOP[:, i, 0:1], -1.0, None, ALU.mult))
                st(ts(TOP[:, i, 33:34], TOP[:, i, 16:17], -1.0, None, ALU.mult), ("neg", i))
                st(dve.tensor_copy(TOP[:, i, 38:40], TOPU[:, i, 24:26]))
                st(ts(TOP[:, i, 37:38], TOP[:, i, 36:37], float(PER_GROUP), None, ALU.mult))
                st(ts(TOP[:, i, 38:40], TOP[:, i, 38:40], TOP[:, i, 37:38], None, ALU.add))
                for q in range(2):
                    st(ts(HOT[:, i, q, :], iota[:, 0:32], TOP[:, i, 38 + q:39 + q], None, ALU.is_equal))
                st(tt(BOTH[:, i, :], HOT[:, i, 0, :], HOT[:, i, 1, :], ALU.add), "both")
            for i in range(QT):
                need(dve, "route_act", ("exp", i))
                st(dve.reciprocal(TOP[:, i, 44:45], TOP[:, i, 34:35]))
                st(ts(TOP[:, i, 45:46], TOP[:, i, 35:36], 1.0, None, ALU.add))
                st(dve.reciprocal(TOP[:, i, 46:47], TOP[:, i, 45:46]))
                st(tt(WTS[:, i, 0:1], TOP[:, i, 44:45], TOP[:, i, 46:47], ALU.mult))
                st(tt(WTS[:, i, 1:2], WTS[:, i, 0:1], TOP[:, i, 35:36], ALU.mult))
            need(dve, "route_pe", "ranks")
            st(ts(NBI, ps_m[:, 128:160], float(SLOTS - 1), None, ALU.add))
            st(ts(NBI, NBI, SLOT_BITS, None, ALU.arith_shift_right))
            st(dve.tensor_copy(NBF, NBI))
            st(dve.tensor_tensor_scan(END, const("ones")[:, 0:32], NBF, 0.0, ALU.mult, ALU.add))
            st(tt(BEG, END, NBF, ALU.subtract))
            st(ts(BEG, BEG, float(SLOTS), None, ALU.mult))
            for i in range(QT):
                st(tt(POS, BEG, ps_m[:, 32 * i:32 * i + 32], ALU.add), "ranks_read")
                for q in range(2):
                    st(dve.tensor_tensor_reduce(out=JUNK, in0=HOT[:, i, q, :], in1=POS, scale=1.0, scalar=0.0,
                                                op0=ALU.mult, op1=ALU.add,
                                                accum_out=DEST[:, 2 * i + q:2 * i + q + 1]))
            st(ts(YIDX, DEST, float(SLOTS), None, ALU.add))
            st(dve.tensor_copy(DESTI, DEST))
            st(ts(DBLK, DESTI, SLOT_BITS, None, ALU.arith_shift_right))
            st(ts(DROW, DESTI, SLOTS - 1, None, ALU.bitwise_and))
            st(dve.tensor_copy(FBLK, DBLK))
            st(dve.tensor_copy(FROW, DROW))
            st(dve.scalar_tensor_tensor(out=FROW, in0=FROW, scalar=float(NBC), in1=FBLK, op0=ALU.mult, op1=ALU.add))
            st(dve.tensor_copy(IDX, FROW))
            for i in range(QT):
                st(ts(TOKI[:, i:i + 1], col(C_TOKEN), float(i * P), None, ALU.add), "slots")
            table = AF[0:1, 16:20, :].rearrange("p k s -> p (k s)")[:, 0:NBC * 32].rearrange(
                "p (b e) -> p b e", e=32)
            st(tt(table, END[0:1, :].unsqueeze(1).to_broadcast([1, NBC, 32]),
                  iota[0:1, 0:NBC].unsqueeze(2).to_broadcast([1, NBC, 32]), ALU.is_le))
            st(dve.tensor_reduce(G[0:1, 19, 64:64 + NBC], table, AX_X, ALU.add))
            st(ts(BLK_E, G[0:1, 19, 64:64 + NBC], float(N_EXPERTS - 1), None, ALU.min))
            st(dve.tensor_copy(N_BLK, END[0:1, 31:32]), "plan")

        fl.append(On(tensor=router_tensor, scalar=router_scalar, vector=router_vector))
        rows_out = Transposes("rows", [
            ([(H[:, 4 * half + c, i * P:(i + 1) * P], c * P) for c in range(4)],
             (g(4 + 2 * i + half), lambda b: b[:, :]), None) for i in range(QT) for half in range(2)],
            wait_first=lambda e: need(e, "norm_dve", ("ffn", "h", KT - 1)))
        fl.append(rows_out)

        msem = lambda n: ctx.enter_context(nc.semaphore(n))
        m_load = [msem(f"m_load{p}") for p in range(6)]
        m_high, m_low, m_done = msem("m_high"), msem("m_low"), msem("m_done")
        x_ids, x_rows, x_turned, x_high, x_low = (msem(n) for n in ("x_ids", "x_rows", "x_turned", "x_high", "x_low"))
        m_silu, m_hidden, h_turned, h_high, h_low = (msem(n) for n in ("m_silu", "m_hidden", "h_turned", "h_high",
                                                                       "h_low"))
        y_taken, y_stored, y_over, x_go, pe_go, w_over = (msem(n) for n in ("y_taken", "y_stored", "y_over", "x_go", "pe_go", "w_over"))
        rows = slice(0, SLOTS)
        XB = G[rows, 12:14, :].rearrange("p k s -> p (k s)")
        YB = G[rows, 14:16, :]
        SG, HID = G[rows, 16, 0:256], G[rows, 16, 256:512]
        XH, XL = AR[:, 0, :], AR[:, 1, :]
        HH, HL = AR[:, 4, 0:2 * SLOTS], AR[:, 5, 0:2 * SLOTS]
        ps_gu, ps_y = ps_s[0], (ps_o, ps_s[1])
        PIECES, EARLY = 6, 4
        WHM = AR[:, 8:20, :].rearrange("p (q k) s -> p q (k s)", k=2)
        WLM = AR[:, 20:32, :].rearrange("p (q k) s -> p q (k s)", k=2)
        whm, wlm = (lambda p: WHM[:, p, :]), (lambda p: WLM[:, p, :])

        def n_blocks(eng):
            need(eng, "route_dve", "plan")
            return eng.value_load(N_BLK, min_val=NB_MIN, max_val=NB_MAX)

        def moe_sync(sp):
            cnt = n_blocks(sp)

            def load(b, e, p):
                sp.wait_ge(m_low, 6 * b + p + 1)
                sp.dma_start(WRAW[:, p, :], a["w_experts"][bass.ds(e, 1), p, :, :].rearrange("a p n -> (a p) n")
                             ).then_inc(m_load[p], 16)

            expert = lambda b: sp.value_load(BLK_E[:, bass.ds(b, 1)], min_val=0, max_val=N_EXPERTS - 1)
            e0 = sp.value_load(BLK_E[:, 0:1], min_val=0, max_val=N_EXPERTS - 1)
            ev.wait(sp, "st_fill", 16)
            sp.wait_ge(low_ready, MOE_AT)
            for p in range(EARLY):
                load(0, e0, p)
            with sp.Fori(0, cnt) as b:
                e = expert(b)
                for p in range(EARLY, PIECES):
                    load(b, e, p)
                e = expert(b + 1)
                for p in range(EARLY):
                    load(b + 1, e, p)
                sp.wait_ge(y_taken, 2 * b + 2)
                sp.dma_start(rows_y[bass.ds(b * SLOTS, SLOTS), :],
                             YB.rearrange("p k s -> p (k s)")).then_inc(y_stored, 16)
            sp.wait_ge(y_taken, 2 * cnt + 2)
            sp.dma_start(rows_y[bass.ds(cnt * SLOTS, SLOTS), :],
                         YB.rearrange("p k s -> p (k s)")).then_inc(y_stored, 16)
            sp.wait_ge(m_low, 6 * cnt + 10)

        def moe_high(act, b, p):
            act.wait_ge(m_load[p], 16 * b + 16)
            act.wait_ge(m_done, 6 * b + p + 1)
            act.activation(whm(p), WRAW[:, p, :], ACT.Copy).then_inc(m_high, 1)

        def moe_low(dve, b, p):
            dve.wait_ge(m_high, 6 * b + p + 1)
            dve.tensor_tensor(wlm(p), WRAW[:, p, :], whm(p).bitcast(F32), ALU.subtract).then_inc(m_low, 1)

        def x_split_high(act, b):
            act.wait_ge(x_turned, b + 1)
            act.activation(XH, ps_t[0][:, :], ACT.Copy).then_inc(x_high, 1)

        def x_split_low(dve, b):
            dve.wait_ge(x_high, b + 1)
            dve.tensor_tensor(XL, ps_t[0][:, :], XH.bitcast(F32), ALU.subtract).then_inc(x_low, 1)

        def x_turn(pe, b):
            pe.wait_ge(x_rows, 16 * b + 16)
            pe.sem_inc(pe_go, 1)
            for k in range(KT):
                last = pe.transpose(ps_t[0][:, k * SLOTS:(k + 1) * SLOTS], XB[:, k * P:(k + 1) * P],
                                    ident[rows, rows])
            last.then_inc(x_turned, 1)

        def moe_tensor(pe):
            cnt = n_blocks(pe)
            pe.wait_ge(tile_done, MOE_AT)
            need(pe, "turn_act", rows_out.t0 + 2 * QT - 1)
            pe.sem_inc(m_done, PIECES)
            x_turn(pe, 0)
            with pe.Fori(0, cnt) as b:
                pe.wait_ge(x_low, b + 1)
                for p in range(4):
                    pe.wait_ge(m_low, 6 * b + p + 7)
                    for kk in range(2):
                        k = 2 * p + kk
                        xs, w = slice(k * SLOTS, (k + 1) * SLOTS), slice(kk * 512, kk * 512 + 512)
                        pe.matmul(ps_gu[rows, :], XH[:, xs], whm(p)[:, w], start=(k == 0), stop=False)
                        pe.matmul(ps_gu[rows, :], XH[:, xs], wlm(p)[:, w], start=False, stop=False)
                        last = pe.matmul(ps_gu[rows, :], XL[:, xs], whm(p)[:, w], start=False, stop=(k == 7))
                    last.then_inc(m_done, 1)
                x_turn(pe, b + 1)
                pe.wait_ge(m_hidden, b + 1)
                pe.sem_inc(pe_go, 1)
                for q in range(2):
                    last = pe.transpose(ps_m[:, q * SLOTS:(q + 1) * SLOTS], HID[:, q * P:(q + 1) * P],
                                        ident[rows, rows])
                last.then_inc(h_turned, 1)
                pe.wait_ge(h_low, b + 1)
                for k in range(2):
                    pe.wait_ge(m_low, 6 * b + k + 11)
                    hs = slice(k * SLOTS, (k + 1) * SLOTS)
                    for n in range(2):
                        w = slice(n * 512, n * 512 + 512)
                        pe.matmul(ps_y[n][rows, :], HH[:, hs], whm(4 + k)[:, w], start=(k == 0), stop=False)
                        pe.matmul(ps_y[n][rows, :], HH[:, hs], wlm(4 + k)[:, w], start=False, stop=False)
                        last = pe.matmul(ps_y[n][rows, :], HL[:, hs], whm(4 + k)[:, w], start=False, stop=(k == 1))
                    last.then_inc(m_done, 1)

        def moe_scalar(act):
            cnt = n_blocks(act)
            act.wait_ge(tile_done, MOE_AT)
            for p in range(EARLY):
                moe_high(act, 0, p)
            x_split_high(act, 0)
            with act.Fori(0, cnt) as b:
                act.activation(ROOTS[:, 63:64], col(C_EPS), ACT.Silu)
                for p in range(EARLY, PIECES):
                    moe_high(act, b, p)
                act.wait_ge(m_done, 6 * b + 10)
                act.activation(SG, ps_gu[rows, 0:256], ACT.Silu).then_inc(m_silu, 1)
                act.wait_ge(h_turned, b + 1)
                act.activation(HH, ps_m[:, 0:2 * SLOTS], ACT.Copy).then_inc(h_high, 1)
                x_split_high(act, b + 1)
                for p in range(EARLY):
                    moe_high(act, b + 1, p)
                act.wait_ge(m_done, 6 * b + 12)
                act.wait_ge(y_stored, 16 * b + 16)
                act.copy(YB[:, 0, :], ps_y[0][rows, :]).then_inc(y_taken, 1)
            act.wait_ge(m_done, 6 * cnt + 6)
            act.wait_ge(m_low, 6 * cnt + 10)
            act.sem_inc(w_over, 1)

        def moe_vector(dve):
            cnt = n_blocks(dve)
            dve.memset(YB, 0.0).then_inc(y_taken, 2)
            dve.sem_inc(m_low, 6)
            for p in range(EARLY):
                moe_low(dve, 0, p)
            x_split_low(dve, 0)
            with dve.Fori(0, cnt) as b:
                for p in range(EARLY, PIECES):
                    moe_low(dve, b, p)
                dve.wait_ge(m_silu, b + 1)
                dve.tensor_tensor(HID, SG, ps_gu[rows, 256:512], ALU.mult).then_inc(m_hidden, 1)
                dve.wait_ge(h_high, b + 1)
                dve.tensor_tensor(HL, ps_m[:, 0:2 * SLOTS], HH.bitcast(F32), ALU.subtract).then_inc(h_low, 1)
                x_split_low(dve, b + 1)
                for p in range(EARLY):
                    moe_low(dve, b + 1, p)
                dve.wait_ge(m_done, 6 * b + 12)
                dve.wait_ge(y_stored, 16 * b + 16)
                dve.tensor_copy(YB[:, 1, :], ps_y[1][rows, :]).then_inc(y_taken, 1)

        def gather_rows(pool, ids):
            pool.indirect_dma_start(out=XB, out_offset=None, in_=rows_h,
                                    in_offset=bass.IndirectOffsetOnAxis(ap=ids, axis=0)).then_inc(x_rows, 16)

        def moe_gpsimd(pool):
            need(pool, "route_dve", "slots")
            ev.wait(pool, "st_zero", 16)
            for c in range(2 * QT):
                done(pool.indirect_dma_start(out=slot_tok, out_offset=bass.IndirectOffsetOnAxis(
                    ap=IDX[:, c:c + 1], axis=0), in_=TOKI[:, c // 2:c // 2 + 1], in_offset=None,
                    bounds_check=SLOTS * NBC - 1), "st_slots", by=16)
            ev.wait(pool, "st_slots", 2 * QT * 16)
            done(pool.dma_start(IDS, slot_tok.rearrange("(p b) a -> p (b a)", b=NBC)), "ld_slots", by=16)
            ev.wait(pool, "ld_slots", 16)
            ev.wait(pool, "st_rows", 16 * QT)
            cnt = n_blocks(pool)
            pool.tensor_copy(ID_COL, IDS[:, 0:1]).then_inc(x_ids, 1)
            pool.wait_ge(x_ids, 1)
            gather_rows(pool, ID_COL)
            with pool.Fori(0, cnt) as b:
                pool.wait_ge(x_rows, 16 * b + 16)
                pool.tensor_copy(ID_COL, IDS[:, bass.ds(b + 1, 1)]).then_inc(x_ids, 1)
                pool.wait_ge(x_ids, b + 2)
                pool.wait_ge(x_turned, b + 1)
                pool.sem_inc(x_go, 1)
                gather_rows(pool, ID_COL)
            pool.wait_ge(y_stored, 16 * cnt + 16)
            pool.sem_inc(y_over, 1)
            for i in range(QT):
                for q in range(2):
                    if i >= 2:
                        need(pool, "comb_dve", ("sum", i - 2))
                        need(pool, "comb_pe", (i - 2, 1))
                    done(pool.indirect_dma_start(
                        out=YG(i, q), out_offset=None, in_=rows_y, in_offset=bass.IndirectOffsetOnAxis(
                            ap=YIDX[:, 2 * i + q:2 * i + q + 1], axis=0), bounds_check=(NB_MAX + 1) * SLOTS - 1),
                        f"ld_y{i}", by=16)

        YG = lambda i, q: G[:, 4 * (i % 2) + 2 * q:4 * (i % 2) + 2 * q + 2, :].rearrange("p k s -> p (k s)")
        fl.append(On(tensor=moe_tensor, scalar=moe_scalar, vector=moe_vector, gpsimd=moe_gpsimd))

        def combine_vector(dve):
            for i in range(QT):
                ev.wait(dve, f"ld_y{i}", 32)
                step(dve, dve.tensor_scalar(YG(i, 0), YG(i, 0), WTS[:, i, 0:1], None, ALU.mult), "comb_dve")
                step(dve, dve.scalar_tensor_tensor(out=YG(i, 0), in0=YG(i, 1), scalar=WTS[:, i, 1:2],
                                                   in1=YG(i, 0), op0=ALU.mult, op1=ALU.add),
                     "comb_dve", ("sum", i))
                for q in range(2):
                    need(dve, "comb_pe", (i, q))
                    xs = X[:, 4 * q:4 * q + 4, i * P:(i + 1) * P]
                    done(dve.tensor_tensor(xs, xs, ps_s[q][:, :].rearrange("p (c t) -> p c t", t=P), ALU.add),
                         "comb_dve", ("x", i, q))

        def combine_tensor(pe):
            for i in range(QT):
                need(pe, "comb_dve", ("sum", i))
                for q in range(2):
                    if i:
                        need(pe, "comb_dve", ("x", i - 1, q))
                    for c in range(4):
                        k = 4 * q + c
                        last = pe.transpose(ps_s[q][:, c * P:(c + 1) * P], YG(i, 0)[:, k * P:(k + 1) * P], ident)
                    done(last, "comb_pe", (i, q))

        fl.append(On(tensor=combine_tensor, vector=combine_vector))
        moe_through = lambda e: need(e, "comb_dve", ("x", QT - 1, 1))
        cuts["moe"] = (len(fl), moe_through, MOE_AT)
        n_final1 = Norm("final1", KT, S, x_tile, lambda k: vec("norm_final", k), x_tile, None, None, moe_through)
        fl.append(n_final1)
        cuts["first"] = (len(fl), lambda e: need(e, "norm_dve", ("final1", "h", KT - 1)), MOE_AT)

        def ff_norm(l, x_done):
            return Norm(f"ffn{l}", KT, S, x_tile, lambda k: vec(f"ln_ffn{l}", k), h_tile, hi, lo, x_done,
                        wait_dst=x_done, early=True)

        x_final1 = lambda e: need(e, "norm_dve", ("final1", "h", KT - 1))
        fl.append(Prime(MOE_AT))
        mh2 = AR[:, 24:28, :].rearrange("p k (a s) -> p (k a) s", a=2)
        ml2 = AR[:, 28:32, :].rearrange("p k (a s) -> p (k a) s", a=2)
        n_mem2 = Norm("mem2", KT, NMEM, lambda k: raw1[:, k, :], lambda k: vec("ln_mem", k),
                      lambda k: raw1[:, k, :], lambda k: mh2[:, k, :], lambda k: ml2[:, k, :],
                      lambda e: (load_waits(e, "mem2"), moe_through(e)), wait_dst=x_final1)
        n_mem2.sq = n_mem2.total = H[:, 0:4, :].rearrange("p k s -> p (k s)")
        k2 = lambda l: G[:, 20 + l, :].rearrange("p (c m) -> p c m", c=2)
        v2f = lambda l: G[:, l, :].rearrange("p (c m) -> p c m", c=2)
        v2 = lambda l: G[:, 22 + l, :].rearrange("p (t f) -> p t f", t=2)
        fl += [n_mem2, Linear("mem2", lambda k: mh2[:, k, :], lambda k: ml2[:, k, :], n_mem2.ready,
                              taker(lambda j: (k2 if j % 4 < 2 else v2f)(j // 4)[:, j % 2, :]))]
        fl.append(Transposes("mem2_v", [
            ([(v2f(l)[:, c, t * P:(t + 1) * P], (2 * t + c) * P) for t in range(2) for c in range(2)],
             (G[:, 22 + l, :], lambda b: b[:, :]), None) for l in range(2)],
            wait_first=lambda e: wait_stage_evac(e, "mem2")))
        mem2_turned = fl[-1]

        n_mix0 = Norm("mix0", KT, S, x_tile, lambda k: vec("ln_mix0", k), h_tile, hi, lo, x_final1,
                      wait_dst=lambda e: (wait_products(e, "mem2"), need(e, *n_mem2.ready(KT - 1))))
        fl.append(n_mix0)
        cbuf = lambda j: AF[:, 24:27, :].rearrange("p k s -> p (k s)")[:, 516 * (j % 2):516 * (j % 2) + 515]
        PAD = CONV_K - 1
        N_CONV = 3 * GDN_HEADS

        def gdn_act(act, j, t, out):
            act.wait_ge(tile_done, t + 1)
            if j < N_CONV:
                if j == 0:
                    need(act, "conv_dve", "pad")
                elif j >= 2:
                    need(act, "conv_dve", j - 2)
                act.copy(cbuf(j)[:, PAD:PAD + S], out).then_inc(evacuated[t % BANKS], 1)
            elif j < N_CONV + GDN_HEADS:
                act.activation(AF[:, 16 + j - N_CONV, :], out, ACT.Silu).then_inc(evacuated[t % BANKS], 1)
            else:
                act.copy(AF[:, 22 + j - N_CONV - GDN_HEADS, :], out).then_inc(evacuated[t % BANKS], 1)
            if 1 <= j <= N_CONV:
                need(act, "conv_dve", j - 1)
                if j == 1:
                    need(act, "turn_act", mem2_turned.t0 + 1)
                done(act.activation(g(j - 1), SC[:, (j - 1) % 2, :], ACT.Silu), "conv_act", j - 1)

        def gdn_dve(dve, j, t, out):
            if j == 0:
                need(dve, "norm_dve", ("mix0", "low", KT - 1))
                for q in range(2):
                    step(dve, dve.memset(cbuf(q)[:, 0:PAD], 0.0), "conv_dve", "pad")
            if j < N_CONV:
                wait_evac(dve, t)
                if j >= 2:
                    need(dve, "conv_act", j - 2)
                acc = SC[:, j % 2, :]
                step(dve, dve.tensor_scalar(acc, cbuf(j)[:, 0:S], vec("conv", 4 * j), None, ALU.mult), "conv_dve")
                for q in range(1, CONV_K):
                    step(dve, dve.scalar_tensor_tensor(out=acc, in0=cbuf(j)[:, q:q + S],
                                                       scalar=vec("conv", 4 * j + q), in1=acc,
                                                       op0=ALU.mult, op1=ALU.add), "conv_dve", j)

        fl.append(Linear("gdnin", hi, lo, n_mix0.ready, gdn_act, gdn_dve))
        BETA, GC = G[0:GDN_HEADS, 18, :], G[0:GDN_HEADS, 19, :]
        fl.append(Linear("ba", hi, lo, None, taker(lambda j: G[0:GDN_HEADS, 18 + j, :])))

        def l2_scale(dve, k, s, label):
            if k < GDN_HEADS:
                done(dve.scalar_tensor_tensor(out=g(k), in0=g(k), scalar=GDN_D ** -0.5, in1=s, op0=ALU.mult,
                                              op1=ALU.mult), "hn_dve", label)
            else:
                done(dve.tensor_tensor(g(k), g(k), s, ALU.mult), "hn_dve", label)

        fl.append(HeadNorm("qk", 2 * GDN_HEADS, g, 1, 1.0, l2_scale,
                           lambda e: need(e, "conv_act", 2 * GDN_HEADS - 1)))

        def gates_vector(dve):
            st = lambda ins, label=None: step(dve, ins, "gate_dve", label)
            r = slice(0, GDN_HEADS)
            ts = dve.tensor_scalar
            wait_stage_evac(dve, "ba")
            need(dve, "gate_act", "beta")
            st(ts(BETA, BETA, 1.0, None, ALU.add), "beta")
            sp_, ab = SC[r, 0, :], SC[r, 1, :]
            st(ts(GC, GC, vec("dt", rows=r), None, ALU.add))
            st(dve.scalar_tensor_tensor(out=ab, in0=GC, scalar=-1.0, in1=GC, op0=ALU.mult, op1=ALU.min), "ab")
            need(dve, "gate_act", "exp")
            st(ts(ab, ab, 1.0, None, ALU.add), "ab1")
            st(ts(GC, GC, 0.0, None, ALU.max))
            need(dve, "gate_act", "ln")
            st(dve.tensor_tensor(GC, GC, ab, ALU.add))
            st(ts(GC, GC, COL[r, 46:47], -1.0, ALU.mult, ALU.mult))
            for c in range(QT):
                cs = slice(c * P, (c + 1) * P)
                st(dve.tensor_tensor_scan(sp_[:, cs], const("ones", GDN_HEADS), GC[:, cs], 0.0, ALU.mult, ALU.add))
            st(dve.tensor_copy(GC, sp_), "gc")

        def gates_scalar(act):
            r = slice(0, GDN_HEADS)
            ab = SC[r, 1, :]
            need(act, "hn_dve", ("qk", 2 * GDN_HEADS - 1))
            done(act.activation(COL[r, 46:47], vec("a_log", rows=r), ACT.Exp), "gate_act")
            done(act.activation(BETA, BETA, ACT.Exp, scale=-1.0), "gate_act", "beta")
            need(act, "gate_dve", "ab")
            done(act.activation(ab, ab, ACT.Exp), "gate_act", "exp")
            need(act, "gate_dve", "ab1")
            done(act.activation(ab, ab, ACT.Ln), "gate_act", "ln")

        fl.append(On(scalar=gates_scalar, vector=gates_vector))
        gate_cols = Transposes("gate_cols", [
            ([(G[0:GDN_HEADS, 18 + q, c * P:(c + 1) * P], 24 * q + GDN_HEADS * c) for q in range(2)
              for c in range(QT)], (COL[:, 48:96], lambda b: b[:, 0:48]), None)],
            wait_first=lambda e: need(e, "gate_dve", "gc"))
        fl.append(gate_cols)
        flat = lambda a, k, n: a[:, k:k + n, :].rearrange("p k s -> p (k s)")
        heads_of = lambda f, at_=0: f[:, at_:at_ + GDN_W].rearrange("p (h c) -> p h c", c=P)
        VROW, KROW = flat(AF, 0, 6), flat(AF, 6, 6)

        def row_groups(first, dest):
            out = []
            for c in range(QT):
                for h0, n in ((0, 4), (4, 2)):
                    at_ = c * GDN_W + h0 * P
                    out.append(([(G[:, first + h0 + h, c * P:(c + 1) * P], h * P) for h in range(n)],
                                (dest[:, at_:at_ + n * P], (lambda n: lambda b: b[:, 0:n * P])(n)), None))
            return out

        v_rows = Transposes("v_rows", row_groups(12, VROW), wait_first=lambda e: (
            need(e, "conv_act", N_CONV - 1), wait_products(e, "ba")))
        k_rows = Transposes("k_rows", row_groups(6, KROW),
                            wait_first=lambda e: need(e, "hn_dve", ("qk", 2 * GDN_HEADS - 1)))
        fl += [v_rows, k_rows]

        def gcb_tensor(pe):
            claim(pe)
            for h in range(GDN_HEADS):
                if h:
                    need(pe, "gcb_act", h - 1)
                else:
                    need(pe, "gate_dve", "gc")
                done(pe.matmul(ps_m[:, :], ident[0:GDN_HEADS, h:h + 1].to_broadcast([GDN_HEADS, P]), GC,
                               start=True, stop=True), "gcb_pe", h)
            held.append(("gcb_act", GDN_HEADS - 1))

        def gcb_scalar(act):
            need(act, "turn_pe", k_rows.t0 - 1)
            for h in range(GDN_HEADS):
                need(act, "gcb_pe", h)
                done(act.copy(g(12 + h), ps_m[:, :]), "gcb_act", h)
            need(act, "cc_dve", "args")
            done(act.activation(CC[:, 0:24], COL[:, 72:96], ACT.Exp), "cc_act")
            done(act.activation(CC[:, 24:72], CC[:, 24:72], ACT.Exp), "cc_act", "exp")

        CC = SC[:, 1, :]
        BG, KGC, GLAST = CC[:, 0:24], CC[:, 24:48], CC[:, 48:72]
        gc_last = G[:, 12:18, :].rearrange("p h (c j) -> p c h j", j=P)[:, :, :, P - 1]

        def cols_vector(dve):
            st = lambda ins, label=None: step(dve, ins, "cc_dve", label)
            need(dve, "gcb_act", GDN_HEADS - 1)
            need(dve, "turn_act", gate_cols.t0)
            need(dve, "gate_act", "ln")
            as_ch = lambda f: f.rearrange("p (c h) -> p c h", h=GDN_HEADS)
            st(dve.tensor_copy(as_ch(GLAST), gc_last))
            st(dve.tensor_tensor(KGC, GLAST, COL[:, 72:96], ALU.subtract), "args")
            st(dve.reciprocal(COL[:, 48:72], COL[:, 48:72]))
            need(dve, "cc_act", "exp")
            st(dve.tensor_tensor(BG, BG, COL[:, 48:72], ALU.mult), "cols")
            st(dve.memset(flat(AF, 12, 2)[:, 0:GDN_W], 0.0), "state0")

        fl.append(On(tensor=gcb_tensor, scalar=gcb_scalar, vector=cols_vector))
        k0_of = lambda l, h: k2(l)[64 * (h % 2):64 * (h % 2) + 64, h // 2, :]

        def mem2_attention(name, l, q, out, probs, turned, wait_scores, next_tile):
            return Attention(
                name, MEM_HEADS, "full", MEM_DH2 ** -0.5,
                lambda h, i, r: (q(h)[:, i * P:(i + 1) * P], k0_of(l, h)), probs, turned,
                lambda h: (out_rows(h), [(v2(l)[:, j, h * 64:(h + 1) * 64], (j, 0, 0, S), j == 0, j == 1)
                                         for j in range(2)]), out, wait_scores, lambda e: None,
                next_tile)

        att_mem0 = mem2_attention("mem0", 0, lambda h: AF[out_rows(h), 22 + h // 2, :],
                                  lambda o: AF[:, 22 + o, :], (AF[:, 24:26, :], AF[:, 26:28, :]),
                                  (AF[:, 28:30, :], AF[:, 30:32, :]),
                                  lambda e: (wait_stage_evac(e, "gdnin"), need(e, "conv_dve", N_CONV - 1)),
                                  BASE["out0"])
        fl.append(att_mem0)

        W4 = flat(AF, 24, 8)
        LT, TT, RR, UU, INT = (heads_of(W4, q * GDN_W) for q in range(5))
        DEC, CM, WT = heads_of(flat(G, 18, 2)), heads_of(flat(H, 6, 2)), heads_of(flat(AF, 14, 2))
        ST = heads_of(flat(AF, 12, 2))
        KBG = DEC
        halves = ((0, 3), (3, 6))
        wide = lambda c_: c_.unsqueeze(1).to_broadcast([P, GDN_HEADS, P])
        pair = lambda banks, q: banks[q][:, 0:3 * P].rearrange("p (h c) -> p h c", c=P)
        bank_a, bank_b, bank_c = ps_s, ps_t, (ps_o, ps_m)
        level = lambda l: CB[:, CONST["levels"][0] + l * P:CONST["levels"][0] + (l + 1) * P]
        LEVELS = 7
        by_col = lambda cols, c: cols[:, 6 * c:6 * c + 6].unsqueeze(2).to_broadcast([P, GDN_HEADS, P])
        rows_of = lambda f, c: heads_of(f, c * GDN_W)
        BETA_C, GC_C = COL[:, 48:72], COL[:, 72:96]

        def six(pe, banks, lhs, rhs, name, label, waits=lambda q: None, more=None):
            for q, (h0, h1) in enumerate(halves):
                waits(q)
                for h in range(h0, h1):
                    out = pair(banks, q)[:, h - h0, :]
                    last = pe.matmul(out, lhs(h), rhs(h), start=True, stop=more is None)
                    if more:
                        last = pe.matmul(out, more[0](h), more[1](h), start=False, stop=True)
                done(last, name, (label, q))

        def gdn_tensor(pe):
            N = "gdn_pe"
            for c in range(QT):
                cs = slice(c * P, (c + 1) * P)
                kT, qT = (lambda h: G[:, 6 + h, cs]), (lambda h: G[:, h, cs])
                if c == 0:
                    need(pe, *att_mem0.last)
                else:
                    need(pe, "gdn_act", (c - 1, "o", 1))
                    need(pe, "gdn_dve", (c - 1, "v", 1))
                six(pe, bank_a, kT, kT, N, (c, "kk"))
                six(pe, bank_c, qT, kT, N, (c, "qk"))
                need(pe, "gdn_dve", (c, "L"))
                if c:
                    need(pe, "gdn_dve", (c - 1, "S"))
                for q, (h0, h1) in enumerate(halves):
                    for h in range(h0, h1):
                        last = pe.transpose(pair(bank_b, q)[:, h - h0, :], TT[:, h, :], ident)
                    done(last, N, ((c, "Lt"), q))
                need(pe, "gdn_dve", (c, "intra", 1))
                for q, (h0, h1) in enumerate(halves):
                    need(pe, "gdn_act", (c, "Lt", q))
                    for h in range(h0, h1):
                        last = pe.transpose(pair(bank_b, q)[:, h - h0, :], UU[:, h, :], ident)
                    done(last, N, ((c, "It"), q))
                for l in range(1, LEVELS):
                    need(pe, "gdn_pool", (c, "C", l))
                    six(pe, bank_a, lambda h: CM[:, h, :], lambda h: TT[:, h, :], N, (c, "U", l),
                        waits=lambda q: need(pe, "gdn_dve", (c, "T", l - 1, q)))
                    if l < LEVELS - 1:
                        six(pe, bank_b, lambda h: RR[:, h, :], lambda h: UU[:, h, :], N, (c, "TU", l),
                            waits=lambda q: (need(pe, "gdn_act", (c, "U", l, q)),
                                             need(pe, "gdn_dve", (c, "R", l - 1, q)),
                                             need(pe, "gdn_act", (c, "It", q))))
                    six(pe, bank_c, lambda h: UU[:, h, :], lambda h: RR[:, h, :], N, (c, "UR", l),
                        waits=lambda q: (need(pe, "gdn_act", (c, "U", l, q)),
                                         need(pe, "gdn_dve", (c, "R", l - 1, q))))
                last_r = lambda q: need(pe, "gdn_dve", (c, "R", LEVELS - 1, q))
                need(pe, "gdn_dve", (c, "kbg"))
                six(pe, bank_a, lambda h: KBG[:, h, :], lambda h: RR[:, h, :], N, (c, "w"), waits=last_r)
                six(pe, bank_b, lambda h: RR[:, h, :], lambda h: rows_of(VROW, c)[:, h, :], N, (c, "u"),
                    waits=lambda q: need(pe, "gdn_dve", (c, "T", LEVELS - 2, q)))
                six(pe, bank_c, lambda h: WT[:, h, :], lambda h: ST[:, h, :], N, (c, "wS"),
                    waits=lambda q: (need(pe, "gdn_act", (c, "w", q)),
                                     need(pe, "gdn_dve", (c - 1, "S") if c else (0, "kbg"))))
                six(pe, bank_a, lambda h: ST[:, h, :], qT, N, (c, "o"),
                    waits=lambda q: need(pe, "gdn_dve", (c, "v", q)),
                    more=(lambda h: TT[:, h, :], lambda h: INT[:, h, :]))
                need(pe, "gdn_dve", (c, "kg"))
                six(pe, bank_b, lambda h: LT[:, h, :], lambda h: TT[:, h, :], N, (c, "kv"),
                    waits=lambda q: need(pe, "gdn_act", (c, "u", q)))

        def gdn_scalar(act):
            A = "gdn_act"

            def take(dest, banks, c, label, as_=None):
                for q, (h0, h1) in enumerate(halves):
                    need(act, "gdn_pe", (label, q))
                    done(act.copy(dest(h0, h1), pair(banks, q)), A, label + (q,))

            for c in range(QT):
                cs = slice(c * P, (c + 1) * P)
                need(act, "gdn_dve", (c, "dec"))
                done(act.activation(DEC, DEC, ACT.Exp, scale=-1.0), A, (c, "dec"))
                take(lambda a_, b_: LT[:, a_:b_, :], bank_b, c, (c, "Lt"))
                take(lambda a_, b_: INT[:, a_:b_, :], bank_b, c, (c, "It"))
                need(act, "gdn_dve", (c, "intra", 1))
                done(act.activation(DEC, G[:, 12:18, cs], ACT.Exp), A, (c, "eg"))
                for l in range(1, LEVELS):
                    for q, (h0, h1) in enumerate(halves):
                        need(act, "gdn_pe", ((c, "U", l), q))
                        done(act.copy(UU[:, h0:h1, :], pair(bank_a, q)), A, (c, "U", l, q))
                take(lambda a_, b_: WT[:, a_:b_, :], bank_a, c, (c, "w"))
                take(lambda a_, b_: UU[:, a_:b_, :], bank_b, c, (c, "u"))
                take(lambda a_, b_: H[:, a_:b_, cs], bank_a, c, (c, "o"))

        def gdn_vector(dve):
            N = "gdn_dve"
            st = lambda ins, label=None: step(dve, ins, N, label)
            tt = dve.tensor_tensor
            for c in range(QT):
                cs = slice(c * P, (c + 1) * P)
                if c == 0:
                    need(dve, "turn_act", k_rows.t0 + 7)
                    need(dve, *att_mem0.last)
                    need(dve, "norm_dve", ("mix0", "low", KT - 1))
                else:
                    need(dve, "gdn_pe", ((c - 1, "kv"), 1))
                st(tt(DEC, G[:, 12:18, cs], by_col(GC_C, c), ALU.subtract))
                st(dve.tensor_scalar(DEC, DEC, 0.0, None, ALU.max), (c, "dec"))
                need(dve, "gdn_act", (c, "dec"))
                st(tt(CM, DEC, wide(const("lower")), ALU.mult))
                for q, (h0, h1) in enumerate(halves):
                    need(dve, "gdn_pe", ((c, "kk"), q))
                    for h in range(h0, h1):
                        done(dve.scalar_tensor_tensor(out=TT[:, h, :], in0=pair(bank_a, q)[:, h - h0, :],
                                                      scalar=BETA_C[:, 6 * c + h:6 * c + h + 1], in1=CM[:, h, :],
                                                      op0=ALU.mult, op1=ALU.mult), N, (c, "L"))
                st(tt(DEC, DEC, wide(const("incl")), ALU.mult))
                for q, (h0, h1) in enumerate(halves):
                    need(dve, "gdn_pe", ((c, "qk"), q))
                    st(tt(UU[:, h0:h1, :], pair(bank_c, q), DEC[:, h0:h1, :], ALU.mult), (c, "intra", q))
                need(dve, "gdn_pe", ((c, "Lt"), 1))
                st(tt(TT, TT, wide(const("first_level")), ALU.mult))
                st(tt(TT, wide(ident), TT, ALU.subtract), (c, "T", 0, 0))
                ev.seen[N, (c, "T", 0, 1)] = ev.seen[N, (c, "T", 0, 0)]
                need(dve, "gdn_act", (c, "Lt", 1))
                st(tt(RR, LT, wide(level(0)), ALU.mult))
                st(tt(RR, wide(ident), RR, ALU.subtract), (c, "R", 0, 0))
                ev.seen[N, (c, "R", 0, 1)] = ev.seen[N, (c, "R", 0, 0)]
                need(dve, "gdn_act", (c, "eg"))
                st(tt(G[:, 0:6, cs], G[:, 0:6, cs], DEC, ALU.mult), (c, "qg"))
                st(tt(KBG, rows_of(KROW, c), by_col(BG, c), ALU.mult))
                st(tt(rows_of(VROW, c), rows_of(VROW, c), by_col(BETA_C, c), ALU.mult), (c, "kbg"))
                for l in range(1, LEVELS):
                    for q, (h0, h1) in enumerate(halves):
                        if l < LEVELS - 1:
                            need(dve, "gdn_pe", ((c, "TU", l), q))
                            done(tt(TT[:, h0:h1, :], TT[:, h0:h1, :], pair(bank_b, q), ALU.subtract), N,
                                 (c, "T", l, q))
                    for q, (h0, h1) in enumerate(halves):
                        need(dve, "gdn_pe", ((c, "UR", l), q))
                        done(tt(RR[:, h0:h1, :], RR[:, h0:h1, :], pair(bank_c, q), ALU.subtract), N,
                             (c, "R", l, q))
                need(dve, "gdn_pool", (c, "C", LEVELS - 1))
                done(tt(LT, rows_of(KROW, c), by_col(KGC, c), ALU.mult), N, (c, "kg"))
                for q, (h0, h1) in enumerate(halves):
                    need(dve, "gdn_act", (c, "u", q))
                    need(dve, "gdn_pe", ((c, "wS"), q))
                    st(tt(TT[:, h0:h1, :], UU[:, h0:h1, :], pair(bank_c, q), ALU.subtract), (c, "v", q))
                for q, (h0, h1) in enumerate(halves):
                    need(dve, "gdn_pe", ((c, "kv"), q))
                    for h in range(h0, h1):
                        done(dve.scalar_tensor_tensor(out=ST[:, h, :], in0=ST[:, h, :],
                                                      scalar=GLAST[:, 6 * c + h:6 * c + h + 1],
                                                      in1=pair(bank_b, q)[:, h - h0, :], op0=ALU.mult,
                                                      op1=ALU.add), N, (c, "S"))

        def gdn_gpsimd(pool):
            for c in range(QT):
                for l in range(1, LEVELS):
                    if l == 1:
                        need(pool, "gdn_act", (c, "Lt", 1))
                        need(pool, "gdn_dve", (c, "intra", 1))
                    else:
                        need(pool, "gdn_pe", ((c, "U", l - 1), 1))
                    done(pool.tensor_tensor(CM, LT, wide(level(l)), ALU.mult), "gdn_pool", (c, "C", l))

        fl.append(On(tensor=gdn_tensor, scalar=gdn_scalar, vector=gdn_vector, gpsimd=gdn_gpsimd))

        def gdn_gain(dve, k, s, label):
            step(dve, dve.scalar_tensor_tensor(out=h_tile(k), in0=h_tile(k), scalar=vec("gdn_norm"), in1=s,
                                               op0=ALU.mult, op1=ALU.mult), "hn_dve")
            done(dve.tensor_tensor(h_tile(k), h_tile(k), AF[:, 16 + k, :], ALU.mult), "hn_dve", label)

        gdn_out = lambda e: (need(e, "gdn_act", (QT - 1, "o", 1)), need(e, "gdn_dve", (QT - 1, "S")))
        fl.append(HeadNorm("gdn", GDN_HEADS, h_tile, 1, 1.0 / GDN_D, gdn_gain, gdn_out))
        s_gdn = Split("gdn", 8, lambda k: h_tile(k) if k < 6 else AF[:, 16 + k, :], hi, lo,
                      lambda e: need(e, "hn_dve", ("gdn", GDN_HEADS - 1)))
        n_ff0 = ff_norm(0, lambda e: wait_stage_evac(e, "out0"))
        fl += [s_gdn, Linear("out0", hi, lo, s_gdn.ready, *add_and_square(n_ff0))]
        cuts["s1"] = (len(fl), lambda e: wait_stage_evac(e, "out0"), BASE["gu00"])

        def swiglu(l, n, following):
            fl.append(n)
            for p, width in enumerate(FF_PARTS):
                name = f"gu{l}{p}"
                ready = {}

                def take_act(act, j, t, out, name=name, width=width, p=p):
                    i, up = j // 2, j % 2
                    if not up:
                        act.wait_ge(tile_done, t + 1)
                        if i >= 2:
                            wait_evac(act, t - 3)
                        act.activation(H[:, i % 2, :], out, ACT.Silu).then_inc(evacuated[t % BANKS], 1)
                    else:
                        wait_evac(act, t)
                        if i == 0 and p:
                            wait_products(act, f"down{l}{p - 1}")
                        done(act.activation(AR[:, 16 + i, :], H[:, 2 + i % 2, :], ACT.Copy), "ff_act", (name, i))

                def take_dve(dve, j, t, out, name=name, width=width, p=p):
                    i, up = j // 2, j % 2
                    if up:
                        wait_evac(dve, t - 1)
                        dve.wait_ge(tile_done, t + 1)
                        dve.tensor_tensor(H[:, 2 + i % 2, :], H[:, i % 2, :], out,
                                          ALU.mult).then_inc(evacuated[t % BANKS], 1)
                        need(dve, "ff_act", (name, i))
                        done(dve.tensor_tensor(AR[:, 24 + i, :], H[:, 2 + i % 2, :],
                                               AR[:, 16 + i, :].bitcast(F32), ALU.subtract), "ff_dve", (name, i))

                fl.append(Linear(name, hi, lo, n.ready if p == 0 else None, take_act, take_dve))
                fl.append(Linear(f"down{l}{p}", lambda k: AR[:, 16 + k, :], lambda k: AR[:, 24 + k, :],
                                 (lambda name: lambda k: ("ff_dve", (name, k)))(name),
                                 *(add_and_square(following) if p == len(FF_PARTS) - 1 else (None, add_to_x))))

        x_ff0, x_ff1 = (lambda e: wait_stage_evac(e, f"down0{len(FF_PARTS) - 1}"),
                        lambda e: wait_stage_evac(e, f"down1{len(FF_PARTS) - 1}"))
        n_kv = Norm("kv", KT, S, x_tile, lambda k: vec("ln_kv", k), h_tile, hi, lo, x_ff0, wait_dst=x_ff0,
                    early=True)
        swiglu(0, n_ff0, n_kv)
        cuts["s2"] = (len(fl), x_ff0, BASE["kv"])

        cos_s, sin_s = g(3), g(4)
        fl.append(Angles("swa", GI[:, 16, :], col(C_INV_SWA), col(C_SIGN_SWA), cos_s, sin_s,
                         lambda e: load_waits(e, "pos2")))
        fl += [n_kv, Linear("kv", hi, lo, n_kv.ready, taker(lambda j: g(j) if j < 2 else g(5)))]
        swa_v = Transposes("swa_v", [([(G[:, 5, i * P:(i + 1) * P], i * P) for i in range(QT)],
                                      (g(2), lambda b: b[:, :]), None)],
                           wait_first=lambda e: wait_stage_evac(e, "kv"))
        fl.append(swa_v)
        fl.append(Rope("swa_k", [g(0), g(1)], P, const("perm_swa"), cos_s, sin_s,
                       lambda e: wait_stage_evac(e, "kv")))

        n_mix1 = Norm("mix1", KT, S, x_tile, lambda k: vec("ln_mix1", k), h_tile, hi, lo, x_ff0,
                      wait_dst=lambda e: (wait_products(e, "kv"), need(e, "rope_dve", ("swa_k", 1)),
                                          need(e, *n_kv.ready(KT - 1))), roots_of=n_kv)
        fl += [n_mix1, Linear("swaq", hi, lo, n_mix1.ready, taker(lambda j: g(5 + j), lambda e: need(
            e, "turn_pe", swa_v.t0)))]
        fl.append(Rope("swa_q", [g(5 + k) for k in range(6)], P, const("perm_swa"), cos_s, sin_s,
                       lambda e: wait_stage_evac(e, "swaq")))
        per_kv = SWA_HEADS // SWA_KV

        def window_mask(dve):
            need(dve, *n_mix1.ready(KT - 1))
            wait_stage_evac(dve, "kv")
            for i in range(QT):
                first, second = (("causal", None) if i == 0 else ("prev", "causal"))
                step(dve, dve.tensor_copy(WINDOW[:, i, 0:P], const(first)), "window_dve")
                if second:
                    step(dve, dve.tensor_copy(WINDOW[:, i, P:2 * P], const(second)), "window_dve")
                else:
                    step(dve, dve.memset(WINDOW[:, i, P:2 * P], NEG), "window_dve")

        fl.append(On(vector=window_mask))

        def swa_scores(h, i, r):
            rows = out_rows(h)
            return G[rows, 5 + h // 2, i * P:(i + 1) * P], G[rows, h // per_kv, max(i - 1, 0) * P:max(i + 1, 2) * P]

        def swa_pv(h):
            plan_ = []
            for i in range(QT):
                tiles = [i] if i == 0 else [i - 1, i]
                for b, j in enumerate(tiles):
                    v = G[:, 2, j * P + 64 * (h // per_kv):j * P + 64 * (h // per_kv) + 64]
                    plan_.append((v, (b, i * P, i * P, (i + 1) * P), b == 0, b == len(tiles) - 1))
            return out_rows(h), plan_

        probs_s = (G[:, 14:16, :], G[:, 16:18, :])
        turned_s = (AF[:, 16:18, :], AF[:, 18:20, :])
        swa = Attention("swa", SWA_HEADS, "window", SWA_DH ** -0.5, swa_scores,
                        probs_s, turned_s, swa_pv, h_tile,
                        lambda e: need(e, "rope_dve", ("swa_q", 5)), lambda e: need(e, "turn_act", swa_v.t0), BASE["out1"],
                        wait_out=lambda e: (wait_products(e, "swaq"), need(e, *n_mix1.ready(KT - 1))))
        att_mem1 = mem2_attention("mem1", 1, lambda h: G[out_rows(h), 11 + h // 2, :],
                                  lambda o: h_tile(6 + o), probs_s, turned_s,
                                  lambda e: wait_stage_evac(e, "swaq"), BASE["out1"])
        s_swa = Split("swa", 8, h_tile, hi, lo, last_head(att_mem1))
        n_ff1 = ff_norm(1, lambda e: wait_stage_evac(e, "out1"))
        fl += [swa, att_mem1, s_swa, Linear("out1", hi, lo, s_swa.ready, *add_and_square(n_ff1))]
        cuts["s4"] = (len(fl), lambda e: wait_stage_evac(e, "out1"), BASE["gu10"])
        n_final = Norm("final", KT, S, x_tile, lambda k: vec("ln_final", k), x_tile, None, None, x_ff1,
                       early=True)
        swiglu(1, n_ff1, n_final)
        fl.append(n_final)
        cuts["final"] = (len(fl), lambda e: need(e, "norm_dve", ("final", "h", KT - 1)), N_TILES)

        def load_tile(sp, t):
            name, _, kt, m, _ = TILE[t]
            if t >= RING:
                sp.wait_ge(low_ready, t - RING + 1)
            sp.dma_start(WRAW[:, t % RING, 0:kt * m], a["w_" + name][t - BASE[name]]).then_inc(w_loaded[t % RING], 16)

        if stop:
            fl = fl[:cuts[stop][0]]
        last_tile = cuts[stop or "final"][2]
        block = ctx.enter_context(nc.Block())

        @block.sync
        def _(sp):
            done(sp.dma_start(CB[:, :], a["consts"]), "ld_const", by=16)
            done(sp.dma_start(VB[:, :], a["vectors"]), "ld_vec", by=16)
            done(sp.dma_start(X[:, :, :], a["x_t"]), "ld_x", by=16)
            for t in range(MOE_AT):
                load_tile(sp, t)
            for i in range(QT):
                need(sp, "turn_act", rows_out.t0 + 2 * i + 1)
                done(sp.dma_start(rows_h[i * P:(i + 1) * P, :],
                                  G[:, 4 + 2 * i:6 + 2 * i, :].rearrange("p k s -> p (k s)")), "st_rows", by=16)
            moe_sync(sp)
            for t in range(MOE_AT, min(last_tile + 2, N_TILES)):
                load_tile(sp, t)
            cuts[stop or "final"][1](sp)
            done(sp.dma_start(a["out"], X[:, :, :]), "st_out", by=16)
            ev.wait(sp, "st_out", 16)

        @block.gpsimd
        def _(pool):
            done(pool.dma_start(GI[:, 16, :], a["pos"].partition_broadcast(P)), "ld_pos", by=16)
            done(pool.dma_start(COLI[:, 40:44], a["pos_col"]), "ld_posc", by=16)
            load_waits(pool, "const")
            zeros = CB[0:SLOTS, CONST["perm_mla"][0]:CONST["perm_mla"][0] + NBC].bitcast(I32)
            done(pool.dma_start(slot_tok.rearrange("(p b) a -> p (b a)", b=NBC), zeros), "st_zero", by=16)
            done(pool.dma_start(rows_y[(NB_MIN + 1) * SLOTS:, :].rearrange("(n p) d -> p n d", p=P),
                                CB[:, 0:D].unsqueeze(1).to_broadcast([P, (NB_MAX - NB_MIN) * SLOTS // P, D])),
                 "st_fill", by=16)
            need(pool, "rope_dve", ("mla_q", MLA_HEADS))
            done(pool.dma_start(raw1, a["mem_t"]), "ld_mem", by=16)
            done(pool.dma_start(RW, a["router_w"]), "ld_router", by=16)
            need(pool, *n_mem.ready(KT - 1))
            done(pool.dma_start(raw1, a["mem2_t"]), "ld_mem2", by=16)
            moe_gpsimd(pool)
            if not stop or stop not in ("moe", "first"):
                gdn_gpsimd(pool)
                need(pool, "gdn_dve", (QT - 1, "S"))
                done(pool.dma_start(GI[:, 16, :], a["pos2"].partition_broadcast(P)), "ld_pos2", by=16)

        @block.tensor
        def _(pe):
            load_waits(pe, "const")
            for stage in fl:
                stage.tensor(pe)

        @block.scalar
        def _(act):
            for stage in fl:
                stage.scalar(act)

        @block.vector
        def _(dve):
            for stage in fl:
                stage.vector(dve)
    return ev.seen


def _feature_major(x):
    return np.ascontiguousarray(x.T.reshape(-1, P, x.shape[0]).transpose(1, 0, 2))


def _tiles(w, cols):
    k = w.shape[0] // P
    return np.ascontiguousarray(
        np.stack([w[:, c].reshape(k, P, len(c)).transpose(1, 0, 2).reshape(P, k * len(c)) for c in cols]))


def _blocks(n, width=P, at=0):
    return [np.arange(at + i * width, at + (i + 1) * width) for i in range(n)]


def _constants():
    p, f = np.arange(P)[:, None], np.arange(P)[None, :]
    c = {"ident": p == f, "upper": p < f, "lower": p > f, "incl": p >= f, "ones": p + f >= 0,
         "causal": np.where(f <= p, 0.0, NEG), "prev": np.where(f > p, 0.0, NEG),
         "blk64": p // 64 == f // 64}
    rope = np.where(f >= 64, 64 + (f - 64 + 16) % 32, -1)
    c["perm_mla"] = (p == rope) & (f >= 64) & (f < 96)
    d = f % 64
    c["perm_swa"] = (p == f - d + (d + SWA_ROT // 2) % SWA_ROT) & (d < SWA_ROT)
    pair = lambda i, j, s: (i // (2 * s) == j // (2 * s)) & ((i // s) % 2 == 1) & ((j // s) % 2 == 0)
    c["first_level"] = pair(p, f, 1)
    c["levels"] = np.concatenate([pair(f, p, 1 << k) for k in range(7)], axis=1)
    c["iota"] = np.broadcast_to(np.arange(56), (P, 56))
    q = np.arange(P)
    cols = np.zeros((P, 8), np.float64)
    r = (q - 64) % 32
    cols[:, C_INV_MLA] = np.where((q >= 64) & (q < 96), 10000.0 ** (-(2.0 * (r % 16)) / 32), 0)
    cols[:, C_SIGN_MLA] = np.where(r < 16, -1, 1)
    e = q % 64
    cols[:, C_INV_SWA] = np.where(e < 16, 500000.0 ** (-(2.0 * (e % 8)) / 16), 0)
    cols[:, C_SIGN_SWA] = np.where(e < 8, -1, 1)
    cols[:, C_TOKEN] = q
    cols[:, C_EPS] = EPS
    c["cols"] = cols
    return np.ascontiguousarray(np.concatenate([np.asarray(c[n], np.float32) for n in CONST], axis=1))


def _vectors(i):
    col = lambda v: v.reshape(-1, P).T
    row = lambda v: np.broadcast_to(v.reshape(1, -1), (P, v.size))
    few = lambda v: np.concatenate([v.reshape(-1, 1), np.zeros((P - v.size, 1), v.dtype)])
    v = {"norm_mix": col(i["norm_mix_g"]), "norm_cross": col(i["norm_cross_g"]), "norm_mem": col(i["norm_mem_g"]),
         "norm_ffn": col(i["norm_ffn_g"]), "ln_mem": col(i["ln_mem_2"]), "ln_kv": col(i["ln_kv_2"]),
         "ln_final": col(i["ln_final_2"]), "mla_q": col(i["mla_q_norm_g"]), "mla_kv": col(i["mla_kv_norm_g"]),
         "mla_out": col(i["mla_out_g"]), "diff_out": np.concatenate([i["diff_out_g"].reshape(-1, 1)] * 2),
         "gdn_norm": col(i["gdn_norm_2"]), "sinks": row(i["swa_sinks_2"]),
         "conv": i["gdn_conv_2"][0].reshape(CONV_K, 18, P).transpose(2, 1, 0).reshape(P, -1),
         "lam": row(np.concatenate([i[f"diff_lambda_{n}"].reshape(-1) for n in ("q1", "k1", "q2", "k2")])),
         "a_log": few(i["gdn_A_log_2"]), "dt": few(i["gdn_dt_bias_2"]),
         "router_b": row(np.concatenate([i["b_group_router"].reshape(-1), i["b_expert_router"].reshape(-1)])),
         "norm_final": col(i["norm_final_g"])}
    for l in range(2):
        v[f"ln_mix{l}"], v[f"ln_ffn{l}"] = col(i["ln_mix_2"][l]), col(i["ln_ffn_2"][l])
    return np.ascontiguousarray(np.concatenate([v[n] for n in VEC], axis=1))


def _arrays(i):
    w_in, w_gdn = i["w_in"][0], i["gdn_w_in_2"][0]
    a = {"x_t": _feature_major(i["x"][0]), "mem_t": _feature_major(i["mem"][0]),
         "mem2_t": _feature_major(i["mem_2"][0]), "consts": _constants(), "vectors": _vectors(i),
         "pos": i["positions"].reshape(S), "pos2": i["positions_2"].reshape(S),
         "pos_col": np.ascontiguousarray(i["positions"].reshape(QT, P).T)}
    a["router_w"] = np.ascontiguousarray(
        np.concatenate([i["w_group_router"][0], i["w_expert_router"][0]], axis=1)
        .reshape(KT, P, 36).transpose(1, 0, 2))
    a["w_in"] = _tiles(w_in, _blocks(15))
    a["w_kpe"] = _tiles(w_in, [np.arange(15 * P, 15 * P + MLA_ROPE)])
    a["w_uq"] = _tiles(i["w_mla_uq"][0], _blocks(MLA_HEADS, MLA_QK))
    a["w_ukv"] = _tiles(i["w_mla_ukv"][0], _blocks(MLA_HEADS))
    a["w_out"] = _tiles(i["w_out"][0], _blocks(KT))
    a["w_memkv"] = _tiles(i["w_mem_kv"][0], _blocks(8))
    a["w_memq"] = _tiles(i["w_mem_q"][0], _blocks(4))
    a["w_memo"] = _tiles(i["w_mem_o"][0], _blocks(KT))
    gu = np.concatenate([i["w_expert_gate"][0], i["w_expert_up"][0]], axis=2)
    gu = gu.reshape(N_EXPERTS, 4, 2, P, 512).transpose(0, 1, 3, 2, 4).reshape(N_EXPERTS, 4, P, 1024)
    a["w_experts"] = np.ascontiguousarray(
        np.concatenate([gu, i["w_expert_down"][0].reshape(N_EXPERTS, 2, P, 1024)], axis=1))
    a["w_mem2"] = np.concatenate([_tiles(i["w_mem_kv_2"][l], _blocks(4)) for l in range(2)])
    z0 = 3 * GDN_W
    ba = z0 + GDN_W
    a["w_gdnin"] = _tiles(w_gdn, _blocks(24) + _blocks(2, P, ba + 2 * GDN_HEADS))
    a["w_ba"] = _tiles(w_gdn, _blocks(2, GDN_HEADS, ba))
    kv = _blocks(4, 64)
    a["w_kv"] = _tiles(i["w_kv_2"], [np.tile(kv[0], 2), np.tile(kv[1], 2), np.concatenate(kv[2:])])
    a["w_swaq"] = _tiles(i["swa_w_q_2"][0], _blocks(8))
    for l in range(2):
        a[f"w_out{l}"] = _tiles(i["w_out_2"][l], _blocks(KT))
        at = 0
        for p, n in enumerate(FF_PARTS):
            gate, up = _blocks(n, P, at * P), _blocks(n, P, D_FF + at * P)
            a[f"w_gu{l}{p}"] = _tiles(i["w_gate_up_2"][l], [c for pair in zip(gate, up) for c in pair])
            a[f"w_down{l}{p}"] = _tiles(i["w_down_2"][l][at * P:(at + n) * P], _blocks(KT))
            at += n
    return a


def _described(nc, shapes):
    aps = {n: nc.dram_tensor(n, list(shape), mybir.dt.from_np(dtype), kind="ExternalInput").ap()
           for n, (shape, dtype) in shapes.items()}
    aps["out"] = nc.dram_tensor("out", [P, KT, S], F32, kind="ExternalOutput").ap()
    return aps


def kernel(**inputs):
    import concourse.bacc as _bacc
    from concourse.bass_utils import run_bass_kernel_spmd as _run

    arrays = _arrays({k: np.asarray(v) for k, v in inputs.items()})
    shapes = {n: (v.shape, v.dtype) for n, v in arrays.items()}
    counting = _bacc.Bacc("TRN2", target_bir_lowering=False, num_devices=1)
    counted = program(counting, _described(counting, shapes), defaultdict(lambda: 1))
    nc = _bacc.Bacc("TRN2", target_bir_lowering=False, num_devices=1)
    program(nc, _described(nc, shapes), counted)
    r = _run(nc, [arrays], core_ids=[0])
    out = r.results[0]["out"]
    return out.transpose(1, 0, 2).reshape(D, S).T.reshape(1, S, D)
```
